# Optimizing a Trainium2 kernel written in Bass

```python
import jax
import jax.numpy as jnp
from jax import lax
import numpy as np

D_MODEL = 2048
BATCH = 1
SEQ = 256
DEPTH = 1

MEM_LEN = 256
GRID_W = 64
N_MIXERS = 4
GROUP_W = D_MODEL // N_MIXERS
ML_HEADS = 4
ML_DH = GROUP_W // ML_HEADS
ML_CHUNK = 64
ML_CONV = 3
HG_HEADS = 4
HG_DK = GROUP_W // HG_HEADS
HG_CHUNK = 16
FN_GROUPS = 4
FN_CH = GROUP_W // FN_GROUPS
NA_HEADS = 8
NA_DH = GROUP_W // NA_HEADS
NA_KH = 8
NA_KW = 16
XA_HEADS = 4
XA_DH = D_MODEL // XA_HEADS
MOE_GROUPS = 4
MOE_PER_GROUP = 8
MOE_EXPERTS = MOE_GROUPS * MOE_PER_GROUP
MOE_TOPK = 2
MOE_FF = D_MODEL // 4
MOE_BLOCK = 128
EPS = 1e-6
F32 = jnp.float32
IN_SIZES = (GROUP_W, GROUP_W, GROUP_W, GROUP_W, 4 * ML_HEADS,
            GROUP_W, GROUP_W, GROUP_W, GROUP_W, GROUP_W,
            GROUP_W,
            GROUP_W, GROUP_W, GROUP_W)
IN_W = 13 * GROUP_W + 4 * ML_HEADS

kernel_name = 'hybrid_parallel_heads_hmoe_encoder'

def rms_norm(x, g):
    xf = x.astype(F32)
    y = xf * lax.rsqrt(jnp.mean(xf * xf, axis=-1, keepdims=True) + EPS)
    return (y * g.astype(F32)).astype(x.dtype)

def to_heads(t, n_heads):
    b, s, _ = t.shape
    return t.reshape(b, s, n_heads, -1).transpose(0, 2, 1, 3).astype(F32)

def merge_heads(t):
    b, h, s, d = t.shape
    return t.transpose(0, 2, 1, 3).reshape(b, s, h * d)

def centred_dwconv(x, w):
    k, c = w.shape
    return lax.conv_general_dilated(x, w[:, None, :].astype(x.dtype), window_strides=(1,),
                                    padding=[(k // 2, k // 2)],
                                    dimension_numbers=('NWC', 'WIO', 'NWC'),
                                    feature_group_count=c)

def mlstm_chunkwise(q, k, v, ig, fg):
    b_, h_, s_, d_ = q.shape
    L = ML_CHUNK
    nc = s_ // L
    q = q.reshape(b_, h_, nc, L, d_)
    k = k.reshape(b_, h_, nc, L, d_)
    v = v.reshape(b_, h_, nc, L, d_)
    ig = ig.reshape(b_, h_, nc, L)
    bcum = jnp.cumsum(jax.nn.log_sigmoid(fg).reshape(b_, h_, nc, L), axis=-1)
    b_end = bcum[..., -1]
    causal = jnp.tril(jnp.ones((L, L), dtype=bool))
    dmat = jnp.where(causal, bcum[..., :, None] - bcum[..., None, :] + ig[..., None, :], -jnp.inf)
    a = b_end[..., None] - bcum + ig
    m_loc = jnp.max(a, axis=-1)
    wa = jnp.exp(a - m_loc[..., None])
    c_loc = jnp.einsum('bhcs,bhcsd,bhcse->bhcde', wa, k, v)
    n_loc = jnp.einsum('bhcs,bhcsd->bhcd', wa, k)

    def step(carry, xs):
        c, n, m = carry
        cl, nl, ml, bl = xs
        m_new = jnp.maximum(bl + m, ml)
        s_old = jnp.exp(bl + m - m_new)
        s_new = jnp.exp(ml - m_new)
        c_next = s_old[..., None, None] * c + s_new[..., None, None] * cl
        n_next = s_old[..., None] * n + s_new[..., None] * nl
        return (c_next, n_next, m_new), (c, n, m)

    init = (jnp.zeros((b_, h_, d_, d_), F32), jnp.zeros((b_, h_, d_), F32), jnp.zeros((b_, h_), F32))
    xs = (jnp.moveaxis(c_loc, 2, 0), jnp.moveaxis(n_loc, 2, 0), jnp.moveaxis(m_loc, 2, 0), jnp.moveaxis(b_end, 2, 0))
    _, (c_prev, n_prev, m_prev) = lax.scan(step, init, xs)
    c_prev = jnp.moveaxis(c_prev, 0, 2)
    n_prev = jnp.moveaxis(n_prev, 0, 2)
    m_prev = jnp.moveaxis(m_prev, 0, 2)
    inter = bcum + m_prev[..., None]
    m_t = jnp.maximum(inter, jnp.max(dmat, axis=-1))
    w = jnp.exp(dmat - m_t[..., None])
    s_inter = jnp.exp(inter - m_t)
    qk = jnp.einsum('bhctd,bhcsd->bhcts', q, k) * w
    num = jnp.einsum('bhcts,bhcse->bhcte', qk, v) + s_inter[..., None] * jnp.einsum('bhctd,bhcde->bhcte', q, c_prev)
    den = qk.sum(-1) + s_inter * jnp.einsum('bhctd,bhcd->bhct', q, n_prev)
    h = num / jnp.maximum(jnp.abs(den), jnp.exp(-m_t))[..., None]
    return h.reshape(b_, h_, s_, d_)

def hgrn2_chunkwise(q, k, v, logf):
    b_, h_, s_, dk = q.shape
    dv = v.shape[-1]
    L = HG_CHUNK
    nc = s_ // L
    q = q.reshape(b_, h_, nc, L, dk)
    k = k.reshape(b_, h_, nc, L, dk)
    v = v.reshape(b_, h_, nc, L, dv)
    bcum = jnp.cumsum(logf.reshape(b_, h_, nc, L, dk), axis=-2)
    b_end = bcum[..., -1, :]
    causal = jnp.tril(jnp.ones((L, L), dtype=bool))[..., None]
    decay = jnp.exp(jnp.where(causal, bcum[..., :, None, :] - bcum[..., None, :, :], -jnp.inf))
    attn = jnp.einsum('bhctd,bhctsd,bhcsd->bhcts', q, decay, k)
    o_intra = jnp.einsum('bhcts,bhcse->bhcte', attn, v)
    s_loc = jnp.einsum('bhcsd,bhcse->bhcde', k * jnp.exp(b_end[..., None, :] - bcum), v)

    def step(s, xs):
        sl, dl = xs
        return jnp.exp(dl)[..., None] * s + sl, s

    _, s_prev = lax.scan(step, jnp.zeros((b_, h_, dk, dv), F32),
                         (jnp.moveaxis(s_loc, 2, 0), jnp.moveaxis(b_end, 2, 0)))
    s_prev = jnp.moveaxis(s_prev, 0, 2)
    o_inter = jnp.einsum('bhctd,bhcde->bhcte', q * jnp.exp(bcum), s_prev)
    return (o_intra + o_inter).reshape(b_, h_, s_, dv)

def neighbourhood_attention(q, k, v, rpb):
    b_, s_, _ = q.shape
    rows = s_ // GRID_W
    kh = min(NA_KH, rows)
    grid = lambda t: t.reshape(b_, rows, GRID_W, NA_HEADS, NA_DH).astype(F32)
    qg = grid(q) * (NA_DH ** -0.5)
    kg = grid(k)
    vg = grid(v)
    r = jnp.arange(rows)
    row_idx = jnp.clip(r - kh // 2, 0, rows - kh)[:, None] + jnp.arange(kh)[None, :]
    c = jnp.arange(GRID_W)
    col_start = jnp.clip(c - NA_KW // 2, 0, GRID_W - NA_KW)
    col_ok = (c[None, :] >= col_start[:, None]) & (c[None, :] < col_start[:, None] + NA_KW)
    k_band = jnp.take(kg, row_idx, axis=1)
    v_band = jnp.take(vg, row_idx, axis=1)
    scores = jnp.einsum('brchd,brawhd->bhrcaw', qg, k_band)
    dr = row_idx - r[:, None] + NA_KH - 1
    dc = jnp.clip(c[None, :] - c[:, None] + NA_KW - 1, 0, 2 * NA_KW - 2)
    bias = rpb.astype(F32)[:, dr[:, None, :, None], dc[None, :, None, :]]
    scores = jnp.where(col_ok[:, None, :], scores + bias[None], -jnp.inf)
    shp = scores.shape
    p = jax.nn.softmax(scores.reshape(shp[:4] + (kh * GRID_W,)), axis=-1).reshape(shp)
    out = jnp.einsum('bhrcaw,brawhd->brchd', p, v_band)
    return out.reshape(b_, s_, GROUP_W)

def hybrid_mixer(hn, w_in, conv_w, gate_b, lb, rpb, group_gain, w_out):
    b_, s_, _ = hn.shape
    split_at = np.cumsum(IN_SIZES)[:-1].tolist()
    (mq, mk, mv, mo, mg, hq, hff, hfb, hi, hg, fu, nq, nk, nv) = jnp.split(hn @ w_in, split_at, axis=-1)
    flip = lambda t: jnp.flip(t, axis=2)

    qk = jax.nn.silu(centred_dwconv(jnp.concatenate([mq, mk], axis=-1), conv_w))
    q = to_heads(qk[..., :GROUP_W], ML_HEADS)
    k = to_heads(qk[..., GROUP_W:], ML_HEADS) * (ML_DH ** -0.5)
    v = to_heads(mv, ML_HEADS)
    gates = (mg.astype(F32) + gate_b.astype(F32)).reshape(b_, s_, 4, ML_HEADS).transpose(2, 0, 3, 1)
    h_fwd = mlstm_chunkwise(q, k, v, gates[0], gates[1])
    h_bwd = flip(mlstm_chunkwise(flip(q), flip(k), flip(v), flip(gates[2]), flip(gates[3])))
    y_ml = jax.nn.sigmoid(mo.astype(F32)) * merge_heads(h_fwd + h_bwd)

    lb = lb.astype(F32)
    hq_ = to_heads(jax.nn.silu(hq.astype(F32)), HG_HEADS)
    hi_ = to_heads(hi, HG_HEADS)

    def forget(fp):
        fp = fp.astype(F32)
        logf = jnp.logaddexp(jnp.log(lb), jnp.log1p(-lb) + jax.nn.log_sigmoid(fp))
        kk = (1.0 - lb) * jax.nn.sigmoid(-fp)
        return to_heads(logf, HG_HEADS), to_heads(kk, HG_HEADS)

    lf_f, k_f = forget(hff)
    lf_b, k_b = forget(hfb)
    o = hgrn2_chunkwise(hq_, k_f, hi_, lf_f) + flip(hgrn2_chunkwise(flip(hq_), flip(k_b), flip(hi_), flip(lf_b)))
    o = o * lax.rsqrt(jnp.mean(o * o, axis=-1, keepdims=True) + EPS)
    y_hg = merge_heads(o) * jax.nn.silu(hg.astype(F32))

    u = fu.astype(F32).reshape(b_, s_, FN_GROUPS, FN_CH)
    y_fn = jnp.fft.fft2(u, axes=(1, 3), norm='ortho').real.reshape(b_, s_, GROUP_W)

    y_na = neighbourhood_attention(nq, nk, nv, rpb)

    y = jnp.concatenate([y_ml, y_hg, y_fn, y_na], axis=-1).reshape(b_, s_, N_MIXERS, GROUP_W)
    y = rms_norm(y, group_gain.reshape(N_MIXERS, GROUP_W)).reshape(b_, s_, D_MODEL)
    return y.astype(hn.dtype) @ w_out

def memory_cross_attention(hn, mem_n, wq, wk, wv, wo):
    b_, s_, _ = hn.shape
    m_ = mem_n.shape[1]
    q = (hn @ wq).reshape(b_, s_, XA_HEADS, XA_DH)
    k = (mem_n @ wk).reshape(b_, m_, XA_HEADS, XA_DH)
    v = (mem_n @ wv).reshape(b_, m_, XA_HEADS, XA_DH)
    sc = jnp.einsum('bshd,bmhd->bhsm', q, k).astype(F32) * (XA_DH ** -0.5)
    p = jax.nn.softmax(sc, axis=-1).astype(v.dtype)
    o = jnp.einsum('bhsm,bmhd->bshd', p, v).reshape(b_, s_, D_MODEL)
    return o @ wo

def hierarchical_moe(hn, w_rg, w_re, w1, w3, w2):
    b_, s_, d_ = hn.shape
    n = b_ * s_
    xf = hn.reshape(n, d_)
    p_group = jax.nn.softmax((xf @ w_rg).astype(F32), axis=-1)
    g_idx = jnp.argmax(p_group, axis=-1)
    g_gate = jnp.take_along_axis(p_group, g_idx[:, None], axis=-1)
    fine = (xf @ w_re).astype(F32).reshape(n, MOE_GROUPS, MOE_PER_GROUP)
    fine = jnp.take_along_axis(fine, g_idx[:, None, None], axis=1)[:, 0]
    top_v, top_i = lax.top_k(fine, MOE_TOPK)
    gate = g_gate * jax.nn.softmax(top_v, axis=-1)
    expert = g_idx[:, None].astype(jnp.int32) * MOE_PER_GROUP + top_i.astype(jnp.int32)
    a_ = n * MOE_TOPK
    e_flat = expert.reshape(a_)
    tok = jnp.repeat(jnp.arange(n, dtype=jnp.int32), MOE_TOPK)
    w_flat = gate.reshape(a_)
    order = jnp.argsort(e_flat)
    e_s = e_flat[order]
    tok_s = tok[order]
    w_s = w_flat[order]
    counts = jnp.bincount(e_flat, length=MOE_EXPERTS)
    padded = (counts + MOE_BLOCK - 1) // MOE_BLOCK * MOE_BLOCK
    pad_end = jnp.cumsum(padded)
    pad_start = pad_end - padded
    start = jnp.cumsum(counts) - counts
    dest = pad_start[e_s] + jnp.arange(a_, dtype=jnp.int32) - start[e_s]
    nb = -(-a_ // MOE_BLOCK) + MOE_EXPERTS
    p_ = nb * MOE_BLOCK
    slot_tok = jnp.full((p_,), n, dtype=jnp.int32).at[dest].set(tok_s)
    slot_w = jnp.zeros((p_,), F32).at[dest].set(w_s)
    block_e = jnp.minimum(jnp.searchsorted(pad_end, jnp.arange(nb) * MOE_BLOCK, side='right'), MOE_EXPERTS - 1)
    xb = jnp.concatenate([xf, jnp.zeros((1, d_), xf.dtype)], axis=0)[slot_tok].reshape(nb, MOE_BLOCK, d_)

    def expert_block(args):
        xblk, e = args
        return (jax.nn.silu(xblk @ w1[e]) * (xblk @ w3[e])) @ w2[e]

    yb = lax.map(expert_block, (xb, block_e)).reshape(p_, d_)
    y = jnp.zeros((n + 1, d_), F32).at[slot_tok].add(yb.astype(F32) * slot_w[:, None])[:n]
    return y.astype(hn.dtype).reshape(b_, s_, d_)

def setup_inputs(seed: int = 0) -> dict:
    key = jax.random.key(seed)
    ks = jax.random.split(key, 24)
    nrm = lambda k, shape, scale: jax.random.normal(k, shape, F32) * scale
    gain = lambda k, shape: 1.0 + 0.02 * jax.random.normal(k, shape, F32)
    gate_base = jnp.tile(jnp.concatenate([jnp.zeros((ML_HEADS,), F32), jnp.linspace(3.0, 6.0, ML_HEADS, dtype=F32)]), 2)
    dsc = D_MODEL ** -0.5
    return {
        'x': nrm(ks[0], (BATCH, SEQ, D_MODEL), 1.0),
        'mem': nrm(ks[1], (BATCH, MEM_LEN, D_MODEL), 1.0),
        'norm_mix': gain(ks[2], (DEPTH, D_MODEL)),
        'norm_cross': gain(ks[3], (DEPTH, D_MODEL)),
        'norm_ffn': gain(ks[4], (DEPTH, D_MODEL)),
        'norm_final': gain(ks[5], (D_MODEL,)),
        'norm_mem': gain(ks[6], (D_MODEL,)),
        'w_in': nrm(ks[7], (DEPTH, D_MODEL, IN_W), dsc),
        'mlstm_conv': nrm(ks[8], (DEPTH, ML_CONV, 2 * GROUP_W), ML_CONV ** -0.5),
        'mlstm_gate_bias': gate_base[None, :] + nrm(ks[9], (DEPTH, 4 * ML_HEADS), 0.1),
        'hgrn_lower_bound': nrm(ks[10], (DEPTH, GROUP_W), 0.1),
        'na_rpb': nrm(ks[11], (DEPTH, NA_HEADS, 2 * NA_KH - 1, 2 * NA_KW - 1), 0.05),
        'group_gain': gain(ks[12], (DEPTH, D_MODEL)),
        'w_out': nrm(ks[13], (DEPTH, D_MODEL, D_MODEL), dsc),
        'xa_wq': nrm(ks[14], (DEPTH, D_MODEL, D_MODEL), dsc),
        'xa_wk': nrm(ks[15], (DEPTH, D_MODEL, D_MODEL), dsc),
        'xa_wv': nrm(ks[16], (DEPTH, D_MODEL, D_MODEL), dsc),
        'xa_wo': nrm(ks[17], (DEPTH, D_MODEL, D_MODEL), dsc),
        'moe_router_group': nrm(ks[18], (DEPTH, D_MODEL, MOE_GROUPS), dsc),
        'moe_router_expert': nrm(ks[19], (DEPTH, D_MODEL, MOE_EXPERTS), dsc),
        'moe_w1': nrm(ks[20], (DEPTH, MOE_EXPERTS, D_MODEL, MOE_FF), dsc),
        'moe_w3': nrm(ks[21], (DEPTH, MOE_EXPERTS, D_MODEL, MOE_FF), dsc),
        'moe_w2': nrm(ks[22], (DEPTH, MOE_EXPERTS, MOE_FF, D_MODEL), MOE_FF ** -0.5),
    }

def reference(x, mem, norm_mix, norm_cross, norm_ffn, norm_final, norm_mem, w_in, mlstm_conv,
              mlstm_gate_bias, hgrn_lower_bound, na_rpb, group_gain, w_out, xa_wq, xa_wk, xa_wv, xa_wo,
              moe_router_group, moe_router_expert, moe_w1, moe_w3, moe_w2):
    mem_n = rms_norm(mem, norm_mem)
    lbs = jnp.cumsum(jax.nn.softmax(hgrn_lower_bound.astype(F32), axis=0), axis=0)
    lbs = lbs - lbs[0]
    h = x
    for l in range(DEPTH):
        h = h + hybrid_mixer(rms_norm(h, norm_mix[l]), w_in[l], mlstm_conv[l], mlstm_gate_bias[l],
                             lbs[l], na_rpb[l], group_gain[l], w_out[l])
        h = h + memory_cross_attention(rms_norm(h, norm_cross[l]), mem_n, xa_wq[l], xa_wk[l], xa_wv[l], xa_wo[l])
        h = h + hierarchical_moe(rms_norm(h, norm_ffn[l]), moe_router_group[l], moe_router_expert[l],
                                 moe_w1[l], moe_w3[l], moe_w2[l])
    return rms_norm(h, norm_final)


_drawn_inputs = setup_inputs


def setup_inputs(seed=0):
    import zlib

    import numpy as np

    out = dict(_drawn_inputs(seed))
    spreads = {}
    factors = {'norm_cross': 8.0, 'norm_final': 7.543, 'norm_mem': 8.0, 'na_rpb': 2.695, 'norm_ffn': 8.0}
    for name, (base, spread) in spreads.items():
        noise = np.random.default_rng([zlib.crc32(name.encode()), seed]).standard_normal(out[name].shape)
        drawn = base * np.exp(spread * noise) if base else spread * noise
        out[name] = jnp.asarray(drawn.astype(out[name].dtype))
    for name, factor in factors.items():
        out[name] = (out[name] * factor).astype(out[name].dtype)
    return out
```

```python
from contextlib import ExitStack

import numpy as np

import concourse.bass as bass
from concourse import mybir

ALU = mybir.AluOpType
ACT = mybir.ActivationFunctionType
AX = mybir.AxisListType
F32 = mybir.dt.float32
I32 = mybir.dt.int32
U32 = mybir.dt.uint32
U8 = mybir.dt.uint8

P = 128
D = 2048
KT = D // P
T = 256
NT = T // P
GW = 512
NH = 4
CH = 4
NCH = KT // CH
RING_A = 4
FF = 512
NE = 32
NG = 4
PG = NE // NG
ECH = 12
EB = 96
OVK = -(-(T - EB) // EB)
OVB = 2 * T // EB
SLOTS = 2 * T
EPS = 1e-6
GRID_W = 64
NA_H = 8
NA_D = 64
NA_KW = 16
RPB_R, RPB_C = 15, 31
XA_H = 4
XA_D = D // XA_H
NEG = -1.0e30
LOWEST = -3.0e38

W_IN = [
    ("mq", True, 0, 1.0), ("mk", True, 512, 1.0), ("mv", False, 1024, 1.0), ("mo", False, 1536, 1.0),
    ("hq", True, 2064, 1.0), ("hff", True, 2576, 1.0), ("hfb", True, 3088, 1.0), ("hi", False, 3600, 1.0),
    ("hg", False, 4112, 1.0), ("fu", True, 4624, 1.0), ("nq", True, 5136, NA_D ** -0.5), ("nk", True, 5648, 1.0),
    ("nv", False, 6160, 1.0),
]
G_COL = 2048
G_IN = len(W_IN)
G_WK, G_WV, G_WO, G_WQ, G_XO = G_IN, G_IN + 4, G_IN + 8, G_IN + 12, G_IN + 16

HG_LEVELS = 8


def constants():
    c = np.arange(P)
    ang = 2 * np.pi * np.outer(c, c) / P
    s = np.arange(T)
    angs = 2 * np.pi * np.outer(s, s) / T
    norm = 1.0 / np.sqrt(T * P)
    tok = lambda m: m.reshape(NT, P, T).transpose(1, 0, 2).reshape(P, NT * T)
    dft = np.concatenate([np.cos(ang), np.sin(ang), tok(np.cos(angs) * norm), tok(-np.sin(angs) * norm)], 1)
    flip = np.eye(P)[::-1]
    fwd = np.where(c[:, None] <= c[None, :], 0.0, NEG)
    bwd = np.where(c[:, None] >= c[None, :], 0.0, NEG)
    selh = np.zeros((P, NH, P))
    for h in range(NH):
        selh[h, h] = 1.0
    col = np.arange(GRID_W)
    start = np.clip(col - NA_KW // 2, 0, GRID_W - NA_KW)
    ok = (col[None] >= start[:, None]) & (col[None] < start[:, None] + NA_KW)
    win = np.tile(np.where(ok, 0.0, NEG), (NT, 1))
    mix = np.concatenate([flip, fwd, bwd, selh.reshape(P, -1), win], 1)
    masks = np.zeros((P, 2, HG_LEVELS - 1, P), np.float32)
    for lev in range(HG_LEVELS - 1):
        h = 1 << lev
        same = (c[:, None] // (2 * h)) == (c[None, :] // (2 * h))
        odd = (c // h) % 2
        masks[:, 0, lev] = same & (odd[:, None] == 0) & (odd[None, :] == 1)
        masks[:, 1, lev] = same & (odd[:, None] == 1) & (odd[None, :] == 0)
    before = (c[:, None] < c[None, :]) * 1.0
    route = np.concatenate([before, np.ones((P, P)), np.tile(np.arange(SLOTS), (P, 1)), c[:, None] * 1.0], 1)
    return {"c_dft": dft.astype(np.float32), "c_mix": mix.astype(np.float32),
            "c_eye": np.eye(P, dtype=np.float32),
            "c_masks": masks.reshape(P, -1), "c_route": route.astype(np.float32)}


class Arena:

    def __init__(self, tensor):
        self.t = tensor

    def __call__(self, kib, *shape, parts=P):
        a = int(round(kib * 256))
        n = int(np.prod(shape))
        v = self.t[0:parts, a:a + n]
        if len(shape) == 2:
            v = v.rearrange("p (a b) -> p a b", b=shape[1])
        if len(shape) == 3:
            v = v.rearrange("p (a b c) -> p a b c", b=shape[1], c=shape[2])
        if len(shape) == 4:
            v = v.rearrange("p (a b c d) -> p a b c d", b=shape[1], c=shape[2], d=shape[3])
        return v


def flat(v):
    if len(v.shape) == 3:
        return v.rearrange("p a b -> p (a b)")
    return v.rearrange("p a b c -> p (a b c)")


def bc_mid(v, n):
    return v.unsqueeze(1).to_broadcast([v.shape[0], n, v.shape[1]])


def bc_last(v, n):
    return v.unsqueeze(2).to_broadcast([v.shape[0], v.shape[1], n])


def program(nc, ins, out, dbg=None):
    dbg = dbg or {}
    with ExitStack() as ctx:
        def sb(name, shape, dt=F32):
            return ctx.enter_context(nc.sbuf_tensor(name, shape, dt))

        def sem(name):
            return ctx.enter_context(nc.semaphore(name))

        arena = Arena(sb("arena", [P, 200 * 256]))
        ident = sb("ident", [P, P])
        cols = sb("cols", [P, 104])
        table = sb("table", [1, 128], I32)
        diag = sb("diag", [P, NT, P])
        st = sb("stats", [P, 64])
        hmask = sb("hmask", [P, 2 * (HG_LEVELS - 1) * P], U8).rearrange("p (d l t) -> p d l t", d=2, t=P)
        ps = ctx.enter_context(nc.psum_tensor("ps", [P, 8, 512], F32))

        h = arena(0, NT, D)
        ring_a = [arena(16 + 8 * i, CH, 512) for i in range(RING_A)]
        xT = arena(48, KT, T)
        memT = arena(64, KT, T)
        mem = arena(80, NT, D)
        y = mem
        kT = arena(96, KT, T)
        v = arena(112, NT, D)
        buf = {}
        buf["q"], buf["k"] = arena(128, NH, T), arena(132, NH, T)
        buf["mv"] = arena(136, NT, NH, P + 1)
        o = 140.25
        for n in ("mo", "hq", "hff", "hfb", "hi", "hg", "fu", "nq", "nk", "nv"):
            a_form = n in ("mo", "hi", "hg", "nv")
            buf[n] = arena(o, NT, GW) if a_form else arena(o, NH, T)
            o += 4
        buf["mq"], buf["mk"] = arena(112, NH, T), arena(116, NH, T)
        decay_to = arena(180.25, NT, NH, T)
        hmask_f = arena(180.25, 2 * (HG_LEVELS - 1) * P)
        dft_c = arena(188.25, 2 * P)
        dft_t = arena(189.25, 2, NT, T)
        mixc = arena(193.25, 7 * P + GRID_W)
        flipm, tri = mixc[:, 0:P], [mixc[:, P:2 * P], mixc[:, 2 * P:3 * P]]
        selh = mixc[0:NH, 3 * P:7 * P].rearrange("p (h t) -> p h t", h=NH)
        win = mixc[:, 7 * P:]
        wg = arena(197, KT, 16)
        rows = arena(198, P)
        gt = arena(120, NH, T, parts=NH)
        gl = arena(124, 2, T, parts=NH)
        lf = arena(126, 2, T, parts=NH)
        gb = arena(96, 2, T, parts=NH)
        gr = arena(98, NH, T, parts=NH)
        gm = arena(102, 2, T, parts=NH)
        gone = arena(104, T)
        gtok = arena(105, NT, 16)
        gbias = st[0:NH, 56:60]
        mlc = arena(106, NT, 4, NH)
        mw = [arena(107, 3, P), arena(108.5, 3, P)]
        msw = [arena(110, 3, P), arena(120, 3, P)]
        marg = [arena(122, T), arena(123, T)]
        mt_ = arena(121.5, P)
        fa = arena(112, NT, NH, 2, P)
        hb = [arena(48, NH, T), arena(52, NH, T)]
        hqk = [arena(56, NH, T), arena(60, NH, T)]
        he = [arena(112, NH, T), arena(116, NH, T)]
        htmp = arena(120, NH, T)
        hone = arena(124, T)
        nbias = [arena(144.25, 2, T), arena(146.25, 2, T)]
        ns, npr, npt = arena(148.25, 2, T), arena(150.25, 2, T), arena(152.25, 2, NT, P)
        qT = arena(80, KT, T)
        oT = memT
        xp, xpt = arena(128, NT, T), arena(130, NT, T)
        xsT = arena(16, KT, SLOTS + EB)
        ysT = arena(54, KT, SLOTS + EB)
        xe = arena(92, KT, EB)
        selgT = arena(98, SLOTS // P, T)
        sg, hT = sb("sg", [P, FF // P, EB]), sb("hT", [P, FF // P, EB])
        sel_r, sel_g, sel_t = arena(64, NT, SLOTS), arena(68, NT, SLOTS), arena(78, SLOTS)
        wr = arena(101, KT, 36)
        rt = arena(72, 1024)
        routec = arena(80, 2 * P + SLOTS + 1)
        before, ones, iota, iotap = (routec[:, 0:P], routec[:, P:2 * P], routec[:, 2 * P:2 * P + SLOTS],
                                     routec[:, 2 * P + SLOTS:])
        r_at = [0]

        def small(*shape):
            a = r_at[0]
            r_at[0] += int(np.prod(shape))
            assert r_at[0] <= 1024
            vv = rt[:, a:r_at[0]]
            return vv.rearrange("p (a b) -> p a b", b=shape[1]) if len(shape) == 2 else vv

        logit, lgrp, gmax8, fine, fmax8 = small(NT, 36), small(NT, 8), small(NT, 8), small(NT, 8), small(NT, 8)
        gidx8, fidx8 = small(NT, 8).bitcast(U32), small(NT, 8).bitcast(U32)
        hit0, hit1, hit, rank = small(NT, NE), small(NT, NE), small(NT, NE), small(3, NE)
        hits, n_first, n_over, st_first, st_over, st_gap, blocks, blk_in, rtmp = [small(NE) for _ in range(9)]
        ftmp = small(NT, 8)
        egrp, gsum, ggate, vdif, w0, w1, e0, e1, slot0, slot1, negm, goh = [small(NT) for _ in range(12)]
        goh4 = small(NT, 4)
        eid, ost, gexp = small(1), small(1), small(4)
        slot_kib = [136 + 8 * i for i in range(8)] + [104 + 8 * i for i in range(4)]
        ering = [arena(k, CH, 512) for k in slot_kib]
        ys = arena(16, SLOTS // P, D)
        fgain = arena(136, D)
        res = arena(144, NT, D)

        def bank(b, *shape):
            w = int(np.prod(shape))
            vv = ps[:, b, 0:w]
            if len(shape) == 2:
                return vv.rearrange("p (a b) -> p a b", b=shape[1])
            if len(shape) == 3:
                return vv.rearrange("p (a b c) -> p a b c", b=shape[1], c=shape[2])
            return vv

        S = {}
        for n in ["x_in", "mem_in", "eye_in", "rows_in", "cmix_in", "cdft_in", "cmask_in", "wg_in", "gbias_in",
                  "bias_in0", "bias_in1", "route_in", "wr_in", "fgain_in", "out_done",
                  "chunk_used", "proj_pe", "proj_a", "proj_b", "act_step", "dve_step", "pool_step",
                  "sq_act", "var_dve", "rs_act", "diag_dve", "tp_pe", "tp_act", "tp_dve", "cols_pe", "cols_act",
                  "conv_dve", "silu_act", "gate_pe", "gate_dve", "gate_act", "ml_pe_s", "ml_pe_m", "ml_arg",
                  "ml_w", "ml_sw", "ml_pv", "ml_den", "ml_y", "fn_pe", "fn_act", "fn_dve",
                  "hp_act", "hp_dve", "h_sub", "h_exp", "h_mulq", "h_mulk", "h_pe", "h_cp", "h_o", "h_oev",
                  "na_s", "na_m", "na_max", "na_p", "na_r", "na_t", "na_tev", "na_o", "na_y", "y_done", "y_act",
                  "xs_pe", "xs_max", "xs_p", "xs_diag", "xs_t", "xs_tev", "xs_o", "xs_oa", "xs_od",
                  "r_pe", "r_dve", "r_act", "g_pe", "g_act", "g_dve", "sg_pe", "sg_act", "tab_dve",
                  "e_used", "e_x", "e_w1", "e_w3", "e_sg", "e_h", "e_w2a", "e_w2", "e_ya", "e_yd",
                  "c_tp", "c_act", "c_dve", "c_pe", "c_add", "fin_dve"]:
            S[n] = sem(n)
        s_ring = [sem(f"ring_a{i}") for i in range(RING_A)]
        s_er = [sem(f"ering{i}") for i in range(ECH)]
        block = ctx.enter_context(nc.Block())

        w_src = {G_WK: "xa_wk", G_WV: "xa_wv", G_WO: "w_out", G_WQ: "xa_wq", G_XO: "xa_wo"}
        g1, g3, g2 = ins["moe_w1"][0], ins["moe_w3"][0], ins["moe_w2"][0]

        def dense_chunk(g, i):
            if g < G_IN:
                w, c0 = ins["w_in"][0], W_IN[g][2]
            else:
                base = G_IN + 4 * ((g - G_IN) // 4)
                w, c0 = ins[w_src[base]][0], 512 * (g - base)
            return w[i * CH * P:(i + 1) * CH * P, c0:c0 + 512].rearrange("(c p) n -> p c n", p=P)

        def expert_chunk(e, i):
            w = (g1, g3, g2)[i // 4]
            w = w[e] if isinstance(e, int) else w[bass.ds(e, 1)].rearrange("a k n -> (a k) n")
            q = i % 4
            if i < 8:
                return w[q * CH * P:(q + 1) * CH * P, :].rearrange("(c p) n -> p c n", p=P)
            return w[:, q * 512:(q + 1) * 512].rearrange("(c p) n -> p c n", p=P)

        @block.sync
        def _(sp):
            sp.dma_start(ident[:], ins["c_eye"]).then_inc(S["eye_in"], 16)
            for n, name in enumerate(["norm_mix", "norm_cross", "norm_ffn", "norm_mem", "group_gain"]):
                src = ins[name] if name == "norm_mem" else ins[name][0]
                sp.dma_start(rows[n * KT:(n + 1) * KT, :], src.rearrange("(k p) -> k p", p=P)).then_inc(S["rows_in"], 16)
            sp.dma_start(rows[80:104, :], ins["mlstm_conv"][0].rearrange("t (c p) -> (t c) p", p=P)).then_inc(S["rows_in"], 16)
            sp.dma_start(h, ins["x"][0].rearrange("(j p) d -> p j d", p=P)).then_inc(S["x_in"], 16)
            sp.dma_start(mem, ins["mem"][0].rearrange("(j p) d -> p j d", p=P)).then_inc(S["mem_in"], 16)

            def load_dense(g):
                for i in range(NCH):
                    c = g * NCH + i
                    if c >= RING_A:
                        sp.wait_ge(S["chunk_used"], c - RING_A + 1)
                    sp.dma_start(ring_a[i], dense_chunk(g, i)).then_inc(s_ring[i], 16)

            for g in range(4):
                load_dense(g)
                if g == 0:
                    with nc.allow_non_contiguous_dma(reason="gate columns"):
                        sp.dma_start(wg, ins["w_in"][0][:, G_COL:G_COL + 16].rearrange("(c p) n -> p c n", p=P)).then_inc(S["wg_in"], 16)
                        sp.dma_start(gbias, ins["mlstm_gate_bias"][0].rearrange("(k h) -> h k", h=NH)).then_inc(S["gbias_in"], 16)
                    sp.dma_start(mixc, ins["c_mix"]).then_inc(S["cmix_in"], 16)
                    sp.dma_start(arena(188.25, 5 * 256), ins["c_dft"]).then_inc(S["cdft_in"], 16)
                    sp.dma_start(hmask_f, ins["c_masks"]).then_inc(S["cmask_in"], 16)
            for g in range(4, G_WO):
                load_dense(g)
            sp.wait_ge(S["y_done"], 4)
            for i in range(8):
                sp.dma_start(ering[i], expert_chunk(0, i)).then_inc(s_er[i], 16)
            for g in range(G_WO, G_XO + 4):
                load_dense(g)
            sp.wait_ge(S["xs_o"], XA_H)
            for i in range(8, ECH):
                sp.dma_start(ering[i], expert_chunk(0, i)).then_inc(s_er[i], 16)
            with nc.allow_non_contiguous_dma(reason="router columns"):
                sp.dma_start(wr[:, :, 0:NG], ins["moe_router_group"][0].rearrange("(c p) n -> p c n", p=P)).then_inc(S["wr_in"], 16)
                sp.dma_start(wr[:, :, NG:], ins["moe_router_expert"][0].rearrange("(c p) n -> p c n", p=P)).then_inc(S["wr_in"], 16)
            sp.dma_start(routec, ins["c_route"]).then_inc(S["route_in"], 16)
            with sp.Fori(1, NE) as e:
                for i in range(ECH):
                    sp.wait_ge(S["e_used"], e * ECH + (i + 1 - ECH))
                    sp.dma_start(ering[i], expert_chunk(e, i)).then_inc(s_er[i], 16)
            sp.wait_ge(S["tab_dve"], 2)
            nov = sp.value_load(table[0:1, 96:97], min_val=0, max_val=OVB)
            with sp.Fori(0, OVB) as b:
                with sp.If(b < nov):
                    e = sp.value_load(table[0:1, bass.ds(b + 32, 1)], min_val=0, max_val=NE - 1)
                    for i in range(ECH):
                        sp.wait_ge(S["e_used"], b * ECH + (NE * ECH + i + 1 - ECH))
                        sp.dma_start(ering[i], expert_chunk(e, i)).then_inc(s_er[i], 16)
            sp.wait_ge(S["c_tp"], 1)
            sp.dma_start(fgain, ins["norm_final"].rearrange("(a d) -> a d", a=1).to_broadcast([P, D])).then_inc(S["fgain_in"], 16)
            for j in range(NT):
                sp.wait_ge(S["fin_dve"], j + 1)
                sp.dma_start(out[0, j * P:(j + 1) * P, :], res[:, j, :]).then_inc(S["out_done"], 16)
            sp.wait_ge(S["out_done"], 16 * NT)

        @block.gpsimd
        def _(pool):
            nc.gpsimd.memset(gone, 1.0).then_inc(S["pool_step"], 1)
            nc.gpsimd.memset(buf["mv"][:, :, :, P:P + 1], 1.0).then_inc(S["pool_step"], 1)
            for s in range(2 * HG_LEVELS):
                w, half = s // HG_LEVELS, 1 << (s % HG_LEVELS)
                u = 0 if w == 0 else 1
                cut = lambda x: flat(x).rearrange("p (b u t) -> p b u t", u=2, t=half)[:, :, u, :]
                pool.wait_ge(S["h_exp"], s + 1)
                if s >= 1:
                    pool.wait_ge(S["h_pe"], s)
                nc.gpsimd.tensor_tensor(cut(hqk[s % 2]), cut(he[s % 2]), cut(buf["hff" if w == 0 else "hfb"]),
                                        ALU.mult).then_inc(S["h_mulk"], 1)
            rpb = ins["na_rpb"]
            for m in range(NA_H // 2 * NT):
                i, j = m // NT, m % NT
                if m == 0:
                    pool.wait_ge(S["h_pe"], 2 * HG_LEVELS + 1)
                    pool.wait_ge(S["h_mulk"], 2 * HG_LEVELS)
                    pool.wait_ge(S["h_mulq"], 2 * HG_LEVELS)
                if m >= 2:
                    pool.wait_ge(S["na_s"], m - 1)
                for g in range(2):
                    r = 2 * j + 1 - g
                    for u in range(2):
                        hd = 2 * i + u
                        src = bass.AP(tensor=rpb.tensor, offset=rpb.offset + hd * RPB_R * RPB_C + (7 - r) * RPB_C - 48,
                                      ap=[[1, GRID_W], [RPB_C, 4], [1, GRID_W]])
                        pool.dma_start(nbias[m % 2][g * 64:(g + 1) * 64, u, :].rearrange("p (a w) -> p a w", w=GRID_W),
                                       src).then_inc(S["bias_in0" if m % 2 == 0 else "bias_in1"], 16)
            pool.wait_ge(S["g_act"], KT // 2)
            pool.wait_ge(S["g_dve"], KT // 2 + 1)
            pool.wait_ge(S["tab_dve"], 2)

            def tokens_of(n, s):
                nc.gpsimd.tensor_copy(xe, xsT[:, :, bass.ds(s, EB)]).then_inc(S["e_x"], 1)

            s0 = pool.value_load(table[0:1, 0:1], min_val=0, max_val=SLOTS)
            tokens_of(0, s0)
            with pool.Fori(1, NE) as e:
                s = pool.value_load(table[0:1, bass.ds(e, 1)], min_val=0, max_val=SLOTS)
                pool.wait_ge(S["e_used"], e * ECH - 4)
                tokens_of(e, s)
            nov = pool.value_load(table[0:1, 96:97], min_val=0, max_val=OVB)
            with pool.Fori(0, OVB) as b:
                with pool.If(b < nov):
                    s = pool.value_load(table[0:1, bass.ds(b + 64, 1)], min_val=0, max_val=SLOTS)
                    pool.wait_ge(S["e_used"], b * ECH + (NE * ECH - 4))
                    tokens_of(b, s)

        @block.tensor
        def _(pe):
            mm = nc.tensor.matmul

            def turn(n, src, scales):
                for kk in range(KT // 2):
                    q = n * (KT // 2) + kk
                    if q >= 4:
                        pe.wait_ge(S["tp_act" if q % 2 == 0 else "tp_dve"], (q - 4) // 2 + 1)
                    o_ = bank(4 + kk % 4, 2, NT, P)
                    for u in range(2):
                        for j in range(NT):
                            k = 2 * kk + u
                            last = mm(o_[:, u, j, :], src[:, j, k * P:(k + 1) * P], scales[j], start=True, stop=True)
                    last.then_inc(S["tp_pe"], 1)

            def dense(g, feature_major, act, part=range(NCH)):
                b0 = 2 * (g % 2)
                for i in part:
                    if i == 0 and g >= 2:
                        pe.wait_ge(S["proj_a"], g - 1)
                        pe.wait_ge(S["proj_b"], g - 1)
                    pe.wait_ge(s_ring[i], 16 * (g + 1))
                    for c in range(CH):
                        k = i * CH + c
                        if feature_major:
                            for n in range(4):
                                last = mm(ps[:, b0 + n // 2, (n % 2) * T:(n % 2 + 1) * T], ring_a[i][:, c, n * P:(n + 1) * P],
                                          act[:, k, :], start=(k == 0 and n % 2 == 0), stop=(k == KT - 1),
                                          skip_group_check=True)
                        else:
                            for j in range(NT):
                                last = mm(ps[:, b0 + j, :], act[:, k, j * P:(j + 1) * P], ring_a[i][:, c, :],
                                          start=(k == 0), stop=(k == KT - 1))
                    last.then_inc(S["chunk_used"], 1)

            pe.wait_ge(S["eye_in"], 16)
            pe.wait_ge(S["rows_in"], 16 * 6)
            mm(ps[:, 0, 0:104], rows[0:104, :], ident[0:104, 0:104], start=True, stop=True).then_inc(S["cols_pe"], 1)
            pe.wait_ge(S["x_in"], 16)
            pe.wait_ge(S["diag_dve"], 1)
            turn(0, h, [diag[:, j, :] for j in range(NT)])
            pe.wait_ge(S["mem_in"], 16)
            pe.wait_ge(S["diag_dve"], 2)
            turn(1, mem, [diag[:, j, :] for j in range(NT)])
            pe.wait_ge(S["tp_act"], 8)
            pe.wait_ge(S["tp_dve"], 8)
            pe.wait_ge(S["cols_act"], 1)
            for g, (name, fm, _, _) in enumerate(W_IN):
                dense(g, fm, xT)
                if g == 3:
                    pe.wait_ge(S["wg_in"], 16)
                    for j in range(NT):
                        for k in range(KT):
                            last = mm(bank(4, NT, 16)[:, j, :], xT[:, k, j * P:(j + 1) * P], wg[:, k, :],
                                      start=(k == 0), stop=(k == KT - 1))
                    last.then_inc(S["gate_pe"], 1)
                    pe.wait_ge(S["gate_dve"], 1)
                    for kind in range(4):
                        for j in range(NT):
                            last = mm(ps[0:NH, 5 + kind // 2, (kind % 2) * T + j * P:(kind % 2) * T + (j + 1) * P],
                                      gtok[:, j, kind * NH:(kind + 1) * NH], ident[:], start=True, stop=True)
                    last.then_inc(S["gate_pe"], 1)
            pe.wait_ge(S["gate_dve"], 3)
            pe.wait_ge(S["gate_act"], 2)
            for j in range(NT):
                for kind in range(4):
                    last = mm(bank(4, NT, 4, NH)[:, j, kind, :], gr[:, kind, j * P:(j + 1) * P], ident[0:NH, 0:NH],
                              start=True, stop=True)
            last.then_inc(S["gate_pe"], 1)
            pe.wait_ge(S["cmix_in"], 16)
            pe.wait_ge(S["silu_act"], 2)
            pe.wait_ge(S["pool_step"], 2)
            pe.wait_ge(S["proj_a"], 3)
            pe.wait_ge(S["proj_b"], 3)
            pe.wait_ge(S["gate_dve"], 4)
            q, k = buf["q"], buf["k"]
            for hd in range(NH):
                if hd >= 1:
                    pe.wait_ge(S["ml_sw"], 2 * hd)
                    pe.wait_ge(S["ml_w"], 2 * hd)
                for u in range(NT):
                    last = mm(bank(4, NT, T)[:, u, :], k[:, hd, u * P:(u + 1) * P], q[:, hd, :], start=True, stop=True)
                last.then_inc(S["ml_pe_s"], 1)
                for w in range(2):
                    last = mm(bank(6, 2, T)[:, w, :], selh[:, hd, :], gm[:, w, :], start=True, stop=True)
                last.then_inc(S["ml_pe_m"], 1)
                for w in range(2):
                    pe.wait_ge(S["ml_sw"], 2 * hd + w + 1)
                    if hd >= 1:
                        pe.wait_ge(S["ml_y"], hd)
                        pe.wait_ge(S["ml_den"], 2 * hd)
                    o_ = bank(7 if w == 0 else 5, NT, P + 1)
                    parts = [(0, 0, 0, True, True), (1, 1, 0, True, False), (1, 2, 1, False, True)] if w == 0 else \
                            [(0, 0, 0, True, False), (0, 1, 1, False, True), (1, 2, 1, True, True)]
                    for j, tile, u, a, z in parts:
                        last = mm(o_[:, j, :], msw[w][:, tile, :], buf["mv"][:, u, hd, :], start=a, stop=z)
                    last.then_inc(S["ml_pv"], 1)
            pe.wait_ge(S["cdft_in"], 16)
            pe.wait_ge(S["proj_a"], G_IN)
            pe.wait_ge(S["proj_b"], G_IN)
            pe.wait_ge(S["ml_y"], NH)
            pe.wait_ge(S["ml_den"], 2 * NH)
            for j in range(NT):
                for g in range(NH):
                    last = mm(bank(4 + 2 * j + g // 2, 2, 2 * P)[:, g % 2, :], buf["fu"][:, g, j * P:(j + 1) * P], dft_c,
                              start=True, stop=True)
            last.then_inc(S["fn_pe"], 1)
            pe.wait_ge(S["fn_act"], 1)
            pe.wait_ge(S["fn_dve"], 1)
            for j in range(NT):
                for n, (tab, u) in enumerate([(0, 0), (0, 1), (1, 0), (1, 1)]):
                    last = mm(ps[:, 4 + j, :], dft_t[:, tab, u, j * P:(j + 1) * P], fa[:, u, :, tab, :],
                              start=(n == 0), stop=(n == 3))
            last.then_inc(S["fn_pe"], 1)
            pe.wait_ge(S["fn_act"], 2)
            pe.wait_ge(S["fn_dve"], 2)
            pe.wait_ge(S["hp_dve"], 3)
            pe.wait_ge(S["hp_act"], 8)
            pe.wait_ge(S["silu_act"], 4)
            for hd in range(NH):
                for u in range(NT):
                    last = mm(bank(4 + u, NH, P)[:, hd, :], hqk[1][:, hd, u * P:(u + 1) * P],
                              buf["hq"][:, hd, u * P:(u + 1) * P], start=True, stop=True)
            last.then_inc(S["h_pe"], 1)
            for s in range(2 * HG_LEVELS):
                w, lev = s // HG_LEVELS, s % HG_LEVELS
                dense(G_WK + s // 4, True, memT, part=[s % 4])
                pe.wait_ge(S["h_mulq"], s + 1)
                pe.wait_ge(S["h_mulk"], s + 1)
                if s >= 1:
                    pe.wait_ge(S["h_cp"], s)
                qk = hqk[s % 2]
                b0 = 6 - 2 * (s % 2)
                for hd in range(NH):
                    if lev < HG_LEVELS - 1:
                        for u in range(NT):
                            t_ = qk[:, hd, u * P:(u + 1) * P]
                            last = mm(bank(b0 + u, NH, P)[:, hd, :], t_, t_, start=True, stop=True)
                    else:
                        a, z = qk[:, hd, 0:P], qk[:, hd, P:2 * P]
                        last = mm(bank(b0, NH, P)[:, hd, :], *((a, z) if w == 0 else (z, a)), start=True, stop=True)
                last.then_inc(S["h_pe"], 1)
            pe.wait_ge(S["h_cp"], 2 * HG_LEVELS + 1)
            for j in range(NT):
                for hd in range(NH):
                    for u in range(NT):
                        last = mm(bank(4 + j, NH, P)[:, hd, :], decay_to[:, u, hd, j * P:(j + 1) * P],
                                  buf["hi"][:, u, hd * P:(hd + 1) * P], start=(u == 0), stop=(u == NT - 1))
            last.then_inc(S["h_o"], 1)
            for m in range(NA_H // 2 * NT):
                i, j = m // NT, m % NT
                dense(G_WV + m // 2, False, memT, part=[2 * (m % 2), 2 * (m % 2) + 1])
                if m == 0:
                    pe.wait_ge(S["h_oev"], 2)
                else:
                    pe.wait_ge(S["na_m"], m)
                pe.wait_ge(S["bias_in0" if m % 2 == 0 else "bias_in1"], 64 * (m // 2 + 1))
                for u in range(2):
                    o_ = ps[:, 4 + 3 * u, 0:T]
                    mm(o_, flipm, nbias[m % 2][:, u, :], start=True, stop=False)
                    last = mm(o_, buf["nq"][64 * u:64 * u + 64, i, j * P:(j + 1) * P], buf["nk"][64 * u:64 * u + 64, i, :],
                              start=False, stop=True)
                last.then_inc(S["na_s"], 1)
                pe.wait_ge(S["na_p"], 2 * (m + 1))
                if m >= 1:
                    pe.wait_ge(S["na_tev"], m)
                for u in range(2):
                    for s in range(NT):
                        last = mm(bank(5, 2, NT, P)[:, u, s, :], npr[:, u, s * P:(s + 1) * P], ident[:], start=True, stop=True)
                last.then_inc(S["na_t"], 1)
                pe.wait_ge(S["na_tev"], m + 1)
                if m >= 1:
                    pe.wait_ge(S["na_y"], 2 * m)
                for u in range(2):
                    for s in range(NT):
                        last = mm(bank(6, 2, NA_D)[:, u, :], npt[:, u, s, :], buf["nv"][:, s, (2 * i + u) * NA_D:(2 * i + u + 1) * NA_D],
                                  start=(s == 0), stop=(s == NT - 1))
                last.then_inc(S["na_o"], 1)
            pe.wait_ge(S["y_done"], 4)
            turn(2, y, [ident[:]] * 2)
            pe.wait_ge(S["tp_act"], 12)
            pe.wait_ge(S["tp_dve"], 12)
            for g in range(4):
                dense(G_WO + g, False, memT)
            pe.wait_ge(S["diag_dve"], 3)
            turn(3, h, [diag[:, j, :] for j in range(NT)])
            pe.wait_ge(S["tp_act"], 16)
            pe.wait_ge(S["tp_dve"], 16)
            for g in range(4):
                dense(G_WQ + g, True, xT)
            pe.wait_ge(S["proj_a"], G_WQ + 4)
            pe.wait_ge(S["proj_b"], G_WQ + 4)

            def xa_scores(hd):
                if hd >= 1:
                    pe.wait_ge(S["xs_p"], 2 * hd)
                for j in range(NT):
                    for c in range(NH):
                        last = mm(bank(4, NT, T)[:, j, :], qT[:, 4 * hd + c, j * P:(j + 1) * P], kT[:, 4 * hd + c, :],
                                  start=(c == 0), stop=(c == NH - 1))
                last.then_inc(S["xs_pe"], 1)

            for hd in range(XA_H):
                xa_scores(hd)
                pe.wait_ge(S["xs_diag"], hd + 1)
                if hd >= 1:
                    pe.wait_ge(S["xs_tev"], hd)
                for s in range(NT):
                    for j in range(NT):
                        last = mm(bank(5, NT, NT, P)[:, s, j, :], xp[:, j, s * P:(s + 1) * P], diag[:, j, :], start=True, stop=True)
                last.then_inc(S["xs_t"], 1)
                pe.wait_ge(S["xs_tev"], hd + 1)
                if hd >= 1:
                    pe.wait_ge(S["xs_oa"], hd)
                    pe.wait_ge(S["xs_od"], hd)
                for c in range(NH):
                    for s in range(NT):
                        last = mm(bank(6 + c // 2, 2, T)[:, c % 2, :], v[:, s, (4 * hd + c) * P:(4 * hd + c + 1) * P], xpt[:, s, :],
                                  start=(s == 0), stop=(s == NT - 1))
                last.then_inc(S["xs_o"], 1)
            pe.wait_ge(S["xs_oa"], XA_H)
            pe.wait_ge(S["xs_od"], XA_H)
            for g in range(4):
                dense(G_XO + g, False, oT)
            pe.wait_ge(S["diag_dve"], 4)
            turn(4, h, [diag[:, j, :] for j in range(NT)])
            pe.wait_ge(S["tp_act"], 20)
            pe.wait_ge(S["tp_dve"], 20)
            pe.wait_ge(S["wr_in"], 32)
            for j in range(NT):
                for k_ in range(KT):
                    last = mm(bank(4, NT, 36)[:, j, :], xT[:, k_, j * P:(j + 1) * P], wr[:, k_, :], start=(k_ == 0), stop=(k_ == KT - 1))
            last.then_inc(S["r_pe"], 1)
            pe.wait_ge(S["route_in"], 16)
            pe.wait_ge(S["r_dve"], 3)
            o_ = bank(5, 3, NE)
            mm(o_[:, 0, :], before, hit[:, 0, :], start=True, stop=True)
            mm(o_[:, 1, :], before, hit[:, 1, :], start=True, stop=False)
            mm(o_[:, 1, :], ones, hit[:, 0, :], start=False, stop=True)
            mm(o_[:, 2, :], ones, hits, start=True, stop=True).then_inc(S["r_pe"], 1)
            pe.wait_ge(S["r_dve"], 4)
            mm(ps[0:1, 6, 0:P], eid, ident[:], start=True, stop=True)
            mm(ps[0:1, 6, P:2 * P], ost, ident[:], start=True, stop=True).then_inc(S["r_pe"], 1)
            pe.wait_ge(S["tab_dve"], 1)
            for k_ in range(KT):
                if k_ >= 4:
                    pe.wait_ge(S["g_act" if k_ % 2 == 0 else "g_dve"], (k_ - 4) // 2 + 1)
                elif k_ == 2:
                    pe.wait_ge(S["tab_dve"], 2)
                for j in range(NT):
                    last = mm(ps[:, 4 + k_ % 4, :], h[:, j, k_ * P:(k_ + 1) * P], sel_r[:, j, :], start=(j == 0), stop=(j == NT - 1))
                last.then_inc(S["g_pe"], 1)
            pe.wait_ge(S["g_act"], KT // 2)
            pe.wait_ge(S["g_dve"], KT // 2 + 1)
            for s in range(SLOTS // P):
                for j in range(NT):
                    last = mm(bank(4 + s // 2, 2, NT, P)[:, s % 2, j, :], sel_g[:, j, s * P:(s + 1) * P], ident[:], start=True, stop=True)
            last.then_inc(S["sg_pe"], 1)
            def expert(n):
                pe.wait_ge(S["e_x"], n + 1)
                for half in range(2):
                    for i in range(4):
                        pe.wait_ge(s_er[4 * half + i], (n + 1) * 16)
                        for c in range(CH):
                            for f in range(FF // P):
                                first = i == 0 and c == 0 and f == 0
                                last = mm(bank(half, FF // P, EB)[:, f, :], ering[4 * half + i][:, c, f * P:(f + 1) * P],
                                          xe[:, i * CH + c, :], start=first, stop=(i == 3 and c == CH - 1), skip_group_check=True)
                        last.then_inc(S["e_used"], 1)
                pe.wait_ge(S["e_h"], n + 1)
                for i in range(4):
                    pe.wait_ge(s_er[8 + i], (n + 1) * 16)
                    if i == 0:
                        pe.wait_ge(S["e_ya"], n + 1)
                    if i == 1:
                        pe.wait_ge(S["e_yd"], n + 1)
                    for c in range(4):
                        for f in range(FF // P):
                            last = mm(bank(2 + i, 4, EB)[:, c, :], ering[8 + i][:, f, c * P:(c + 1) * P],
                                      hT[:, f, :], start=(f == 0), stop=(f == FF // P - 1))
                    last.then_inc(S["e_used"], 1)

            pe.wait_ge(S["sg_act"], 1)
            pe.wait_ge(S["proj_b"], G_XO + 4)
            with pe.Fori(0, NE) as e:
                expert(e)
            pe.wait_ge(S["tab_dve"], 2)
            nov = pe.value_load(table[0:1, 96:97], min_val=0, max_val=OVB)
            with pe.Fori(0, OVB) as b:
                with pe.If(b < nov):
                    expert(b + NE)
            nc.tensor.matmul(ps[:, 6, 0:P], ident[:], ident[:], start=True, stop=True).then_inc(S["c_tp"], 1)
            pe.wait_ge(S["c_act"], 1)
            pe.wait_ge(S["c_dve"], 1)
            n = 0
            for s in range(SLOTS // P):
                for kk in range(4):
                    if n >= 4:
                        pe.wait_ge(S["c_act" if n % 2 == 0 else "c_dve"], (n - 4) // 2 + 2)
                    for u in range(4):
                        k_ = 4 * kk + u
                        last = mm(ps[:, 4 + n % 4, u * P:(u + 1) * P], ysT[:, k_, s * P:(s + 1) * P], ident[:], start=True, stop=True)
                    last.then_inc(S["c_tp"], 1)
                    n += 1
            pe.wait_ge(S["c_act"], 9)
            pe.wait_ge(S["c_dve"], 9)
            for j in range(NT):
                for g in range(4):
                    m = 4 * j + g
                    if m >= 4:
                        pe.wait_ge(S["c_add"], m - 3)
                    for s in range(SLOTS // P):
                        last = mm(ps[:, m % 4, :], selgT[:, s, j * P:(j + 1) * P], ys[:, s, g * 512:(g + 1) * 512],
                                  start=(s == 0), stop=(s == SLOTS // P - 1))
                    last.then_inc(S["c_pe"], 1)

        @block.scalar
        def _(act):
            fn = nc.scalar.activation
            steps, calls = [0], [0]

            def step(ins_):
                steps[0] += 1
                ins_.then_inc(S["act_step"], 1)
                act.wait_ge(S["act_step"], steps[0])

            def squares(src):
                step(fn(flat(ps[:, 0:4, :]), src[:, 0, :], ACT.Square, accum_out=st[:, 0:1]))
                fn(flat(ps[:, 0:4, :]), src[:, 1, :], ACT.Square, accum_out=st[:, 1:2]).then_inc(S["sq_act"], 1)

            def rsqrt(w):
                calls[0] += 1
                act.wait_ge(S["var_dve"], calls[0])
                step(fn(st[:, 16:16 + w], st[:, 8:8 + w], ACT.Ln))
                fn(st[:, 24:24 + w], st[:, 16:16 + w], ACT.Exp, scale=-0.5).then_inc(S["rs_act"], 1)

            def turned(n, dst, gain):
                for kk in range(0, KT // 2, 2):
                    act.wait_ge(S["tp_pe"], n * (KT // 2) + kk + 1)
                    for u in range(2):
                        k = 2 * kk + u
                        last = fn(dst[:, k, :], ps[:, 4 + kk % 4, u * T:(u + 1) * T], ACT.Copy, scale=cols[:, gain * KT + k:gain * KT + k + 1])
                    last.then_inc(S["tp_act"], 1)

            def dense_out(g, dst, scale=1.0):
                act.wait_ge(S["chunk_used"], NCH * (g + 1))
                fn(dst, ps[:, 2 * (g % 2), :] if len(dst.shape) == 2 else bank(2 * (g % 2), NH, P), ACT.Copy, scale=scale).then_inc(S["proj_a"], 1)

            act.wait_ge(S["cols_pe"], 1)
            fn(cols[:], ps[:, 0, 0:104], ACT.Copy).then_inc(S["cols_act"], 1)
            act.wait_ge(S["cols_act"], 1)
            act.wait_ge(S["x_in"], 16)
            squares(h)
            rsqrt(NT)
            act.wait_ge(S["mem_in"], 16)
            act.wait_ge(S["diag_dve"], 1)
            squares(mem)
            turned(0, xT, 0)
            rsqrt(NT)
            turned(1, memT, 3)
            for g, (name, fm, _, scale) in enumerate(W_IN):
                if name == "mv":
                    dst = buf[name][:, 0, :, 0:P]
                elif fm:
                    dst = flat(buf[name][:, 0:2, :])
                else:
                    dst = buf[name][:, 0, :]
                dense_out(g, dst, scale)
                if g == 2:
                    act.wait_ge(S["conv_dve"], 1)
                    fn(flat(buf["q"]), flat(buf["q"]), ACT.Silu).then_inc(S["silu_act"], 1)
                    act.wait_ge(S["conv_dve"], 2)
                    fn(flat(buf["k"]), flat(buf["k"]), ACT.Silu).then_inc(S["silu_act"], 1)
                if g in (3, 4, 8):
                    b_ = buf[name]
                    act.wait_ge(S["proj_a"], g + 1)
                    act.wait_ge(S["proj_b"], g + 1)
                    fn(flat(b_), flat(b_), ACT.Sigmoid if g == 3 else ACT.Silu).then_inc(S["silu_act"], 1)
                if g == 5:
                    act.wait_ge(S["gate_dve"], 2)
                    step(fn(gl, gt[:, 1::2, :], ACT.Abs))
                    step(fn(gl, gl, ACT.Exp, scale=-1.0))
                    fn(gl, gl, ACT.Ln, bias=1.0).then_inc(S["gate_act"], 1)
                    act.wait_ge(S["gate_dve"], 3)
                    fn(gr[:, 2:4, :], gr[:, 2:4, :], ACT.Exp, scale=-1.0).then_inc(S["gate_act"], 1)
            act.wait_ge(S["gate_dve"], 4)
            for hd in range(NH):
                act.wait_ge(S["ml_pe_m"], hd + 1)
                for w in range(2):
                    act.wait_ge(S["ml_arg"], 2 * hd + 2)
                    if hd >= 1:
                        act.wait_ge(S["ml_sw"], 2 * hd - 1 + w)
                    nm = bank(6, 2, T)[:, w, :]
                    tiles = [(marg[w], 0, 0), (nm, 1, 0), (marg[w], 1, 1)] if w == 0 else [(marg[w], 0, 0), (nm, 0, 1), (marg[w], 1, 1)]
                    for n, (src, j, u) in enumerate(tiles):
                        last = fn(mw[w][:, n, :], src[:, j * P:(j + 1) * P], ACT.Exp, bias=mlc[:, u, w, hd:hd + 1])
                    last.then_inc(S["ml_w"], 1)
                if hd >= 1:
                    act.wait_ge(S["ml_y"], hd)
                for w in range(2):
                    act.wait_ge(S["ml_pv"], 2 * hd + w + 1)
                    fn(st[:, 44 + 2 * w:46 + 2 * w], bank(7 if w == 0 else 5, NT, P + 1)[:, :, P], ACT.Abs).then_inc(S["ml_den"], 1)
            rsqrt(NT)
            act.wait_ge(S["fn_pe"], 1)
            fn(fa[:, 0].rearrange("p g c n -> p (g c n)"), flat(ps[:, 4:6, :]), ACT.Copy).then_inc(S["fn_act"], 1)
            act.wait_ge(S["fn_pe"], 2)
            fn(y[:, 0, 2 * GW:3 * GW], ps[:, 4, :], ACT.Copy).then_inc(S["fn_act"], 1)
            rsqrt(NT)
            for w, name in enumerate(("hff", "hfb")):
                f = flat(buf[name])
                if w == 1:
                    act.wait_ge(S["hp_act"], 4)
                act.wait_ge(S["ml_y"], NH)
                fn(flat(htmp), f, ACT.Abs).then_inc(S["hp_act"], 1)
                act.wait_ge(S["hp_act"], 4 * w + 1)
                fn(flat(htmp), flat(htmp), ACT.Exp, scale=-1.0).then_inc(S["hp_act"], 1)
                act.wait_ge(S["hp_act"], 4 * w + 2)
                fn(flat(htmp), flat(htmp), ACT.Ln, bias=1.0).then_inc(S["hp_act"], 1)
                act.wait_ge(S["hp_dve"], w + 1)
                fn(f, flat(htmp), ACT.Exp).then_inc(S["hp_act"], 1)
            for s in range(2 * HG_LEVELS):
                act.wait_ge(S["h_sub"], s + 1)
                fn(flat(he[s % 2]), flat(he[s % 2]), ACT.Exp).then_inc(S["h_exp"], 1)
                if s % 4 == 3:
                    g = G_WK + s // 4
                    dense_out(g, flat(kT[:, 4 * (g - G_WK):4 * (g - G_WK) + 2, :]))
            act.wait_ge(S["h_o"], 1)
            fn(y[:, 0, GW:2 * GW], ps[:, 4, :], ACT.Copy).then_inc(S["h_oev"], 1)
            rsqrt(NT * NH)
            rsqrt(NT)
            for m in range(NA_H // 2 * NT):
                act.wait_ge(S["na_max"], m + 1)
                if m >= 1:
                    act.wait_ge(S["na_t"], m)
                    act.wait_ge(S["na_r"], m)
                for u in range(2):
                    fn(npr[:, u, :], ns[:, u, :], ACT.Exp, bias=st[:, 52 + u:53 + u], accum_out=st[:, 54 + u:55 + u]).then_inc(S["na_p"], 1)
                act.wait_ge(S["na_t"], m + 1)
                if m >= 1:
                    act.wait_ge(S["na_o"], m)
                fn(npt.rearrange("p u s t -> p (u s t)"), ps[:, 5, :], ACT.Copy).then_inc(S["na_tev"], 1)
                if m % 2 == 1:
                    g = G_WV + m // 2
                    dense_out(g, v[:, 0, GW * (m // 2):GW * (m // 2 + 1)])
            rsqrt(NT)
            turned(2, memT, 4)
            act.wait_ge(S["proj_a"], G_WO + 4)
            act.wait_ge(S["proj_b"], G_WO + 4)
            squares(h)
            rsqrt(NT)
            turned(3, xT, 1)
            for g in range(G_WQ, G_WQ + 4):
                n = 4 * (g - G_WQ)
                dense_out(g, flat(qT[:, n:n + 2, :]))
            for hd in range(XA_H):
                act.wait_ge(S["xs_max"], hd + 1)
                if hd >= 1:
                    act.wait_ge(S["xs_t"], hd)
                for j in range(NT):
                    fn(xp[:, j, :], bank(4, NT, T)[:, j, :], ACT.Exp, bias=st[:, 52 + j:53 + j], scale=XA_D ** -0.5,
                       accum_out=st[:, 54 + j:55 + j]).then_inc(S["xs_p"], 1)
                act.wait_ge(S["xs_t"], hd + 1)
                if hd >= 1:
                    act.wait_ge(S["xs_o"], hd)
                fn(flat(xpt), ps[:, 5, :], ACT.Copy).then_inc(S["xs_tev"], 1)
                act.wait_ge(S["xs_o"], hd + 1)
                fn(flat(oT[:, 4 * hd:4 * hd + 2, :]), ps[:, 6, :], ACT.Copy).then_inc(S["xs_oa"], 1)
            act.wait_ge(S["proj_a"], G_XO + 4)
            act.wait_ge(S["proj_b"], G_XO + 4)
            squares(h)
            rsqrt(NT)
            turned(4, xT, 2)
            act.wait_ge(S["r_dve"], 1)
            for j in range(NT):
                step(fn(gexp, logit[:, j, 0:NG], ACT.Exp, bias=negm[:, j:j + 1], accum_out=gsum[:, j:j + 1]))
            act.wait_ge(S["r_dve"], 2)
            fn(vdif, vdif, ACT.Exp).then_inc(S["r_act"], 1)
            for k in range(0, KT, 2):
                act.wait_ge(S["g_pe"], k + 1)
                fn(xsT[:, k, 0:SLOTS], ps[:, 4 + k % 4, :], ACT.Copy, scale=cols[:, 2 * KT + k:2 * KT + k + 1]).then_inc(S["g_act"], 1)
            act.wait_ge(S["sg_pe"], 1)
            fn(flat(selgT), flat(ps[:, 4:6, :]), ACT.Copy).then_inc(S["sg_act"], 1)
            act.wait_ge(S["sg_act"], 1)
            act.wait_ge(S["tab_dve"], 2)
            fn(sg[:, 0, 0:1], selgT[:, 0, 0:1], ACT.Copy).then_inc(S["e_ya"], 1)

            def expert(n, s):
                act.wait_ge(S["e_used"], n * ECH + 4)
                fn(flat(sg[:]), ps[:, 0, 0:FF // P * EB], ACT.Silu).then_inc(S["e_sg"], 1)
                act.wait_ge(S["e_used"], n * ECH + 9)
                act.wait_ge(S["e_ya"], n + 1)
                fn(ysT[:, 0:4, bass.ds(s, EB)], bank(2, 4, EB), ACT.Copy)
                act.wait_ge(S["e_used"], n * ECH + 11)
                fn(ysT[:, 8:12, bass.ds(s, EB)], bank(4, 4, EB), ACT.Copy).then_inc(S["e_ya"], 1)

            act.wait_ge(S["e_ya"], 1)
            with act.Fori(0, NE) as e:
                s = act.value_load(table[0:1, bass.ds(e, 1)], min_val=0, max_val=SLOTS)
                expert(e, s)
            nov = act.value_load(table[0:1, 96:97], min_val=0, max_val=OVB)
            with act.Fori(0, OVB) as b:
                with act.If(b < nov):
                    s = act.value_load(table[0:1, bass.ds(b + 64, 1)], min_val=0, max_val=SLOTS)
                    expert(b + NE, s)
            act.wait_ge(S["c_tp"], 1)
            fn(sg[:, 0, 0:1], selgT[:, 0, 0:1], ACT.Copy).then_inc(S["c_act"], 1)
            n = 0
            for s in range(SLOTS // P):
                for kk in range(4):
                    if n % 2 == 0:
                        act.wait_ge(S["c_tp"], n + 2)
                        fn(ys[:, s, kk * 512:(kk + 1) * 512], ps[:, 4 + n % 4, :], ACT.Copy).then_inc(S["c_act"], 1)
                    n += 1
            act.wait_ge(S["c_add"], 8)
            squares(h)
            rsqrt(NT)

        @block.vector
        def _(dve):
            V = nc.vector
            steps, calls, norms = [0], [0], [0]

            def step(ins_):
                steps[0] += 1
                ins_.then_inc(S["dve_step"], 1)
                dve.wait_ge(S["dve_step"], steps[0])

            def rsqrt(w, inv):
                calls[0] += 1
                ss, var, r, t_ = st[:, 0:w], st[:, 8:8 + w], st[:, 24:24 + w], st[:, 32:32 + w]
                V.tensor_scalar(var, ss, inv, EPS, ALU.mult, ALU.add).then_inc(S["var_dve"], 1)
                dve.wait_ge(S["rs_act"], calls[0])
                step(V.tensor_tensor(t_, r, r, ALU.mult))
                step(V.tensor_tensor(t_, t_, var, ALU.mult))
                step(V.tensor_scalar(t_, t_, -0.5, 1.5, ALU.mult, ALU.add))
                step(V.tensor_tensor(r, r, t_, ALU.mult))

            def row_scale():
                norms[0] += 1
                dve.wait_ge(S["sq_act"], norms[0])
                rsqrt(NT, 1.0 / D)
                for j in range(NT):
                    last = V.tensor_scalar(diag[:, j, :], ident[:], st[:, 24 + j:25 + j], None, ALU.mult)
                last.then_inc(S["diag_dve"], 1)

            def turned(n, dst, gain):
                for kk in range(1, KT // 2, 2):
                    dve.wait_ge(S["tp_pe"], n * (KT // 2) + kk + 1)
                    for u in range(2):
                        k = 2 * kk + u
                        last = V.tensor_scalar(dst[:, k, :], ps[:, 4 + kk % 4, u * T:(u + 1) * T],
                                               cols[:, gain * KT + k:gain * KT + k + 1], None, ALU.mult)
                    last.then_inc(S["tp_dve"], 1)

            def dense_out(g, dst, scale=1.0):
                dve.wait_ge(S["chunk_used"], NCH * (g + 1))
                src = ps[:, 2 * (g % 2) + 1, :] if len(dst.shape) == 2 else bank(2 * (g % 2) + 1, NH, P)
                (V.tensor_copy(dst, src) if scale == 1.0 else V.tensor_scalar(dst, src, scale, None, ALU.mult)).then_inc(S["proj_b"], 1)

            def dense_add(g, n):
                dve.wait_ge(S["chunk_used"], NCH * (g + 1))
                for j in range(NT):
                    hv = h[:, j, GW * n:GW * (n + 1)]
                    V.tensor_tensor(hv, ps[:, 2 * (g % 2) + j, :], hv, ALU.add).then_inc(S["proj_a" if j == 0 else "proj_b"], 1)

            def group_norm(m):
                yv = y[:, :, GW * m:GW * (m + 1)]
                gtmp = arena(128, NT, GW)
                step(V.tensor_tensor(gtmp, yv, yv, ALU.mult))
                step(V.tensor_reduce(st[:, 0:NT], gtmp, AX.X, ALU.add))
                rsqrt(NT, 1.0 / GW)
                for j in range(NT):
                    last = V.tensor_scalar(yv[:, j, :], yv[:, j, :], st[:, 24 + j:25 + j], None, ALU.mult)
                last.then_inc(S["y_done"], 1)

            dve.wait_ge(S["eye_in"], 16)
            row_scale()
            dve.wait_ge(S["cols_act"], 1)
            turned(0, xT, 0)
            dve.wait_ge(S["tp_pe"], 8)
            row_scale()
            turned(1, memT, 3)
            for g, (name, fm, _, scale) in enumerate(W_IN):
                if name == "mv":
                    dst = buf[name][:, 1, :, 0:P]
                elif fm:
                    dst = flat(buf[name][:, 2:4, :])
                else:
                    dst = buf[name][:, 1, :]
                dense_out(g, dst, scale)
                if g == 0:
                    dve.wait_ge(S["cmask_in"], 16)
                    step(V.tensor_copy(hmask.rearrange("p d l t -> p (d l t)"), hmask_f))
                if g == 1:
                    dve.wait_ge(S["proj_a"], 2)
                    dve.wait_ge(S["proj_b"], 2)
                    for n, (raw, dst) in enumerate((("mq", "q"), ("mk", "k"))):
                        tap = lambda t_, c: cols[:, 80 + 8 * t_ + 4 * n + c:81 + 8 * t_ + 4 * n + c]
                        for c in range(NH):
                            last = V.tensor_scalar(buf[dst][:, c, :], buf[raw][:, c, :], tap(1, c), None, ALU.mult)
                        step(last)
                        for c in range(NH):
                            o_, i_ = buf[dst][:, c, 1:T], buf[raw][:, c, 0:T - 1]
                            last = V.scalar_tensor_tensor(o_, i_, tap(0, c), o_, ALU.mult, ALU.add)
                        step(last)
                        for c in range(NH):
                            o_, i_ = buf[dst][:, c, 0:T - 1], buf[raw][:, c, 1:T]
                            last = V.scalar_tensor_tensor(o_, i_, tap(2, c), o_, ALU.mult, ALU.add)
                        last.then_inc(S["conv_dve"], 1)
                if g == 3:
                    dve.wait_ge(S["gate_pe"], 1)
                    V.tensor_copy(gtok, bank(4, NT, 16)).then_inc(S["gate_dve"], 1)
                    dve.wait_ge(S["gbias_in"], 16)
                    dve.wait_ge(S["gate_pe"], 2)
                    for kind in range(4):
                        last = V.tensor_scalar(gt[:, kind, :], ps[0:NH, 5 + kind // 2, (kind % 2) * T:(kind % 2 + 1) * T],
                                               gbias[:, kind:kind + 1], None, ALU.add)
                    last.then_inc(S["gate_dve"], 1)
                if g == 5:
                    dve.wait_ge(S["gate_dve"], 2)
                    dve.wait_ge(S["gate_act"], 1)
                    dve.wait_ge(S["pool_step"], 1)
                    step(V.scalar_tensor_tensor(lf, gt[:, 1::2, :], 0.0, gl, ALU.min, ALU.subtract))
                    V.tensor_tensor_scan(gb[:, 0, :], gone[0:NH, :], lf[:, 0, :], 0.0, ALU.mult, ALU.add)
                    step(V.tensor_tensor_scan(gb[:, 1, ::-1], gone[0:NH, :], lf[:, 1, ::-1], 0.0, ALU.mult, ALU.add))
                    step(V.tensor_tensor(gr[:, 0:2, :], gt[:, 0::2, :], gb, ALU.subtract))
                    V.tensor_tensor_scan(gm[:, 0, :], gr[:, 0, :], gr[:, 0, :], 0.0, ALU.max, ALU.max)
                    step(V.tensor_tensor_scan(gm[:, 1, ::-1], gr[:, 1, ::-1], gr[:, 1, ::-1], 0.0, ALU.max, ALU.max))
                    step(V.tensor_tensor(gr[:, 2:4, :], gb, gm, ALU.add))
                    V.tensor_scalar(gm, gm, -1.0, None, ALU.mult).then_inc(S["gate_dve"], 1)
            dve.wait_ge(S["gate_pe"], 3)
            V.tensor_copy(mlc.rearrange("p j k h -> p (j k h)"), ps[:, 4, 0:NT * 4 * NH]).then_inc(S["gate_dve"], 1)
            dve.wait_ge(S["gate_dve"], 4)
            dve.wait_ge(S["cmix_in"], 16)
            den, rden = st[:, 44:48].rearrange("p (w j) -> p w j", w=2), st[:, 48:52].rearrange("p (w j) -> p w j", w=2)
            for hd in range(NH):
                dve.wait_ge(S["ml_pe_m"], hd + 1)
                for w in range(2):
                    if hd >= 1:
                        dve.wait_ge(S["ml_w"], 2 * hd - 1 + w)
                    V.tensor_tensor(marg[w].rearrange("p (j t) -> p j t", j=NT), bank(6, 2, NT, P)[:, w], bc_mid(tri[w], NT),
                                    ALU.add).then_inc(S["ml_arg"], 1)
                dve.wait_ge(S["ml_pe_s"], hd + 1)
                for w in range(2):
                    dve.wait_ge(S["ml_w"], 2 * hd + w + 1)
                    if hd >= 1:
                        dve.wait_ge(S["ml_pv"], 2 * hd - 1 + w)
                    sc = ps[:, 4, :]
                    cuts = [(0, 2, 0), (2, 3, 3)] if w == 0 else [(0, 1, 0), (1, 3, 2)]
                    for a, z, at in cuts:
                        last = V.scalar_tensor_tensor(flat(msw[w][:, a:z, :]), sc[:, at * P:(at + z - a) * P], P ** -0.5,
                                                      flat(mw[w][:, a:z, :]), ALU.mult, ALU.mult)
                    last.then_inc(S["ml_sw"], 1)
                dve.wait_ge(S["ml_den"], 2 * hd + 2)
                step(V.tensor_tensor(den, den, mlc[:, :, 2:4, hd].rearrange("p j w -> p w j"), ALU.max))
                step(V.reciprocal(rden, den))
                for j in range(NT):
                    step(V.tensor_scalar(mt_, bank(7, NT, P + 1)[:, j, 0:P], rden[:, 0, j:j + 1], None, ALU.mult))
                    last = V.scalar_tensor_tensor(y[:, j, hd * P:(hd + 1) * P], bank(5, NT, P + 1)[:, j, 0:P], rden[:, 1, j:j + 1],
                                                  mt_, ALU.mult, ALU.add)
                    if j == 0:
                        step(last)
                last.then_inc(S["ml_y"], 1)
            dve.wait_ge(S["ml_y"], NH)
            dve.wait_ge(S["silu_act"], 3)
            step(V.tensor_tensor(y[:, :, 0:GW], y[:, :, 0:GW], buf["mo"], ALU.mult))
            group_norm(0)
            dve.wait_ge(S["fn_pe"], 1)
            V.tensor_copy(fa[:, 1].rearrange("p g c n -> p (g c n)"), flat(ps[:, 6:8, :])).then_inc(S["fn_dve"], 1)
            dve.wait_ge(S["fn_pe"], 2)
            V.tensor_copy(y[:, 1, 2 * GW:3 * GW], ps[:, 5, :]).then_inc(S["fn_dve"], 1)
            dve.wait_ge(S["fn_act"], 2)
            dve.wait_ge(S["fn_dve"], 2)
            dve.wait_ge(S["y_done"], 1)
            group_norm(2)
            dve.wait_ge(S["proj_a"], G_IN)
            dve.wait_ge(S["proj_b"], G_IN)
            step(V.memset(hone, 1.0))
            for w, name in enumerate(("hff", "hfb")):
                f = flat(buf[name])
                dve.wait_ge(S["hp_act"], 4 * w + 3)
                step(V.scalar_tensor_tensor(flat(he[w]), f, 0.0, flat(htmp), ALU.min, ALU.subtract))
                V.tensor_tensor(flat(htmp), flat(he[w]), f, ALU.subtract).then_inc(S["hp_dve"], 1)
                for c in range(NH):
                    o_, i_ = hb[w][:, c, :], he[w][:, c, :]
                    if w == 1:
                        o_, i_ = o_[:, ::-1], i_[:, ::-1]
                    last = V.tensor_tensor_scan(o_, hone, i_, 0.0, ALU.mult, ALU.add)
                step(last)
            dve.wait_ge(S["hp_act"], 8)
            V.tensor_tensor(flat(hqk[1]), flat(buf["hff"]), flat(buf["hfb"]), ALU.add).then_inc(S["hp_dve"], 1)

            def halves(x, half):
                vv = flat(x).rearrange("p (b u t) -> p b u t", u=2, t=half)
                return vv[:, :, 0, :], vv[:, :, 1, :]

            def decay(s):
                w, half = s // HG_LEVELS, 1 << (s % HG_LEVELS)
                if s >= 2:
                    dve.wait_ge(S["h_mulk"], s - 1)
                    dve.wait_ge(S["h_mulq"], s - 1)
                (e0_, e1_), (b0_, b1_) = halves(he[s % 2], half), halves(hb[w], half)
                mid = (b0_[:, :, half - 1:half] if w == 0 else b1_[:, :, 0:1]).to_broadcast(list(b0_.shape))
                if w == 0:
                    V.tensor_tensor(e0_, mid, b0_, ALU.subtract)
                    V.tensor_tensor(e1_, b1_, mid, ALU.subtract).then_inc(S["h_sub"], 1)
                else:
                    V.tensor_tensor(e0_, b0_, mid, ALU.subtract)
                    V.tensor_tensor(e1_, mid, b1_, ALU.subtract).then_inc(S["h_sub"], 1)

            def queries(s):
                w, half = s // HG_LEVELS, 1 << (s % HG_LEVELS)
                dve.wait_ge(S["h_exp"], s + 1)
                if s >= 1:
                    dve.wait_ge(S["h_pe"], s)
                u = 1 if w == 0 else 0
                V.tensor_tensor(halves(hqk[s % 2], half)[u], halves(he[s % 2], half)[u], halves(buf["hq"], half)[u],
                                ALU.mult).then_inc(S["h_mulq"], 1)

            def scores(s):
                w, lev = s // HG_LEVELS, s % HG_LEVELS
                dve.wait_ge(S["h_pe"], s + 2)
                dve.wait_ge(S["h_cp"], s + 1)
                b0 = 6 - 2 * (s % 2)
                if lev == HG_LEVELS - 1:
                    o_ = decay_to[:, w, :, P:2 * P] if w == 0 else decay_to[:, w, :, 0:P]
                    V.tensor_copy(o_, bank(b0, NH, P)).then_inc(S["h_cp"], 1)
                else:
                    for u in range(NT):
                        last = V.copy_predicated(decay_to[:, u, :, u * P:(u + 1) * P], bc_mid(hmask[:, w, lev, :], NH), bank(b0 + u, NH, P))
                    last.then_inc(S["h_cp"], 1)

            dve.wait_ge(S["silu_act"], 4)
            decay(0)
            dve.wait_ge(S["h_pe"], 1)
            for u in range(NT):
                last = V.tensor_copy(decay_to[:, u, :, u * P:(u + 1) * P], bank(4 + u, NH, P))
            last.then_inc(S["h_cp"], 1)
            for s in range(2 * HG_LEVELS):
                if s + 1 < 2 * HG_LEVELS:
                    decay(s + 1)
                queries(s)
                if s >= 1:
                    scores(s - 1)
                if s >= 4 and s % 4 == 0:
                    g = G_WK + s // 4 - 1
                    dense_out(g, flat(kT[:, 4 * (g - G_WK) + 2:4 * (g - G_WK) + 4, :]))
            scores(2 * HG_LEVELS - 1)
            dense_out(G_WK + 3, flat(kT[:, 14:16, :]))
            dve.wait_ge(S["h_o"], 1)
            V.tensor_copy(y[:, 1, GW:2 * GW], ps[:, 5, :]).then_inc(S["h_oev"], 1)
            dve.wait_ge(S["h_oev"], 2)
            dve.wait_ge(S["y_done"], 2)
            yh = y[:, :, GW:2 * GW]
            sq = arena(128, NT, GW)
            step(V.tensor_tensor(sq, yh, yh, ALU.mult))
            step(V.tensor_reduce(st[:, 0:NT * NH], sq.rearrange("p j (h d) -> p (j h) d", h=NH), AX.X, ALU.add))
            rsqrt(NT * NH, 1.0 / P)
            for j in range(NT):
                yj = yh[:, j, :].rearrange("p (h d) -> p h d", h=NH)
                last = V.tensor_tensor(yj, yj, bc_last(st[:, 24 + NH * j:24 + NH * (j + 1)], P), ALU.mult)
            step(last)
            dve.wait_ge(S["silu_act"], 5)
            step(V.tensor_tensor(yh, yh, buf["hg"], ALU.mult))
            group_norm(1)
            for m in range(NA_H // 2 * NT):
                i, j = m // NT, m % NT
                dve.wait_ge(S["na_s"], m + 1)
                if m >= 1:
                    dve.wait_ge(S["na_p"], 2 * m)
                grid = lambda x: x.rearrange("p u (a w) -> p u a w", w=GRID_W)
                V.tensor_tensor(grid(ns), grid(ps[:, 4::3, 0:T]), win.unsqueeze(1).unsqueeze(1).to_broadcast([P, 2, 4, GRID_W]),
                                ALU.add).then_inc(S["na_m"], 1)
                dve.wait_ge(S["na_m"], m + 1)
                step(V.tensor_reduce(st[:, 52:54], ns, AX.X, ALU.max))
                V.tensor_scalar(st[:, 52:54], st[:, 52:54], -1.0, None, ALU.mult).then_inc(S["na_max"], 1)
                dve.wait_ge(S["na_p"], 2 * m + 2)
                V.reciprocal(st[:, 44:46], st[:, 54:56]).then_inc(S["na_r"], 1)
                dve.wait_ge(S["na_r"], m + 1)
                dve.wait_ge(S["na_o"], m + 1)
                for u in range(2):
                    c0 = 3 * GW + (2 * i + u) * NA_D
                    V.tensor_scalar(y[:, j, c0:c0 + NA_D], bank(6, 2, NA_D)[:, u, :], st[:, 44 + u:45 + u], None, ALU.mult).then_inc(S["na_y"], 1)
                if m % 2 == 1:
                    dense_out(G_WV + m // 2, v[:, 1, GW * (m // 2):GW * (m // 2 + 1)])
            dve.wait_ge(S["na_y"], 16)
            dve.wait_ge(S["y_done"], 3)
            group_norm(3)
            turned(2, memT, 4)
            for n in range(4):
                dense_add(G_WO + n, n)
            row_scale()
            turned(3, xT, 1)
            for g in range(G_WQ, G_WQ + 4):
                n = 4 * (g - G_WQ) + 2
                dense_out(g, flat(qT[:, n:n + 2, :]))
            for hd in range(XA_H):
                dve.wait_ge(S["xs_pe"], hd + 1)
                if hd >= 1:
                    dve.wait_ge(S["xs_p"], 2 * hd)
                step(V.tensor_reduce(st[:, 52:54], bank(4, NT, T), AX.X, ALU.max))
                V.tensor_scalar(st[:, 52:54], st[:, 52:54], -(XA_D ** -0.5), None, ALU.mult).then_inc(S["xs_max"], 1)
                dve.wait_ge(S["xs_p"], 2 * hd + 2)
                step(V.reciprocal(st[:, 44:46], st[:, 54:56]))
                if hd >= 1:
                    dve.wait_ge(S["xs_t"], hd)
                for j in range(NT):
                    last = V.tensor_scalar(diag[:, j, :], ident[:], st[:, 44 + j:45 + j], None, ALU.mult)
                last.then_inc(S["xs_diag"], 1)
                dve.wait_ge(S["xs_o"], hd + 1)
                V.tensor_copy(flat(oT[:, 4 * hd + 2:4 * hd + 4, :]), ps[:, 7, :]).then_inc(S["xs_od"], 1)
            for n in range(4):
                dense_add(G_XO + n, n)
            row_scale()
            V.tensor_copy(st[:, 40:42], st[:, 24:26])
            turned(4, xT, 2)
            dve.wait_ge(S["r_pe"], 1)
            dve.wait_ge(S["route_in"], 16)
            V.memset(lgrp, LOWEST)
            step(V.tensor_copy(logit, bank(4, NT, 36)))
            step(V.tensor_copy(lgrp[:, :, 0:NG], logit[:, :, 0:NG]))
            for j in range(NT):
                last = V.max(gmax8[:, j, :], lgrp[:, j, :])
            step(last)
            for j in range(NT):
                V.max_index(gidx8[:, j, :], gmax8[:, j, :], lgrp[:, j, :])
            V.tensor_scalar(negm, gmax8[:, :, 0], -1.0, None, ALU.mult).then_inc(S["r_dve"], 1)
            dve.wait_ge(S["r_dve"], 1)
            step(V.tensor_copy(egrp, gidx8[:, :, 0]))
            for j in range(NT):
                last = V.tensor_scalar(goh4[:, j, :], iota[:, 0:NG], egrp[:, j:j + 1], None, ALU.is_equal)
            step(last)
            for g in range(NG):
                for j in range(NT):
                    src = logit[:, j, NG + PG * g:NG + PG * (g + 1)]
                    if g == 0:
                        last = V.tensor_scalar(fine[:, j, :], src, goh4[:, j, g:g + 1], None, ALU.mult)
                    else:
                        last = V.scalar_tensor_tensor(fine[:, j, :], src, goh4[:, j, g:g + 1], fine[:, j, :], ALU.mult, ALU.add)
                step(last)
            for j in range(NT):
                last = V.max(fmax8[:, j, :], fine[:, j, :])
            step(last)
            for j in range(NT):
                last = V.max_index(fidx8[:, j, :], fmax8[:, j, :], fine[:, j, :])
            step(last)
            V.tensor_copy(e0, fidx8[:, :, 0])
            step(V.tensor_copy(e1, fidx8[:, :, 1]))
            V.tensor_tensor(vdif, fmax8[:, :, 1], fmax8[:, :, 0], ALU.subtract).then_inc(S["r_dve"], 1)
            V.scalar_tensor_tensor(e0, egrp, float(PG), e0, ALU.mult, ALU.add)
            step(V.scalar_tensor_tensor(e1, egrp, float(PG), e1, ALU.mult, ALU.add))
            for j in range(NT):
                V.tensor_scalar(hit0[:, j, :], iota[:, 0:NE], e0[:, j:j + 1], None, ALU.is_equal)
                last = V.tensor_scalar(hit1[:, j, :], iota[:, 0:NE], e1[:, j:j + 1], None, ALU.is_equal)
            step(last)
            step(V.tensor_tensor(hit, hit0, hit1, ALU.add))
            V.tensor_tensor(hits, hit[:, 0, :], hit[:, 1, :], ALU.add).then_inc(S["r_dve"], 1)
            dve.wait_ge(S["r_act"], 1)
            V.reciprocal(ggate, gsum)
            step(V.tensor_scalar(w0, vdif, 1.0, None, ALU.add))
            step(V.reciprocal(w0, w0))
            step(V.tensor_tensor(w0, w0, ggate, ALU.mult))
            step(V.tensor_tensor(w1, vdif, w0, ALU.mult))
            dve.wait_ge(S["r_pe"], 2)
            step(V.tensor_copy(flat(rank), ps[:, 5, 0:3 * NE]))
            count = rank[:, 2, :]
            one32 = ones[:, 0:NE]
            step(V.tensor_scalar(n_first, count, float(EB), None, ALU.min))
            V.tensor_tensor(n_over, count, n_first, ALU.subtract)
            step(V.tensor_tensor_scan(st_first, one32, n_first, 0.0, ALU.mult, ALU.add))
            step(V.tensor_tensor_scan(st_over, one32, n_over, st_first[:, NE - 1:NE], ALU.mult, ALU.add))
            V.tensor_tensor(st_first, st_first, n_first, ALU.subtract)
            step(V.tensor_tensor(st_over, st_over, n_over, ALU.subtract))
            step(V.scalar_tensor_tensor(st_gap, st_over, float(-EB), st_first, ALU.add, ALU.subtract))
            step(V.tensor_scalar(blocks, n_over, 0.0, None, ALU.is_gt))
            for k in range(1, OVK):
                step(V.tensor_scalar(rtmp, n_over, float(k * EB), None, ALU.is_gt))
                step(V.tensor_tensor(blocks, blocks, rtmp, ALU.add))
            step(V.tensor_tensor_scan(blk_in, one32, blocks, 0.0, ALU.mult, ALU.add))
            step(V.tensor_scalar(rtmp, blk_in, iotap, None, ALU.is_le))
            step(V.tensor_reduce(eid, rtmp, AX.X, ALU.add))
            step(V.tensor_scalar(eid, eid, float(NE - 1), None, ALU.min))
            step(V.tensor_tensor(blocks, blk_in, blocks, ALU.subtract))
            step(V.scalar_tensor_tensor(blocks, blocks, float(-EB), st_over, ALU.mult, ALU.add))
            step(V.tensor_scalar(rtmp, iota[:, 0:NE], eid, None, ALU.is_equal))
            step(V.tensor_tensor(rtmp, rtmp, blocks, ALU.mult))
            step(V.tensor_reduce(ost, rtmp, AX.X, ALU.add))
            step(V.scalar_tensor_tensor(ost, iotap, float(EB), ost, ALU.mult, ALU.add))
            V.tensor_scalar(ost, ost, float(SLOTS), None, ALU.min).then_inc(S["r_dve"], 1)
            for j in range(NT):
                rj = rank[:, j, :]
                step(V.scalar_tensor_tensor(rtmp, rj, float(EB), st_gap, ALU.is_ge, ALU.mult))
                step(V.tensor_tensor(rtmp, rtmp, rj, ALU.add))
                step(V.tensor_tensor(rj, rtmp, st_first, ALU.add))
            slot = rank[:, 0:NT, :]
            step(V.tensor_tensor(hit0, hit0, slot, ALU.mult))
            step(V.tensor_reduce(slot0, hit0, AX.X, ALU.add))
            step(V.tensor_tensor(hit1, hit1, slot, ALU.mult))
            step(V.tensor_reduce(slot1, hit1, AX.X, ALU.add))
            for j in range(NT):
                for sel, a0, a1 in ((sel_r, st[:, 40 + j:41 + j], st[:, 40 + j:41 + j]), (sel_g, w0[:, j:j + 1], w1[:, j:j + 1])):
                    V.tensor_scalar(sel[:, j, :], iota, slot0[:, j:j + 1], a0, ALU.is_equal, ALU.mult)
                    step(V.tensor_scalar(sel_t, iota, slot1[:, j:j + 1], a1, ALU.is_equal, ALU.mult))
                    last = V.tensor_tensor(sel[:, j, :], sel[:, j, :], sel_t, ALU.add)
                    if not (j == 1 and sel is sel_g):
                        step(last)
            last.then_inc(S["tab_dve"], 1)
            dve.wait_ge(S["r_pe"], 3)
            V.tensor_copy(table[0:1, 0:NE], st_first[0:1, :])
            V.tensor_copy(table[0:1, 32:64], ps[0:1, 6, 0:32])
            V.tensor_copy(table[0:1, 64:96], ps[0:1, 6, P:P + 32])
            V.tensor_copy(table[0:1, 96:97], blk_in[0:1, NE - 1:NE]).then_inc(S["tab_dve"], 1)
            for k in range(1, KT, 2):
                dve.wait_ge(S["g_pe"], k + 1)
                V.tensor_scalar(xsT[:, k, 0:SLOTS], ps[:, 4 + k % 4, :], cols[:, 2 * KT + k:2 * KT + k + 1], None, ALU.mult).then_inc(S["g_dve"], 1)
            V.memset(xsT[:, :, SLOTS:], 0.0).then_inc(S["g_dve"], 1)
            dve.wait_ge(S["sg_act"], 1)
            V.tensor_copy(hT[:, 0, 0:1], ident[:, 0:1]).then_inc(S["e_yd"], 1)
            dve.wait_ge(S["tab_dve"], 2)

            def expert(n, s):
                dve.wait_ge(S["e_used"], n * ECH + 8)
                dve.wait_ge(S["e_sg"], n + 1)
                V.tensor_tensor(flat(hT[:]), ps[:, 1, 0:FF // P * EB], flat(sg[:]), ALU.mult).then_inc(S["e_h"], 1)
                dve.wait_ge(S["e_used"], n * ECH + 10)
                dve.wait_ge(S["e_yd"], n + 1)
                V.tensor_copy(ysT[:, 4:8, bass.ds(s, EB)], bank(3, 4, EB))
                dve.wait_ge(S["e_used"], n * ECH + 12)
                V.tensor_copy(ysT[:, 12:16, bass.ds(s, EB)], bank(5, 4, EB)).then_inc(S["e_yd"], 1)

            dve.wait_ge(S["e_yd"], 1)
            with dve.Fori(0, NE) as e:
                s = dve.value_load(table[0:1, bass.ds(e, 1)], min_val=0, max_val=SLOTS)
                expert(e, s)
            nov = dve.value_load(table[0:1, 96:97], min_val=0, max_val=OVB)
            with dve.Fori(0, OVB) as b:
                with dve.If(b < nov):
                    s = dve.value_load(table[0:1, bass.ds(b + 64, 1)], min_val=0, max_val=SLOTS)
                    expert(b + NE, s)
            dve.wait_ge(S["c_tp"], 1)
            V.tensor_copy(hT[:, 0, 0:1], ident[:, 0:1]).then_inc(S["c_dve"], 1)
            n = 0
            for s in range(SLOTS // P):
                for kk in range(4):
                    if n % 2 == 1:
                        dve.wait_ge(S["c_tp"], n + 2)
                        V.tensor_copy(ys[:, s, kk * 512:(kk + 1) * 512], ps[:, 4 + n % 4, :]).then_inc(S["c_dve"], 1)
                    n += 1
            for j in range(NT):
                for g in range(4):
                    m = 4 * j + g
                    hv = h[:, j, g * 512:(g + 1) * 512]
                    dve.wait_ge(S["c_pe"], m + 1)
                    V.tensor_tensor(hv, ps[:, m % 4, :], hv, ALU.add).then_inc(S["c_add"], 1)
            norms[0] += 1
            dve.wait_ge(S["sq_act"], norms[0])
            rsqrt(NT, 1.0 / D)
            dve.wait_ge(S["fgain_in"], 16)
            for j in range(NT):
                V.scalar_tensor_tensor(res[:, j, :], h[:, j, :], st[:, 24 + j:25 + j], fgain, ALU.mult, ALU.mult).then_inc(S["fin_dve"], 1)


INS = ["x", "mem", "norm_mix", "norm_cross", "norm_ffn", "norm_final", "norm_mem", "w_in", "mlstm_conv", "mlstm_gate_bias",
       "na_rpb", "group_gain", "w_out", "xa_wq", "xa_wk", "xa_wv", "xa_wo", "moe_router_group", "moe_router_expert",
       "moe_w1", "moe_w3", "moe_w2"]


def kernel(**inputs):
    import numpy as _np
    import concourse.bacc as _bacc
    from concourse import mybir as _mybir
    from concourse.bass_utils import run_bass_kernel_spmd as _run

    nc = _bacc.Bacc("TRN2", target_bir_lowering=False, num_devices=1)
    arrays, aps = {}, {}
    given = {n: inputs[n] for n in INS}
    given.update(constants())
    for name, a in given.items():
        a = _np.ascontiguousarray(a)
        arrays[f"in_{name}_dram"] = a
        aps[name] = nc.dram_tensor(f"in_{name}_dram", a.shape, _mybir.dt.from_np(a.dtype), kind="ExternalInput").ap()
    out = nc.dram_tensor("out_0_dram", (1, T, D), _mybir.dt.float32, kind="ExternalOutput").ap()
    program(nc, aps, out)
    r = _run(nc, [arrays], core_ids=[0])
    return r.results[0]["out_0_dram"]
```

```python
from contextlib import ExitStack

import numpy as np

import concourse.bass as bass
from concourse import mybir

ALU = mybir.AluOpType
ACT = mybir.ActivationFunctionType
AX = mybir.AxisListType
F32 = mybir.dt.float32
I32 = mybir.dt.int32
U32 = mybir.dt.uint32
U8 = mybir.dt.uint8
F32R = mybir.dt.float32r

P = 128
D = 2048
KT = D // P
T = 256
NT = T // P
GW = 512
NH = 4
CH = 4
NCH = KT // CH
RING_A = 4
FF = 512
NE = 32
NG = 4
PG = NE // NG
UCH = 8
DCH = 4
RING_E = 4
EB = 64
EW = 96
OVK = -(-(T - EB) // EB)
OVB = 2 * T // EB
SLOTS = 2 * T
EPS = 1e-6
GRID_W = 64
NA_H = 8
NA_D = 64
NA_KW = 16
RPB_R, RPB_C = 15, 31
XA_H = 4
XA_D = D // XA_H
NEG = -1.0e30
LOWEST = -3.0e38

W_IN = [
    ("mq", True, 0, 1.0), ("mk", True, 512, 1.0), ("mv", False, 1024, 1.0), ("mo", False, 1536, 1.0),
    ("hq", True, 2064, 1.0), ("hff", True, 2576, 1.0), ("hfb", True, 3088, 1.0), ("hi", False, 3600, 1.0),
    ("hg", False, 4112, 1.0), ("fu", True, 4624, 1.0), ("nq", True, 5136, NA_D ** -0.5), ("nk", True, 5648, 1.0),
    ("nv", False, 6160, 1.0),
]
G_COL = 2048
G_IN = len(W_IN)
G_WK, G_WV, G_WO, G_WQ, G_XO = G_IN, G_IN + 4, G_IN + 8, G_IN + 12, G_IN + 16

HG_LEVELS = 8


def constants():
    c = np.arange(P)
    ang = 2 * np.pi * np.outer(c, c) / P
    s = np.arange(T)
    angs = 2 * np.pi * np.outer(s, s) / T
    norm = 1.0 / np.sqrt(T * P)
    tok = lambda m: m.reshape(NT, P, T).transpose(1, 0, 2).reshape(P, NT * T)
    dft = np.concatenate([np.cos(ang), np.sin(ang), tok(np.cos(angs) * norm), tok(-np.sin(angs) * norm)], 1)
    flip = np.eye(P)[::-1]
    fwd = np.where(c[:, None] <= c[None, :], 0.0, NEG)
    bwd = np.where(c[:, None] >= c[None, :], 0.0, NEG)
    selh = np.zeros((P, NH, P))
    for h in range(NH):
        selh[h, h] = 1.0
    col = np.arange(GRID_W)
    start = np.clip(col - NA_KW // 2, 0, GRID_W - NA_KW)
    ok = (col[None] >= start[:, None]) & (col[None] < start[:, None] + NA_KW)
    win = np.tile(np.where(ok, 0.0, NEG), (NT, 1))
    mix = np.concatenate([flip, fwd, bwd, selh.reshape(P, -1), win], 1)
    masks = np.zeros((P, 2, HG_LEVELS - 1, P), np.float32)
    for lev in range(HG_LEVELS - 1):
        h = 1 << lev
        same = (c[:, None] // (2 * h)) == (c[None, :] // (2 * h))
        odd = (c // h) % 2
        masks[:, 0, lev] = same & (odd[:, None] == 0) & (odd[None, :] == 1)
        masks[:, 1, lev] = same & (odd[:, None] == 1) & (odd[None, :] == 0)
    before = (c[:, None] < c[None, :]) * 1.0
    route = np.concatenate([before, np.ones((P, P)), np.tile(np.arange(SLOTS), (P, 1)), c[:, None] * 1.0], 1)
    return {"c_dft": dft.astype(np.float32), "c_mix": mix.astype(np.float32),
            "c_eye": np.eye(P, dtype=np.float32),
            "c_masks": masks.reshape(P, -1), "c_route": route.astype(np.float32)}


class Arena:

    def __init__(self, tensor):
        self.t = tensor

    def __call__(self, kib, *shape, parts=P):
        a = int(round(kib * 256))
        n = int(np.prod(shape))
        v = self.t[0:parts, a:a + n]
        if len(shape) == 2:
            v = v.rearrange("p (a b) -> p a b", b=shape[1])
        if len(shape) == 3:
            v = v.rearrange("p (a b c) -> p a b c", b=shape[1], c=shape[2])
        if len(shape) == 4:
            v = v.rearrange("p (a b c d) -> p a b c d", b=shape[1], c=shape[2], d=shape[3])
        return v


def flat(v):
    if len(v.shape) == 3:
        return v.rearrange("p a b -> p (a b)")
    return v.rearrange("p a b c -> p (a b c)")


def bc_mid(v, n):
    return v.unsqueeze(1).to_broadcast([v.shape[0], n, v.shape[1]])


def bc_last(v, n):
    return v.unsqueeze(2).to_broadcast([v.shape[0], v.shape[1], n])


def program(nc, ins, out, dbg=None):
    dbg = dbg or {}
    with ExitStack() as ctx:
        def sb(name, shape, dt=F32):
            return ctx.enter_context(nc.sbuf_tensor(name, shape, dt))

        def sem(name):
            return ctx.enter_context(nc.semaphore(name))

        base = -(-nc.sbuf_base // 32) * 32
        arena = Arena(sb("arena", [P, 200 * 256]))

        def at_r(name, kib, shape):
            return nc.alloc_sbuf_tensor_at(name, shape, F32R, offset=base + int(kib * 1024))

        ident = sb("ident", [P, P])
        cols = sb("cols", [P, 104])
        table = sb("table", [1, 128], I32)
        diag = sb("diag", [P, NT, P])
        st = sb("stats", [P, 64])
        hmask = sb("hmask", [P, 2 * (HG_LEVELS - 1) * P], U8).rearrange("p (d l t) -> p d l t", d=2, t=P)
        ps = ctx.enter_context(nc.psum_tensor("ps", [P, 8, 512], F32))

        h = arena(0, NT, D)
        ring_a = [arena(16 + 8 * i, CH, 512) for i in range(RING_A)]
        xT = arena(48, KT, T)
        memT = arena(64, KT, T)
        mem = arena(80, NT, D)
        y = mem
        kT = arena(96, KT, T)
        v = arena(112, NT, D)
        buf = {}
        buf["q"], buf["k"] = arena(128, NH, T), arena(132, NH, T)
        buf["mv"] = arena(136, NT, NH, P + 1)
        o = 140.25
        for n in ("mo", "hq", "hff", "hfb", "hi", "hg", "fu", "nq", "nk", "nv"):
            a_form = n in ("mo", "hi", "hg", "nv")
            buf[n] = arena(o, NT, GW) if a_form else arena(o, NH, T)
            o += 4
        buf["mq"], buf["mk"] = arena(112, NH, T), arena(116, NH, T)
        decay_to = arena(180.25, NT, NH, T)
        hmask_f = arena(180.25, 2 * (HG_LEVELS - 1) * P)
        dft_c = arena(188.25, 2 * P)
        dft_t = arena(189.25, 2, NT, T)
        mixc = arena(193.25, 7 * P + GRID_W)
        flipm, tri = mixc[:, 0:P], [mixc[:, P:2 * P], mixc[:, 2 * P:3 * P]]
        selh = mixc[0:NH, 3 * P:7 * P].rearrange("p (h t) -> p h t", h=NH)
        win = mixc[:, 7 * P:]
        wg = arena(197, KT, 16)
        rows = arena(198, P)
        gt = arena(120, NH, T, parts=NH)
        gl = arena(124, 2, T, parts=NH)
        lf = arena(126, 2, T, parts=NH)
        gb = arena(96, 2, T, parts=NH)
        gr = arena(98, NH, T, parts=NH)
        gm = arena(102, 2, T, parts=NH)
        gone = arena(104, T)
        gtok = arena(105, NT, 16)
        gbias = st[0:NH, 56:60]
        mlc = arena(106, NT, 4, NH)
        mw = [arena(107, 3, P), arena(108.5, 3, P)]
        msw = [arena(110, 3, P), arena(120, 3, P)]
        marg = [arena(122, T), arena(123, T)]
        mt_ = arena(121.5, P)
        fa = arena(112, NT, NH, 2, P)
        hb = [arena(48, NH, T), arena(52, NH, T)]
        hqk = [arena(56, NH, T), arena(60, NH, T)]
        he = [arena(112, NH, T), arena(116, NH, T)]
        htmp = arena(120, NH, T)
        hone = arena(124, T)
        nbias = [arena(144.25, 2, T), arena(146.25, 2, T)]
        ns, npr, npt = arena(148.25, 2, T), arena(150.25, 2, T), arena(152.25, 2, NT, P)
        qT = arena(80, KT, T)
        oT = memT
        xp, xpt = arena(128, NT, T), arena(130, NT, T)
        xsT = arena(16, KT, SLOTS + EB)
        ysT = arena(52, KT, SLOTS + EB)
        xe_hi, xe_lo = at_r("xe_hi", 88, [P, KT, EB]), at_r("xe_lo", 92, [P, KT, EB])
        selgT = arena(96, SLOTS // P, T)
        hT = arena(100, FF // P, EW)
        sg = arena(102, FF, parts=EB)
        sel_r, sel_g, sel_t = arena(64, NT, SLOTS), arena(68, NT, SLOTS), arena(78, SLOTS)
        wr = arena(101, KT, 36)
        rt = arena(72, 1024)
        routec = arena(80, 2 * P + SLOTS + 1)
        before, ones, iota, iotap = (routec[:, 0:P], routec[:, P:2 * P], routec[:, 2 * P:2 * P + SLOTS],
                                     routec[:, 2 * P + SLOTS:])
        r_at = [0]

        def small(*shape):
            a = r_at[0]
            r_at[0] += int(np.prod(shape))
            assert r_at[0] <= 1024
            vv = rt[:, a:r_at[0]]
            return vv.rearrange("p (a b) -> p a b", b=shape[1]) if len(shape) == 2 else vv

        logit, lgrp, gmax8, fine, fmax8 = small(NT, 36), small(NT, 8), small(NT, 8), small(NT, 8), small(NT, 8)
        gidx8, fidx8 = small(NT, 8).bitcast(U32), small(NT, 8).bitcast(U32)
        hit0, hit1, hit, rank = small(NT, NE), small(NT, NE), small(NT, NE), small(3, NE)
        hits, n_first, n_over, st_first, st_over, st_gap, blocks, blk_in, rtmp = [small(NE) for _ in range(9)]
        ftmp = small(NT, 8)
        egrp, gsum, ggate, vdif, w0, w1, e0, e1, slot0, slot1, negm, goh = [small(NT) for _ in range(12)]
        goh4 = small(NT, 4)
        eid, ost, gexp = small(1), small(1), small(4)
        ring_up = [arena(136 + 8 * i, CH, 512) for i in range(RING_E)]
        up_lo = [at_r(f"up_lo{i}", 136 + 8 * i, [P, CH, 512]) for i in range(RING_E)]
        up_hi = [at_r(f"up_hi{i}", 104 + 8 * i, [P, CH, 512]) for i in range(RING_E)]
        ring_dn = [arena(168 + 8 * i, CH, 512) for i in range(RING_E)]
        ys = arena(16, SLOTS // P, D)
        fgain = arena(136, D)
        res = arena(144, NT, D)

        def bank(b, *shape):
            w = int(np.prod(shape))
            vv = ps[:, b, 0:w]
            if len(shape) == 2:
                return vv.rearrange("p (a b) -> p a b", b=shape[1])
            if len(shape) == 3:
                return vv.rearrange("p (a b c) -> p a b c", b=shape[1], c=shape[2])
            return vv

        S = {}
        for n in ["x_in", "mem_in", "eye_in", "rows_in", "cmix_in", "cdft_in", "cmask_in", "wg_in", "gbias_in",
                  "bias_in0", "bias_in1", "route_in", "wr_in", "fgain_in", "out_done",
                  "chunk_used", "proj_pe", "proj_a", "proj_b", "act_step", "dve_step", "pool_step",
                  "sq_act", "var_dve", "rs_act", "diag_dve", "tp_pe", "tp_act", "tp_dve", "cols_pe", "cols_act",
                  "conv_dve", "silu_act", "gate_pe", "gate_dve", "gate_act", "ml_pe_s", "ml_pe_m", "ml_arg",
                  "ml_w", "ml_sw", "ml_pv", "ml_den", "ml_y", "fn_pe", "fn_act", "fn_dve",
                  "hp_act", "hp_dve", "h_sub", "h_exp", "h_mulq", "h_mulk", "h_pe", "h_cp", "h_o", "h_oev",
                  "na_s", "na_m", "na_max", "na_p", "na_r", "na_t", "na_tev", "na_o", "na_y", "y_done", "y_act",
                  "xs_pe", "xs_max", "xs_p", "xs_diag", "xs_t", "xs_tev", "xs_o", "xs_oa", "xs_od",
                  "r_pe", "r_dve", "r_act", "g_pe", "g_act", "g_dve", "sg_pe", "sg_act", "tab_dve",
                  "xe_hi", "xe_lo", "up_hi", "up_lo", "up_used", "dn_used", "e_sg", "e_h", "e_turn", "e_hT", "e_ya", "e_yd",
                  "c_tp", "c_act", "c_dve", "c_pe", "c_add", "fin_dve"]:
            S[n] = sem(n)
        s_ring = [sem(f"ring_a{i}") for i in range(RING_A)]
        s_up = [sem(f"ring_up{i}") for i in range(RING_E)]
        s_dn = [sem(f"ring_dn{i}") for i in range(RING_E)]
        block = ctx.enter_context(nc.Block())

        w_src = {G_WK: "xa_wk", G_WV: "xa_wv", G_WO: "w_out", G_WQ: "xa_wq", G_XO: "xa_wo"}
        g1, g3, g2 = ins["moe_w1"][0], ins["moe_w3"][0], ins["moe_w2"][0]

        def dense_chunk(g, i):
            if g < G_IN:
                w, c0 = ins["w_in"][0], W_IN[g][2]
            else:
                base = G_IN + 4 * ((g - G_IN) // 4)
                w, c0 = ins[w_src[base]][0], 512 * (g - base)
            return w[i * CH * P:(i + 1) * CH * P, c0:c0 + 512].rearrange("(c p) n -> p c n", p=P)

        def of_expert(w, e):
            return w[e] if isinstance(e, int) else w[bass.ds(e, 1)].rearrange("a k n -> (a k) n")

        def up_chunk(e, i):
            w, q = of_expert((g1, g3)[i // 4], e), i % 4
            return w[q * CH * P:(q + 1) * CH * P, :].rearrange("(c p) n -> p c n", p=P)

        def down_chunk(e, i):
            return of_expert(g2, e)[:, i * 512:(i + 1) * 512].rearrange("(c p) n -> p c n", p=P)

        @block.sync
        def _(sp):
            sp.dma_start(ident[:], ins["c_eye"]).then_inc(S["eye_in"], 16)
            for n, name in enumerate(["norm_mix", "norm_cross", "norm_ffn", "norm_mem", "group_gain"]):
                src = ins[name] if name == "norm_mem" else ins[name][0]
                sp.dma_start(rows[n * KT:(n + 1) * KT, :], src.rearrange("(k p) -> k p", p=P)).then_inc(S["rows_in"], 16)
            sp.dma_start(rows[80:104, :], ins["mlstm_conv"][0].rearrange("t (c p) -> (t c) p", p=P)).then_inc(S["rows_in"], 16)
            sp.dma_start(h, ins["x"][0].rearrange("(j p) d -> p j d", p=P)).then_inc(S["x_in"], 16)
            sp.dma_start(mem, ins["mem"][0].rearrange("(j p) d -> p j d", p=P)).then_inc(S["mem_in"], 16)

            def load_dense(g):
                for i in range(NCH):
                    c = g * NCH + i
                    if c >= RING_A:
                        sp.wait_ge(S["chunk_used"], c - RING_A + 1)
                    sp.dma_start(ring_a[i], dense_chunk(g, i)).then_inc(s_ring[i], 16)

            for g in range(4):
                load_dense(g)
                if g == 0:
                    with nc.allow_non_contiguous_dma(reason="gate columns"):
                        sp.dma_start(wg, ins["w_in"][0][:, G_COL:G_COL + 16].rearrange("(c p) n -> p c n", p=P)).then_inc(S["wg_in"], 16)
                        sp.dma_start(gbias, ins["mlstm_gate_bias"][0].rearrange("(k h) -> h k", h=NH)).then_inc(S["gbias_in"], 16)
                    sp.dma_start(mixc, ins["c_mix"]).then_inc(S["cmix_in"], 16)
                    sp.dma_start(arena(188.25, 5 * 256), ins["c_dft"]).then_inc(S["cdft_in"], 16)
                    sp.dma_start(hmask_f, ins["c_masks"]).then_inc(S["cmask_in"], 16)
            for g in range(4, G_WO):
                load_dense(g)

            def load_up(e, n, i):
                if not (isinstance(n, int) and n == 0 and i < RING_E):
                    sp.wait_ge(S["up_used"], n * UCH + (i + 1 - RING_E))
                sp.dma_start(ring_up[i % RING_E], up_chunk(e, i)).then_inc(s_up[i % RING_E], 16)

            def load_down(e, n, i):
                if not (isinstance(n, int) and n == 0):
                    sp.wait_ge(S["dn_used"], n * DCH + (i + 1 - RING_E))
                sp.dma_start(ring_dn[i], down_chunk(e, i)).then_inc(s_dn[i], 16)

            sp.wait_ge(S["y_done"], 4)
            for i in range(RING_E):
                load_up(0, 0, i)
            for i in range(DCH):
                load_down(0, 0, i)
            for g in range(G_WO, G_XO + 4):
                load_dense(g)
            sp.wait_ge(S["xs_o"], XA_H)
            with nc.allow_non_contiguous_dma(reason="router columns"):
                sp.dma_start(wr[:, :, 0:NG], ins["moe_router_group"][0].rearrange("(c p) n -> p c n", p=P)).then_inc(S["wr_in"], 16)
                sp.dma_start(wr[:, :, NG:], ins["moe_router_expert"][0].rearrange("(c p) n -> p c n", p=P)).then_inc(S["wr_in"], 16)
            sp.dma_start(routec, ins["c_route"]).then_inc(S["route_in"], 16)
            for i in range(RING_E, UCH):
                load_up(0, 0, i)
            for i in range(UCH):
                load_up(1, 1, i)
            with sp.Fori(2, NE) as e:
                for i in range(UCH):
                    load_up(e, e, i)
                    if i % 2 == 1:
                        load_down(e - 1, e - 1, i // 2)
            for i in range(DCH):
                load_down(NE - 1, NE - 1, i)
            sp.wait_ge(S["tab_dve"], 2)
            nov = sp.value_load(table[0:1, 96:97], min_val=0, max_val=OVB)
            with sp.Fori(0, OVB) as b:
                with sp.If(b < nov):
                    e = sp.value_load(table[0:1, bass.ds(b + 32, 1)], min_val=0, max_val=NE - 1)
                    for i in range(UCH):
                        load_up(e, b + NE, i)
                    for i in range(DCH):
                        load_down(e, b + NE, i)
            sp.wait_ge(S["c_tp"], 1)
            sp.dma_start(fgain, ins["norm_final"].rearrange("(a d) -> a d", a=1).to_broadcast([P, D])).then_inc(S["fgain_in"], 16)
            for j in range(NT):
                sp.wait_ge(S["fin_dve"], j + 1)
                sp.dma_start(out[0, j * P:(j + 1) * P, :], res[:, j, :]).then_inc(S["out_done"], 16)
            sp.wait_ge(S["out_done"], 16 * NT)

        @block.gpsimd
        def _(pool):
            nc.gpsimd.memset(gone, 1.0).then_inc(S["pool_step"], 1)
            nc.gpsimd.memset(buf["mv"][:, :, :, P:P + 1], 1.0).then_inc(S["pool_step"], 1)
            for s in range(2 * HG_LEVELS):
                w, half = s // HG_LEVELS, 1 << (s % HG_LEVELS)
                u = 0 if w == 0 else 1
                cut = lambda x: flat(x).rearrange("p (b u t) -> p b u t", u=2, t=half)[:, :, u, :]
                pool.wait_ge(S["h_exp"], s + 1)
                if s >= 1:
                    pool.wait_ge(S["h_pe"], s)
                nc.gpsimd.tensor_tensor(cut(hqk[s % 2]), cut(he[s % 2]), cut(buf["hff" if w == 0 else "hfb"]),
                                        ALU.mult).then_inc(S["h_mulk"], 1)
            rpb = ins["na_rpb"]
            for m in range(NA_H // 2 * NT):
                i, j = m // NT, m % NT
                if m == 0:
                    pool.wait_ge(S["h_pe"], 2 * HG_LEVELS + 1)
                    pool.wait_ge(S["h_mulk"], 2 * HG_LEVELS)
                    pool.wait_ge(S["h_mulq"], 2 * HG_LEVELS)
                if m >= 2:
                    pool.wait_ge(S["na_s"], m - 1)
                for g in range(2):
                    r = 2 * j + 1 - g
                    for u in range(2):
                        hd = 2 * i + u
                        src = bass.AP(tensor=rpb.tensor, offset=rpb.offset + hd * RPB_R * RPB_C + (7 - r) * RPB_C - 48,
                                      ap=[[1, GRID_W], [RPB_C, 4], [1, GRID_W]])
                        pool.dma_start(nbias[m % 2][g * 64:(g + 1) * 64, u, :].rearrange("p (a w) -> p a w", w=GRID_W),
                                       src).then_inc(S["bias_in0" if m % 2 == 0 else "bias_in1"], 16)

        @block.tensor
        def _(pe):
            mm = nc.tensor.matmul

            def turn(n, src, scales):
                for kk in range(KT // 2):
                    q = n * (KT // 2) + kk
                    if q >= 4:
                        pe.wait_ge(S["tp_act" if q % 2 == 0 else "tp_dve"], (q - 4) // 2 + 1)
                    o_ = bank(4 + kk % 4, 2, NT, P)
                    for u in range(2):
                        for j in range(NT):
                            k = 2 * kk + u
                            last = mm(o_[:, u, j, :], src[:, j, k * P:(k + 1) * P], scales[j], start=True, stop=True)
                    last.then_inc(S["tp_pe"], 1)

            def dense(g, feature_major, act, part=range(NCH)):
                b0 = 2 * (g % 2)
                for i in part:
                    if i == 0 and g >= 2:
                        pe.wait_ge(S["proj_a"], g - 1)
                        pe.wait_ge(S["proj_b"], g - 1)
                    pe.wait_ge(s_ring[i], 16 * (g + 1))
                    for c in range(CH):
                        k = i * CH + c
                        if feature_major:
                            for n in range(4):
                                last = mm(ps[:, b0 + n // 2, (n % 2) * T:(n % 2 + 1) * T], ring_a[i][:, c, n * P:(n + 1) * P],
                                          act[:, k, :], start=(k == 0 and n % 2 == 0), stop=(k == KT - 1),
                                          skip_group_check=True)
                        else:
                            for j in range(NT):
                                last = mm(ps[:, b0 + j, :], act[:, k, j * P:(j + 1) * P], ring_a[i][:, c, :],
                                          start=(k == 0), stop=(k == KT - 1))
                    last.then_inc(S["chunk_used"], 1)

            pe.wait_ge(S["eye_in"], 16)
            pe.wait_ge(S["rows_in"], 16 * 6)
            mm(ps[:, 0, 0:104], rows[0:104, :], ident[0:104, 0:104], start=True, stop=True).then_inc(S["cols_pe"], 1)
            pe.wait_ge(S["x_in"], 16)
            pe.wait_ge(S["diag_dve"], 1)
            turn(0, h, [diag[:, j, :] for j in range(NT)])
            pe.wait_ge(S["mem_in"], 16)
            pe.wait_ge(S["diag_dve"], 2)
            turn(1, mem, [diag[:, j, :] for j in range(NT)])
            pe.wait_ge(S["tp_act"], 8)
            pe.wait_ge(S["tp_dve"], 8)
            pe.wait_ge(S["cols_act"], 1)
            for g, (name, fm, _, _) in enumerate(W_IN):
                dense(g, fm, xT)
                if g == 3:
                    pe.wait_ge(S["wg_in"], 16)
                    for j in range(NT):
                        for k in range(KT):
                            last = mm(bank(4, NT, 16)[:, j, :], xT[:, k, j * P:(j + 1) * P], wg[:, k, :],
                                      start=(k == 0), stop=(k == KT - 1))
                    last.then_inc(S["gate_pe"], 1)
                    pe.wait_ge(S["gate_dve"], 1)
                    for kind in range(4):
                        for j in range(NT):
                            last = mm(ps[0:NH, 5 + kind // 2, (kind % 2) * T + j * P:(kind % 2) * T + (j + 1) * P],
                                      gtok[:, j, kind * NH:(kind + 1) * NH], ident[:], start=True, stop=True)
                    last.then_inc(S["gate_pe"], 1)
            pe.wait_ge(S["gate_dve"], 3)
            pe.wait_ge(S["gate_act"], 2)
            for j in range(NT):
                for kind in range(4):
                    last = mm(bank(4, NT, 4, NH)[:, j, kind, :], gr[:, kind, j * P:(j + 1) * P], ident[0:NH, 0:NH],
                              start=True, stop=True)
            last.then_inc(S["gate_pe"], 1)
            pe.wait_ge(S["cmix_in"], 16)
            pe.wait_ge(S["silu_act"], 2)
            pe.wait_ge(S["pool_step"], 2)
            pe.wait_ge(S["proj_a"], 3)
            pe.wait_ge(S["proj_b"], 3)
            pe.wait_ge(S["gate_dve"], 4)
            q, k = buf["q"], buf["k"]
            for hd in range(NH):
                if hd >= 1:
                    pe.wait_ge(S["ml_sw"], 2 * hd)
                    pe.wait_ge(S["ml_w"], 2 * hd)
                for u in range(NT):
                    last = mm(bank(4, NT, T)[:, u, :], k[:, hd, u * P:(u + 1) * P], q[:, hd, :], start=True, stop=True)
                last.then_inc(S["ml_pe_s"], 1)
                for w in range(2):
                    last = mm(bank(6, 2, T)[:, w, :], selh[:, hd, :], gm[:, w, :], start=True, stop=True)
                last.then_inc(S["ml_pe_m"], 1)
                for w in range(2):
                    pe.wait_ge(S["ml_sw"], 2 * hd + w + 1)
                    if hd >= 1:
                        pe.wait_ge(S["ml_y"], hd)
                        pe.wait_ge(S["ml_den"], 2 * hd)
                    o_ = bank(7 if w == 0 else 5, NT, P + 1)
                    parts = [(0, 0, 0, True, True), (1, 1, 0, True, False), (1, 2, 1, False, True)] if w == 0 else \
                            [(0, 0, 0, True, False), (0, 1, 1, False, True), (1, 2, 1, True, True)]
                    for j, tile, u, a, z in parts:
                        last = mm(o_[:, j, :], msw[w][:, tile, :], buf["mv"][:, u, hd, :], start=a, stop=z)
                    last.then_inc(S["ml_pv"], 1)
            pe.wait_ge(S["cdft_in"], 16)
            pe.wait_ge(S["proj_a"], G_IN)
            pe.wait_ge(S["proj_b"], G_IN)
            pe.wait_ge(S["ml_y"], NH)
            pe.wait_ge(S["ml_den"], 2 * NH)
            for j in range(NT):
                for g in range(NH):
                    last = mm(bank(4 + 2 * j + g // 2, 2, 2 * P)[:, g % 2, :], buf["fu"][:, g, j * P:(j + 1) * P], dft_c,
                              start=True, stop=True)
            last.then_inc(S["fn_pe"], 1)
            pe.wait_ge(S["fn_act"], 1)
            pe.wait_ge(S["fn_dve"], 1)
            for j in range(NT):
                for n, (tab, u) in enumerate([(0, 0), (0, 1), (1, 0), (1, 1)]):
                    last = mm(ps[:, 4 + j, :], dft_t[:, tab, u, j * P:(j + 1) * P], fa[:, u, :, tab, :],
                              start=(n == 0), stop=(n == 3))
            last.then_inc(S["fn_pe"], 1)
            pe.wait_ge(S["fn_act"], 2)
            pe.wait_ge(S["fn_dve"], 2)
            pe.wait_ge(S["hp_dve"], 3)
            pe.wait_ge(S["hp_act"], 8)
            pe.wait_ge(S["silu_act"], 4)
            for hd in range(NH):
                for u in range(NT):
                    last = mm(bank(4 + u, NH, P)[:, hd, :], hqk[1][:, hd, u * P:(u + 1) * P],
                              buf["hq"][:, hd, u * P:(u + 1) * P], start=True, stop=True)
            last.then_inc(S["h_pe"], 1)
            for s in range(2 * HG_LEVELS):
                w, lev = s // HG_LEVELS, s % HG_LEVELS
                dense(G_WK + s // 4, True, memT, part=[s % 4])
                pe.wait_ge(S["h_mulq"], s + 1)
                pe.wait_ge(S["h_mulk"], s + 1)
                if s >= 1:
                    pe.wait_ge(S["h_cp"], s)
                qk = hqk[s % 2]
                b0 = 6 - 2 * (s % 2)
                for hd in range(NH):
                    if lev < HG_LEVELS - 1:
                        for u in range(NT):
                            t_ = qk[:, hd, u * P:(u + 1) * P]
                            last = mm(bank(b0 + u, NH, P)[:, hd, :], t_, t_, start=True, stop=True)
                    else:
                        a, z = qk[:, hd, 0:P], qk[:, hd, P:2 * P]
                        last = mm(bank(b0, NH, P)[:, hd, :], *((a, z) if w == 0 else (z, a)), start=True, stop=True)
                last.then_inc(S["h_pe"], 1)
            pe.wait_ge(S["h_cp"], 2 * HG_LEVELS + 1)
            for j in range(NT):
                for hd in range(NH):
                    for u in range(NT):
                        last = mm(bank(4 + j, NH, P)[:, hd, :], decay_to[:, u, hd, j * P:(j + 1) * P],
                                  buf["hi"][:, u, hd * P:(hd + 1) * P], start=(u == 0), stop=(u == NT - 1))
            last.then_inc(S["h_o"], 1)
            for m in range(NA_H // 2 * NT):
                i, j = m // NT, m % NT
                dense(G_WV + m // 2, False, memT, part=[2 * (m % 2), 2 * (m % 2) + 1])
                if m == 0:
                    pe.wait_ge(S["h_oev"], 2)
                else:
                    pe.wait_ge(S["na_m"], m)
                pe.wait_ge(S["bias_in0" if m % 2 == 0 else "bias_in1"], 64 * (m // 2 + 1))
                for u in range(2):
                    o_ = ps[:, 4 + 3 * u, 0:T]
                    mm(o_, flipm, nbias[m % 2][:, u, :], start=True, stop=False)
                    last = mm(o_, buf["nq"][64 * u:64 * u + 64, i, j * P:(j + 1) * P], buf["nk"][64 * u:64 * u + 64, i, :],
                              start=False, stop=True)
                last.then_inc(S["na_s"], 1)
                pe.wait_ge(S["na_p"], 2 * (m + 1))
                if m >= 1:
                    pe.wait_ge(S["na_tev"], m)
                for u in range(2):
                    for s in range(NT):
                        last = mm(bank(5, 2, NT, P)[:, u, s, :], npr[:, u, s * P:(s + 1) * P], ident[:], start=True, stop=True)
                last.then_inc(S["na_t"], 1)
                pe.wait_ge(S["na_tev"], m + 1)
                if m >= 1:
                    pe.wait_ge(S["na_y"], 2 * m)
                for u in range(2):
                    for s in range(NT):
                        last = mm(bank(6, 2, NA_D)[:, u, :], npt[:, u, s, :], buf["nv"][:, s, (2 * i + u) * NA_D:(2 * i + u + 1) * NA_D],
                                  start=(s == 0), stop=(s == NT - 1))
                last.then_inc(S["na_o"], 1)
            pe.wait_ge(S["y_done"], 4)
            turn(2, y, [ident[:]] * 2)
            pe.wait_ge(S["tp_act"], 12)
            pe.wait_ge(S["tp_dve"], 12)
            for g in range(4):
                dense(G_WO + g, False, memT)
            pe.wait_ge(S["diag_dve"], 3)
            turn(3, h, [diag[:, j, :] for j in range(NT)])
            pe.wait_ge(S["tp_act"], 16)
            pe.wait_ge(S["tp_dve"], 16)
            for g in range(4):
                dense(G_WQ + g, True, xT)
            pe.wait_ge(S["proj_a"], G_WQ + 4)
            pe.wait_ge(S["proj_b"], G_WQ + 4)

            def xa_scores(hd):
                if hd >= 1:
                    pe.wait_ge(S["xs_p"], 2 * hd)
                for j in range(NT):
                    for c in range(NH):
                        last = mm(bank(4, NT, T)[:, j, :], qT[:, 4 * hd + c, j * P:(j + 1) * P], kT[:, 4 * hd + c, :],
                                  start=(c == 0), stop=(c == NH - 1))
                last.then_inc(S["xs_pe"], 1)

            for hd in range(XA_H):
                xa_scores(hd)
                pe.wait_ge(S["xs_diag"], hd + 1)
                if hd >= 1:
                    pe.wait_ge(S["xs_tev"], hd)
                for s in range(NT):
                    for j in range(NT):
                        last = mm(bank(5, NT, NT, P)[:, s, j, :], xp[:, j, s * P:(s + 1) * P], diag[:, j, :], start=True, stop=True)
                last.then_inc(S["xs_t"], 1)
                pe.wait_ge(S["xs_tev"], hd + 1)
                if hd >= 1:
                    pe.wait_ge(S["xs_oa"], hd)
                    pe.wait_ge(S["xs_od"], hd)
                for c in range(NH):
                    for s in range(NT):
                        last = mm(bank(6 + c // 2, 2, T)[:, c % 2, :], v[:, s, (4 * hd + c) * P:(4 * hd + c + 1) * P], xpt[:, s, :],
                                  start=(s == 0), stop=(s == NT - 1))
                last.then_inc(S["xs_o"], 1)
            pe.wait_ge(S["xs_oa"], XA_H)
            pe.wait_ge(S["xs_od"], XA_H)
            for g in range(4):
                dense(G_XO + g, False, oT)
            pe.wait_ge(S["diag_dve"], 4)
            turn(4, h, [diag[:, j, :] for j in range(NT)])
            pe.wait_ge(S["tp_act"], 20)
            pe.wait_ge(S["tp_dve"], 20)
            pe.wait_ge(S["wr_in"], 32)
            for j in range(NT):
                for k_ in range(KT):
                    last = mm(bank(4, NT, 36)[:, j, :], xT[:, k_, j * P:(j + 1) * P], wr[:, k_, :], start=(k_ == 0), stop=(k_ == KT - 1))
            last.then_inc(S["r_pe"], 1)
            pe.wait_ge(S["route_in"], 16)
            pe.wait_ge(S["r_dve"], 3)
            o_ = bank(5, 3, NE)
            mm(o_[:, 0, :], before, hit[:, 0, :], start=True, stop=True)
            mm(o_[:, 1, :], before, hit[:, 1, :], start=True, stop=False)
            mm(o_[:, 1, :], ones, hit[:, 0, :], start=False, stop=True)
            mm(o_[:, 2, :], ones, hits, start=True, stop=True).then_inc(S["r_pe"], 1)
            pe.wait_ge(S["r_dve"], 4)
            mm(ps[0:1, 6, 0:P], eid, ident[:], start=True, stop=True)
            mm(ps[0:1, 6, P:2 * P], ost, ident[:], start=True, stop=True).then_inc(S["r_pe"], 1)
            pe.wait_ge(S["tab_dve"], 1)
            for k_ in range(KT):
                if k_ >= 4:
                    pe.wait_ge(S["g_act" if k_ % 2 == 0 else "g_dve"], (k_ - 4) // 2 + 1)
                elif k_ == 2:
                    pe.wait_ge(S["tab_dve"], 2)
                for j in range(NT):
                    last = mm(ps[:, 4 + k_ % 4, :], h[:, j, k_ * P:(k_ + 1) * P], sel_r[:, j, :], start=(j == 0), stop=(j == NT - 1))
                last.then_inc(S["g_pe"], 1)
            pe.wait_ge(S["g_act"], KT // 2)
            pe.wait_ge(S["g_dve"], KT // 2 + 1)
            for s in range(SLOTS // P):
                for j in range(NT):
                    last = mm(bank(4 + s // 2, 2, NT, P)[:, s % 2, j, :], sel_g[:, j, s * P:(s + 1) * P], ident[:], start=True, stop=True)
            last.then_inc(S["sg_pe"], 1)
            def up(n, i):
                r = i % RING_E
                if i == 0:
                    pe.wait_ge(S["xe_lo"], n + 1)
                pe.wait_ge(S["up_lo"], n * UCH + (i + 1))
                for c in range(CH):
                    k_ = (i % 4) * CH + c
                    o_ = ps[0:EB, i // 4, :]
                    mm(o_, xe_hi[:, k_, :], up_hi[r][:, c, :], start=(k_ == 0), stop=False)
                    mm(o_, xe_hi[:, k_, :], up_lo[r][:, c, :], start=False, stop=False)
                    last = mm(o_, xe_lo[:, k_, :], up_hi[r][:, c, :], start=False, stop=(k_ == KT - 1))
                last.then_inc(S["up_used"], 1)

            def turn_h(n):
                pe.wait_ge(S["e_h"], n + 1)
                for f in range(FF // P):
                    last = mm(bank(6, FF // P, P)[:, f, :], sg[:, f * P:(f + 1) * P], ident[0:EB, :], start=True, stop=True)
                last.then_inc(S["e_turn"], 1)

            def down(n, i):
                if i == 0:
                    pe.wait_ge(S["e_hT"], n + 1)
                if not (isinstance(n, int) and n == 0):
                    pe.wait_ge(S["e_ya" if i < 2 else "e_yd"], n * 2 + (i % 2 - 1))
                pe.wait_ge(s_dn[i], (n + 1) * 16)
                for c in range(CH):
                    for f in range(FF // P):
                        last = mm(bank(2 + i, CH, EW)[:, c, :], ring_dn[i][:, f, c * P:(c + 1) * P],
                                  hT[:, f, :], start=(f == 0), stop=(f == FF // P - 1))
                last.then_inc(S["dn_used"], 1)

            def block_n(n, back):
                if back is not None:
                    turn_h(back)
                for i in range(UCH):
                    up(n, i)
                    if back is not None and i % 2 == 1:
                        down(back, i // 2)

            pe.wait_ge(S["sg_act"], 1)
            pe.wait_ge(S["proj_b"], G_XO + 4)
            block_n(0, None)
            block_n(1, 0)
            with pe.Fori(2, NE) as e:
                block_n(e, e - 1)
            turn_h(NE - 1)
            for i in range(DCH):
                down(NE - 1, i)
            pe.wait_ge(S["tab_dve"], 2)
            nov = pe.value_load(table[0:1, 96:97], min_val=0, max_val=OVB)
            with pe.Fori(0, OVB) as b:
                with pe.If(b < nov):
                    block_n(b + NE, None)
                    turn_h(b + NE)
                    for i in range(DCH):
                        down(b + NE, i)
            nc.tensor.matmul(ps[:, 6, 0:P], ident[:], ident[:], start=True, stop=True).then_inc(S["c_tp"], 1)
            pe.wait_ge(S["c_act"], 1)
            pe.wait_ge(S["c_dve"], 1)
            n = 0
            for s in range(SLOTS // P):
                for kk in range(4):
                    if n >= 4:
                        pe.wait_ge(S["c_act" if n % 2 == 0 else "c_dve"], (n - 4) // 2 + 2)
                    for u in range(4):
                        k_ = 4 * kk + u
                        last = mm(ps[:, 4 + n % 4, u * P:(u + 1) * P], ysT[:, k_, s * P:(s + 1) * P], ident[:], start=True, stop=True)
                    last.then_inc(S["c_tp"], 1)
                    n += 1
            pe.wait_ge(S["c_act"], 9)
            pe.wait_ge(S["c_dve"], 9)
            for j in range(NT):
                for g in range(4):
                    m = 4 * j + g
                    if m >= 4:
                        pe.wait_ge(S["c_add"], m - 3)
                    for s in range(SLOTS // P):
                        last = mm(ps[:, m % 4, :], selgT[:, s, j * P:(j + 1) * P], ys[:, s, g * 512:(g + 1) * 512],
                                  start=(s == 0), stop=(s == SLOTS // P - 1))
                    last.then_inc(S["c_pe"], 1)

        @block.scalar
        def _(act):
            fn = nc.scalar.activation
            steps, calls = [0], [0]

            def step(ins_):
                steps[0] += 1
                ins_.then_inc(S["act_step"], 1)
                act.wait_ge(S["act_step"], steps[0])

            def squares(src):
                step(fn(flat(ps[:, 0:4, :]), src[:, 0, :], ACT.Square, accum_out=st[:, 0:1]))
                fn(flat(ps[:, 0:4, :]), src[:, 1, :], ACT.Square, accum_out=st[:, 1:2]).then_inc(S["sq_act"], 1)

            def rsqrt(w):
                calls[0] += 1
                act.wait_ge(S["var_dve"], calls[0])
                step(fn(st[:, 16:16 + w], st[:, 8:8 + w], ACT.Ln))
                fn(st[:, 24:24 + w], st[:, 16:16 + w], ACT.Exp, scale=-0.5).then_inc(S["rs_act"], 1)

            def turned(n, dst, gain):
                for kk in range(0, KT // 2, 2):
                    act.wait_ge(S["tp_pe"], n * (KT // 2) + kk + 1)
                    for u in range(2):
                        k = 2 * kk + u
                        last = fn(dst[:, k, :], ps[:, 4 + kk % 4, u * T:(u + 1) * T], ACT.Copy, scale=cols[:, gain * KT + k:gain * KT + k + 1])
                    last.then_inc(S["tp_act"], 1)

            def dense_out(g, dst, scale=1.0):
                act.wait_ge(S["chunk_used"], NCH * (g + 1))
                fn(dst, ps[:, 2 * (g % 2), :] if len(dst.shape) == 2 else bank(2 * (g % 2), NH, P), ACT.Copy, scale=scale).then_inc(S["proj_a"], 1)

            act.wait_ge(S["cols_pe"], 1)
            fn(cols[:], ps[:, 0, 0:104], ACT.Copy).then_inc(S["cols_act"], 1)
            act.wait_ge(S["cols_act"], 1)
            act.wait_ge(S["x_in"], 16)
            squares(h)
            rsqrt(NT)
            act.wait_ge(S["mem_in"], 16)
            act.wait_ge(S["diag_dve"], 1)
            squares(mem)
            turned(0, xT, 0)
            rsqrt(NT)
            turned(1, memT, 3)
            for g, (name, fm, _, scale) in enumerate(W_IN):
                if name == "mv":
                    dst = buf[name][:, 0, :, 0:P]
                elif fm:
                    dst = flat(buf[name][:, 0:2, :])
                else:
                    dst = buf[name][:, 0, :]
                dense_out(g, dst, scale)
                if g == 2:
                    act.wait_ge(S["conv_dve"], 1)
                    fn(flat(buf["q"]), flat(buf["q"]), ACT.Silu).then_inc(S["silu_act"], 1)
                    act.wait_ge(S["conv_dve"], 2)
                    fn(flat(buf["k"]), flat(buf["k"]), ACT.Silu).then_inc(S["silu_act"], 1)
                if g in (3, 4, 8):
                    b_ = buf[name]
                    act.wait_ge(S["proj_a"], g + 1)
                    act.wait_ge(S["proj_b"], g + 1)
                    fn(flat(b_), flat(b_), ACT.Sigmoid if g == 3 else ACT.Silu).then_inc(S["silu_act"], 1)
                if g == 5:
                    act.wait_ge(S["gate_dve"], 2)
                    step(fn(gl, gt[:, 1::2, :], ACT.Abs))
                    step(fn(gl, gl, ACT.Exp, scale=-1.0))
                    fn(gl, gl, ACT.Ln, bias=1.0).then_inc(S["gate_act"], 1)
                    act.wait_ge(S["gate_dve"], 3)
                    fn(gr[:, 2:4, :], gr[:, 2:4, :], ACT.Exp, scale=-1.0).then_inc(S["gate_act"], 1)
            act.wait_ge(S["gate_dve"], 4)
            for hd in range(NH):
                act.wait_ge(S["ml_pe_m"], hd + 1)
                for w in range(2):
                    act.wait_ge(S["ml_arg"], 2 * hd + 2)
                    if hd >= 1:
                        act.wait_ge(S["ml_sw"], 2 * hd - 1 + w)
                    nm = bank(6, 2, T)[:, w, :]
                    tiles = [(marg[w], 0, 0), (nm, 1, 0), (marg[w], 1, 1)] if w == 0 else [(marg[w], 0, 0), (nm, 0, 1), (marg[w], 1, 1)]
                    for n, (src, j, u) in enumerate(tiles):
                        last = fn(mw[w][:, n, :], src[:, j * P:(j + 1) * P], ACT.Exp, bias=mlc[:, u, w, hd:hd + 1])
                    last.then_inc(S["ml_w"], 1)
                if hd >= 1:
                    act.wait_ge(S["ml_y"], hd)
                for w in range(2):
                    act.wait_ge(S["ml_pv"], 2 * hd + w + 1)
                    fn(st[:, 44 + 2 * w:46 + 2 * w], bank(7 if w == 0 else 5, NT, P + 1)[:, :, P], ACT.Abs).then_inc(S["ml_den"], 1)
            rsqrt(NT)
            act.wait_ge(S["fn_pe"], 1)
            fn(fa[:, 0].rearrange("p g c n -> p (g c n)"), flat(ps[:, 4:6, :]), ACT.Copy).then_inc(S["fn_act"], 1)
            act.wait_ge(S["fn_pe"], 2)
            fn(y[:, 0, 2 * GW:3 * GW], ps[:, 4, :], ACT.Copy).then_inc(S["fn_act"], 1)
            rsqrt(NT)
            for w, name in enumerate(("hff", "hfb")):
                f = flat(buf[name])
                if w == 1:
                    act.wait_ge(S["hp_act"], 4)
                act.wait_ge(S["ml_y"], NH)
                fn(flat(htmp), f, ACT.Abs).then_inc(S["hp_act"], 1)
                act.wait_ge(S["hp_act"], 4 * w + 1)
                fn(flat(htmp), flat(htmp), ACT.Exp, scale=-1.0).then_inc(S["hp_act"], 1)
                act.wait_ge(S["hp_act"], 4 * w + 2)
                fn(flat(htmp), flat(htmp), ACT.Ln, bias=1.0).then_inc(S["hp_act"], 1)
                act.wait_ge(S["hp_dve"], w + 1)
                fn(f, flat(htmp), ACT.Exp).then_inc(S["hp_act"], 1)
            for s in range(2 * HG_LEVELS):
                act.wait_ge(S["h_sub"], s + 1)
                fn(flat(he[s % 2]), flat(he[s % 2]), ACT.Exp).then_inc(S["h_exp"], 1)
                if s % 4 == 3:
                    g = G_WK + s // 4
                    dense_out(g, flat(kT[:, 4 * (g - G_WK):4 * (g - G_WK) + 2, :]))
            act.wait_ge(S["h_o"], 1)
            fn(y[:, 0, GW:2 * GW], ps[:, 4, :], ACT.Copy).then_inc(S["h_oev"], 1)
            rsqrt(NT * NH)
            rsqrt(NT)
            for m in range(NA_H // 2 * NT):
                act.wait_ge(S["na_max"], m + 1)
                if m >= 1:
                    act.wait_ge(S["na_t"], m)
                    act.wait_ge(S["na_r"], m)
                for u in range(2):
                    fn(npr[:, u, :], ns[:, u, :], ACT.Exp, bias=st[:, 52 + u:53 + u], accum_out=st[:, 54 + u:55 + u]).then_inc(S["na_p"], 1)
                act.wait_ge(S["na_t"], m + 1)
                if m >= 1:
                    act.wait_ge(S["na_o"], m)
                fn(npt.rearrange("p u s t -> p (u s t)"), ps[:, 5, :], ACT.Copy).then_inc(S["na_tev"], 1)
                if m % 2 == 1:
                    g = G_WV + m // 2
                    dense_out(g, v[:, 0, GW * (m // 2):GW * (m // 2 + 1)])
            rsqrt(NT)
            turned(2, memT, 4)
            act.wait_ge(S["proj_a"], G_WO + 4)
            act.wait_ge(S["proj_b"], G_WO + 4)
            squares(h)
            rsqrt(NT)
            turned(3, xT, 1)
            for g in range(G_WQ, G_WQ + 4):
                n = 4 * (g - G_WQ)
                dense_out(g, flat(qT[:, n:n + 2, :]))
            for hd in range(XA_H):
                act.wait_ge(S["xs_max"], hd + 1)
                if hd >= 1:
                    act.wait_ge(S["xs_t"], hd)
                for j in range(NT):
                    fn(xp[:, j, :], bank(4, NT, T)[:, j, :], ACT.Exp, bias=st[:, 52 + j:53 + j], scale=XA_D ** -0.5,
                       accum_out=st[:, 54 + j:55 + j]).then_inc(S["xs_p"], 1)
                act.wait_ge(S["xs_t"], hd + 1)
                if hd >= 1:
                    act.wait_ge(S["xs_o"], hd)
                fn(flat(xpt), ps[:, 5, :], ACT.Copy).then_inc(S["xs_tev"], 1)
                act.wait_ge(S["xs_o"], hd + 1)
                fn(flat(oT[:, 4 * hd:4 * hd + 2, :]), ps[:, 6, :], ACT.Copy).then_inc(S["xs_oa"], 1)
            act.wait_ge(S["proj_a"], G_XO + 4)
            act.wait_ge(S["proj_b"], G_XO + 4)
            squares(h)
            rsqrt(NT)
            turned(4, xT, 2)
            act.wait_ge(S["r_dve"], 1)
            for j in range(NT):
                step(fn(gexp, logit[:, j, 0:NG], ACT.Exp, bias=negm[:, j:j + 1], accum_out=gsum[:, j:j + 1]))
            act.wait_ge(S["r_dve"], 2)
            fn(vdif, vdif, ACT.Exp).then_inc(S["r_act"], 1)
            for k in range(0, KT, 2):
                act.wait_ge(S["g_pe"], k + 1)
                fn(xsT[:, k, 0:SLOTS], ps[:, 4 + k % 4, :], ACT.Copy, scale=cols[:, 2 * KT + k:2 * KT + k + 1]).then_inc(S["g_act"], 1)
            act.wait_ge(S["sg_pe"], 1)
            fn(flat(selgT), flat(ps[:, 4:6, :]), ACT.Copy).then_inc(S["sg_act"], 1)
            act.wait_ge(S["sg_act"], 1)
            def start_of(n):
                at = n if isinstance(n, int) else bass.ds(n, 1)
                return act.value_load(table[0:1, at:at + 1] if isinstance(n, int) else table[0:1, at], min_val=0, max_val=SLOTS)

            def tokens_hi(n, s):
                if not (isinstance(n, int) and n == 0):
                    act.wait_ge(S["up_used"], n * UCH)
                fn(xe_hi[:], xsT[:, :, bass.ds(s, EB)], ACT.Copy).then_inc(S["xe_hi"], 1)

            def weights_hi(n, part):
                for i in part:
                    r = i % RING_E
                    act.wait_ge(s_up[r], n * 32 + 16 * (i // RING_E + 1))
                    fn(up_hi[r][:], ring_up[r], ACT.Copy).then_inc(S["up_hi"], 1)

            def silu(n):
                act.wait_ge(S["up_used"], n * UCH + 4)
                if not (isinstance(n, int) and n == 0):
                    act.wait_ge(S["e_turn"], n)
                fn(sg, ps[0:EB, 0, :], ACT.Silu).then_inc(S["e_sg"], 1)

            def output(n, s, i):
                act.wait_ge(S["dn_used"], n * DCH + (i + 1))
                if not (isinstance(n, int) and n == 0):
                    act.wait_ge(S["e_ya"], n * 2 + (i - 1))
                fn(ysT[:, CH * i:CH * (i + 1), bass.ds(s, EB)], bank(2 + i, CH, EW)[:, :, 0:EB], ACT.Copy).then_inc(S["e_ya"], 1)

            def block_n(n, back):
                weights_hi(n, range(0, 1))
                tokens_hi(n, start_of(n))
                weights_hi(n, range(1, 4))
                if back is not None:
                    sb_ = start_of(back)
                    output(back, sb_, 0)
                weights_hi(n, range(4, 6))
                silu(n)
                if back is not None:
                    output(back, sb_, 1)
                weights_hi(n, range(6, UCH))

            act.wait_ge(S["tab_dve"], 2)
            block_n(0, None)
            block_n(1, 0)
            with act.Fori(2, NE) as e:
                block_n(e, e - 1)
            for i in range(2):
                output(NE - 1, start_of(NE - 1), i)
            nov = act.value_load(table[0:1, 96:97], min_val=0, max_val=OVB)
            with act.Fori(0, OVB) as b:
                with act.If(b < nov):
                    s = start_of(b + 64)
                    tokens_hi(b + NE, s)
                    weights_hi(b + NE, range(0, 6))
                    silu(b + NE)
                    weights_hi(b + NE, range(6, UCH))
                    for i in range(2):
                        output(b + NE, s, i)
            act.wait_ge(S["c_tp"], 1)
            fn(st[:, 60:61], ident[:, 0:1], ACT.Copy).then_inc(S["c_act"], 1)
            n = 0
            for s in range(SLOTS // P):
                for kk in range(4):
                    if n % 2 == 0:
                        act.wait_ge(S["c_tp"], n + 2)
                        fn(ys[:, s, kk * 512:(kk + 1) * 512], ps[:, 4 + n % 4, :], ACT.Copy).then_inc(S["c_act"], 1)
                    n += 1
            act.wait_ge(S["c_add"], 8)
            squares(h)
            rsqrt(NT)

        @block.vector
        def _(dve):
            V = nc.vector
            steps, calls, norms = [0], [0], [0]

            def step(ins_):
                steps[0] += 1
                ins_.then_inc(S["dve_step"], 1)
                dve.wait_ge(S["dve_step"], steps[0])

            def rsqrt(w, inv):
                calls[0] += 1
                ss, var, r, t_ = st[:, 0:w], st[:, 8:8 + w], st[:, 24:24 + w], st[:, 32:32 + w]
                V.tensor_scalar(var, ss, inv, EPS, ALU.mult, ALU.add).then_inc(S["var_dve"], 1)
                dve.wait_ge(S["rs_act"], calls[0])
                step(V.tensor_tensor(t_, r, r, ALU.mult))
                step(V.tensor_tensor(t_, t_, var, ALU.mult))
                step(V.tensor_scalar(t_, t_, -0.5, 1.5, ALU.mult, ALU.add))
                step(V.tensor_tensor(r, r, t_, ALU.mult))

            def row_scale():
                norms[0] += 1
                dve.wait_ge(S["sq_act"], norms[0])
                rsqrt(NT, 1.0 / D)
                for j in range(NT):
                    last = V.tensor_scalar(diag[:, j, :], ident[:], st[:, 24 + j:25 + j], None, ALU.mult)
                last.then_inc(S["diag_dve"], 1)

            def turned(n, dst, gain):
                for kk in range(1, KT // 2, 2):
                    dve.wait_ge(S["tp_pe"], n * (KT // 2) + kk + 1)
                    for u in range(2):
                        k = 2 * kk + u
                        last = V.tensor_scalar(dst[:, k, :], ps[:, 4 + kk % 4, u * T:(u + 1) * T],
                                               cols[:, gain * KT + k:gain * KT + k + 1], None, ALU.mult)
                    last.then_inc(S["tp_dve"], 1)

            def dense_out(g, dst, scale=1.0):
                dve.wait_ge(S["chunk_used"], NCH * (g + 1))
                src = ps[:, 2 * (g % 2) + 1, :] if len(dst.shape) == 2 else bank(2 * (g % 2) + 1, NH, P)
                (V.tensor_copy(dst, src) if scale == 1.0 else V.tensor_scalar(dst, src, scale, None, ALU.mult)).then_inc(S["proj_b"], 1)

            def dense_add(g, n):
                dve.wait_ge(S["chunk_used"], NCH * (g + 1))
                for j in range(NT):
                    hv = h[:, j, GW * n:GW * (n + 1)]
                    V.tensor_tensor(hv, ps[:, 2 * (g % 2) + j, :], hv, ALU.add).then_inc(S["proj_a" if j == 0 else "proj_b"], 1)

            def group_norm(m):
                yv = y[:, :, GW * m:GW * (m + 1)]
                gtmp = arena(128, NT, GW)
                step(V.tensor_tensor(gtmp, yv, yv, ALU.mult))
                step(V.tensor_reduce(st[:, 0:NT], gtmp, AX.X, ALU.add))
                rsqrt(NT, 1.0 / GW)
                for j in range(NT):
                    last = V.tensor_scalar(yv[:, j, :], yv[:, j, :], st[:, 24 + j:25 + j], None, ALU.mult)
                last.then_inc(S["y_done"], 1)

            dve.wait_ge(S["eye_in"], 16)
            row_scale()
            dve.wait_ge(S["cols_act"], 1)
            turned(0, xT, 0)
            dve.wait_ge(S["tp_pe"], 8)
            row_scale()
            turned(1, memT, 3)
            for g, (name, fm, _, scale) in enumerate(W_IN):
                if name == "mv":
                    dst = buf[name][:, 1, :, 0:P]
                elif fm:
                    dst = flat(buf[name][:, 2:4, :])
                else:
                    dst = buf[name][:, 1, :]
                dense_out(g, dst, scale)
                if g == 0:
                    dve.wait_ge(S["cmask_in"], 16)
                    step(V.tensor_copy(hmask.rearrange("p d l t -> p (d l t)"), hmask_f))
                if g == 1:
                    dve.wait_ge(S["proj_a"], 2)
                    dve.wait_ge(S["proj_b"], 2)
                    for n, (raw, dst) in enumerate((("mq", "q"), ("mk", "k"))):
                        tap = lambda t_, c: cols[:, 80 + 8 * t_ + 4 * n + c:81 + 8 * t_ + 4 * n + c]
                        for c in range(NH):
                            last = V.tensor_scalar(buf[dst][:, c, :], buf[raw][:, c, :], tap(1, c), None, ALU.mult)
                        step(last)
                        for c in range(NH):
                            o_, i_ = buf[dst][:, c, 1:T], buf[raw][:, c, 0:T - 1]
                            last = V.scalar_tensor_tensor(o_, i_, tap(0, c), o_, ALU.mult, ALU.add)
                        step(last)
                        for c in range(NH):
                            o_, i_ = buf[dst][:, c, 0:T - 1], buf[raw][:, c, 1:T]
                            last = V.scalar_tensor_tensor(o_, i_, tap(2, c), o_, ALU.mult, ALU.add)
                        last.then_inc(S["conv_dve"], 1)
                if g == 3:
                    dve.wait_ge(S["gate_pe"], 1)
                    V.tensor_copy(gtok, bank(4, NT, 16)).then_inc(S["gate_dve"], 1)
                    dve.wait_ge(S["gbias_in"], 16)
                    dve.wait_ge(S["gate_pe"], 2)
                    for kind in range(4):
                        last = V.tensor_scalar(gt[:, kind, :], ps[0:NH, 5 + kind // 2, (kind % 2) * T:(kind % 2 + 1) * T],
                                               gbias[:, kind:kind + 1], None, ALU.add)
                    last.then_inc(S["gate_dve"], 1)
                if g == 5:
                    dve.wait_ge(S["gate_dve"], 2)
                    dve.wait_ge(S["gate_act"], 1)
                    dve.wait_ge(S["pool_step"], 1)
                    step(V.scalar_tensor_tensor(lf, gt[:, 1::2, :], 0.0, gl, ALU.min, ALU.subtract))
                    V.tensor_tensor_scan(gb[:, 0, :], gone[0:NH, :], lf[:, 0, :], 0.0, ALU.mult, ALU.add)
                    step(V.tensor_tensor_scan(gb[:, 1, ::-1], gone[0:NH, :], lf[:, 1, ::-1], 0.0, ALU.mult, ALU.add))
                    step(V.tensor_tensor(gr[:, 0:2, :], gt[:, 0::2, :], gb, ALU.subtract))
                    V.tensor_tensor_scan(gm[:, 0, :], gr[:, 0, :], gr[:, 0, :], 0.0, ALU.max, ALU.max)
                    step(V.tensor_tensor_scan(gm[:, 1, ::-1], gr[:, 1, ::-1], gr[:, 1, ::-1], 0.0, ALU.max, ALU.max))
                    step(V.tensor_tensor(gr[:, 2:4, :], gb, gm, ALU.add))
                    V.tensor_scalar(gm, gm, -1.0, None, ALU.mult).then_inc(S["gate_dve"], 1)
            dve.wait_ge(S["gate_pe"], 3)
            V.tensor_copy(mlc.rearrange("p j k h -> p (j k h)"), ps[:, 4, 0:NT * 4 * NH]).then_inc(S["gate_dve"], 1)
            dve.wait_ge(S["gate_dve"], 4)
            dve.wait_ge(S["cmix_in"], 16)
            den, rden = st[:, 44:48].rearrange("p (w j) -> p w j", w=2), st[:, 48:52].rearrange("p (w j) -> p w j", w=2)
            for hd in range(NH):
                dve.wait_ge(S["ml_pe_m"], hd + 1)
                for w in range(2):
                    if hd >= 1:
                        dve.wait_ge(S["ml_w"], 2 * hd - 1 + w)
                    V.tensor_tensor(marg[w].rearrange("p (j t) -> p j t", j=NT), bank(6, 2, NT, P)[:, w], bc_mid(tri[w], NT),
                                    ALU.add).then_inc(S["ml_arg"], 1)
                dve.wait_ge(S["ml_pe_s"], hd + 1)
                for w in range(2):
                    dve.wait_ge(S["ml_w"], 2 * hd + w + 1)
                    if hd >= 1:
                        dve.wait_ge(S["ml_pv"], 2 * hd - 1 + w)
                    sc = ps[:, 4, :]
                    cuts = [(0, 2, 0), (2, 3, 3)] if w == 0 else [(0, 1, 0), (1, 3, 2)]
                    for a, z, at in cuts:
                        last = V.scalar_tensor_tensor(flat(msw[w][:, a:z, :]), sc[:, at * P:(at + z - a) * P], P ** -0.5,
                                                      flat(mw[w][:, a:z, :]), ALU.mult, ALU.mult)
                    last.then_inc(S["ml_sw"], 1)
                dve.wait_ge(S["ml_den"], 2 * hd + 2)
                step(V.tensor_tensor(den, den, mlc[:, :, 2:4, hd].rearrange("p j w -> p w j"), ALU.max))
                step(V.reciprocal(rden, den))
                for j in range(NT):
                    step(V.tensor_scalar(mt_, bank(7, NT, P + 1)[:, j, 0:P], rden[:, 0, j:j + 1], None, ALU.mult))
                    last = V.scalar_tensor_tensor(y[:, j, hd * P:(hd + 1) * P], bank(5, NT, P + 1)[:, j, 0:P], rden[:, 1, j:j + 1],
                                                  mt_, ALU.mult, ALU.add)
                    if j == 0:
                        step(last)
                last.then_inc(S["ml_y"], 1)
            dve.wait_ge(S["ml_y"], NH)
            dve.wait_ge(S["silu_act"], 3)
            step(V.tensor_tensor(y[:, :, 0:GW], y[:, :, 0:GW], buf["mo"], ALU.mult))
            group_norm(0)
            dve.wait_ge(S["fn_pe"], 1)
            V.tensor_copy(fa[:, 1].rearrange("p g c n -> p (g c n)"), flat(ps[:, 6:8, :])).then_inc(S["fn_dve"], 1)
            dve.wait_ge(S["fn_pe"], 2)
            V.tensor_copy(y[:, 1, 2 * GW:3 * GW], ps[:, 5, :]).then_inc(S["fn_dve"], 1)
            dve.wait_ge(S["fn_act"], 2)
            dve.wait_ge(S["fn_dve"], 2)
            dve.wait_ge(S["y_done"], 1)
            group_norm(2)
            dve.wait_ge(S["proj_a"], G_IN)
            dve.wait_ge(S["proj_b"], G_IN)
            step(V.memset(hone, 1.0))
            for w, name in enumerate(("hff", "hfb")):
                f = flat(buf[name])
                dve.wait_ge(S["hp_act"], 4 * w + 3)
                step(V.scalar_tensor_tensor(flat(he[w]), f, 0.0, flat(htmp), ALU.min, ALU.subtract))
                V.tensor_tensor(flat(htmp), flat(he[w]), f, ALU.subtract).then_inc(S["hp_dve"], 1)
                for c in range(NH):
                    o_, i_ = hb[w][:, c, :], he[w][:, c, :]
                    if w == 1:
                        o_, i_ = o_[:, ::-1], i_[:, ::-1]
                    last = V.tensor_tensor_scan(o_, hone, i_, 0.0, ALU.mult, ALU.add)
                step(last)
            dve.wait_ge(S["hp_act"], 8)
            V.tensor_tensor(flat(hqk[1]), flat(buf["hff"]), flat(buf["hfb"]), ALU.add).then_inc(S["hp_dve"], 1)

            def halves(x, half):
                vv = flat(x).rearrange("p (b u t) -> p b u t", u=2, t=half)
                return vv[:, :, 0, :], vv[:, :, 1, :]

            def decay(s):
                w, half = s // HG_LEVELS, 1 << (s % HG_LEVELS)
                if s >= 2:
                    dve.wait_ge(S["h_mulk"], s - 1)
                    dve.wait_ge(S["h_mulq"], s - 1)
                (e0_, e1_), (b0_, b1_) = halves(he[s % 2], half), halves(hb[w], half)
                mid = (b0_[:, :, half - 1:half] if w == 0 else b1_[:, :, 0:1]).to_broadcast(list(b0_.shape))
                if w == 0:
                    V.tensor_tensor(e0_, mid, b0_, ALU.subtract)
                    V.tensor_tensor(e1_, b1_, mid, ALU.subtract).then_inc(S["h_sub"], 1)
                else:
                    V.tensor_tensor(e0_, b0_, mid, ALU.subtract)
                    V.tensor_tensor(e1_, mid, b1_, ALU.subtract).then_inc(S["h_sub"], 1)

            def queries(s):
                w, half = s // HG_LEVELS, 1 << (s % HG_LEVELS)
                dve.wait_ge(S["h_exp"], s + 1)
                if s >= 1:
                    dve.wait_ge(S["h_pe"], s)
                u = 1 if w == 0 else 0
                V.tensor_tensor(halves(hqk[s % 2], half)[u], halves(he[s % 2], half)[u], halves(buf["hq"], half)[u],
                                ALU.mult).then_inc(S["h_mulq"], 1)

            def scores(s):
                w, lev = s // HG_LEVELS, s % HG_LEVELS
                dve.wait_ge(S["h_pe"], s + 2)
                dve.wait_ge(S["h_cp"], s + 1)
                b0 = 6 - 2 * (s % 2)
                if lev == HG_LEVELS - 1:
                    o_ = decay_to[:, w, :, P:2 * P] if w == 0 else decay_to[:, w, :, 0:P]
                    V.tensor_copy(o_, bank(b0, NH, P)).then_inc(S["h_cp"], 1)
                else:
                    for u in range(NT):
                        last = V.copy_predicated(decay_to[:, u, :, u * P:(u + 1) * P], bc_mid(hmask[:, w, lev, :], NH), bank(b0 + u, NH, P))
                    last.then_inc(S["h_cp"], 1)

            dve.wait_ge(S["silu_act"], 4)
            decay(0)
            dve.wait_ge(S["h_pe"], 1)
            for u in range(NT):
                last = V.tensor_copy(decay_to[:, u, :, u * P:(u + 1) * P], bank(4 + u, NH, P))
            last.then_inc(S["h_cp"], 1)
            for s in range(2 * HG_LEVELS):
                if s + 1 < 2 * HG_LEVELS:
                    decay(s + 1)
                queries(s)
                if s >= 1:
                    scores(s - 1)
                if s >= 4 and s % 4 == 0:
                    g = G_WK + s // 4 - 1
                    dense_out(g, flat(kT[:, 4 * (g - G_WK) + 2:4 * (g - G_WK) + 4, :]))
            scores(2 * HG_LEVELS - 1)
            dense_out(G_WK + 3, flat(kT[:, 14:16, :]))
            dve.wait_ge(S["h_o"], 1)
            V.tensor_copy(y[:, 1, GW:2 * GW], ps[:, 5, :]).then_inc(S["h_oev"], 1)
            dve.wait_ge(S["h_oev"], 2)
            dve.wait_ge(S["y_done"], 2)
            yh = y[:, :, GW:2 * GW]
            sq = arena(128, NT, GW)
            step(V.tensor_tensor(sq, yh, yh, ALU.mult))
            step(V.tensor_reduce(st[:, 0:NT * NH], sq.rearrange("p j (h d) -> p (j h) d", h=NH), AX.X, ALU.add))
            rsqrt(NT * NH, 1.0 / P)
            for j in range(NT):
                yj = yh[:, j, :].rearrange("p (h d) -> p h d", h=NH)
                last = V.tensor_tensor(yj, yj, bc_last(st[:, 24 + NH * j:24 + NH * (j + 1)], P), ALU.mult)
            step(last)
            dve.wait_ge(S["silu_act"], 5)
            step(V.tensor_tensor(yh, yh, buf["hg"], ALU.mult))
            group_norm(1)
            for m in range(NA_H // 2 * NT):
                i, j = m // NT, m % NT
                dve.wait_ge(S["na_s"], m + 1)
                if m >= 1:
                    dve.wait_ge(S["na_p"], 2 * m)
                grid = lambda x: x.rearrange("p u (a w) -> p u a w", w=GRID_W)
                V.tensor_tensor(grid(ns), grid(ps[:, 4::3, 0:T]), win.unsqueeze(1).unsqueeze(1).to_broadcast([P, 2, 4, GRID_W]),
                                ALU.add).then_inc(S["na_m"], 1)
                dve.wait_ge(S["na_m"], m + 1)
                step(V.tensor_reduce(st[:, 52:54], ns, AX.X, ALU.max))
                V.tensor_scalar(st[:, 52:54], st[:, 52:54], -1.0, None, ALU.mult).then_inc(S["na_max"], 1)
                dve.wait_ge(S["na_p"], 2 * m + 2)
                V.reciprocal(st[:, 44:46], st[:, 54:56]).then_inc(S["na_r"], 1)
                dve.wait_ge(S["na_r"], m + 1)
                dve.wait_ge(S["na_o"], m + 1)
                for u in range(2):
                    c0 = 3 * GW + (2 * i + u) * NA_D
                    V.tensor_scalar(y[:, j, c0:c0 + NA_D], bank(6, 2, NA_D)[:, u, :], st[:, 44 + u:45 + u], None, ALU.mult).then_inc(S["na_y"], 1)
                if m % 2 == 1:
                    dense_out(G_WV + m // 2, v[:, 1, GW * (m // 2):GW * (m // 2 + 1)])
            dve.wait_ge(S["na_y"], 16)
            dve.wait_ge(S["y_done"], 3)
            group_norm(3)
            turned(2, memT, 4)
            for n in range(4):
                dense_add(G_WO + n, n)
            row_scale()
            turned(3, xT, 1)
            for g in range(G_WQ, G_WQ + 4):
                n = 4 * (g - G_WQ) + 2
                dense_out(g, flat(qT[:, n:n + 2, :]))
            for hd in range(XA_H):
                dve.wait_ge(S["xs_pe"], hd + 1)
                if hd >= 1:
                    dve.wait_ge(S["xs_p"], 2 * hd)
                step(V.tensor_reduce(st[:, 52:54], bank(4, NT, T), AX.X, ALU.max))
                V.tensor_scalar(st[:, 52:54], st[:, 52:54], -(XA_D ** -0.5), None, ALU.mult).then_inc(S["xs_max"], 1)
                dve.wait_ge(S["xs_p"], 2 * hd + 2)
                step(V.reciprocal(st[:, 44:46], st[:, 54:56]))
                if hd >= 1:
                    dve.wait_ge(S["xs_t"], hd)
                for j in range(NT):
                    last = V.tensor_scalar(diag[:, j, :], ident[:], st[:, 44 + j:45 + j], None, ALU.mult)
                last.then_inc(S["xs_diag"], 1)
                dve.wait_ge(S["xs_o"], hd + 1)
                V.tensor_copy(flat(oT[:, 4 * hd + 2:4 * hd + 4, :]), ps[:, 7, :]).then_inc(S["xs_od"], 1)
            for n in range(4):
                dense_add(G_XO + n, n)
            row_scale()
            V.tensor_copy(st[:, 40:42], st[:, 24:26])
            turned(4, xT, 2)
            dve.wait_ge(S["r_pe"], 1)
            dve.wait_ge(S["route_in"], 16)
            V.memset(lgrp, LOWEST)
            step(V.tensor_copy(logit, bank(4, NT, 36)))
            step(V.tensor_copy(lgrp[:, :, 0:NG], logit[:, :, 0:NG]))
            for j in range(NT):
                last = V.max(gmax8[:, j, :], lgrp[:, j, :])
            step(last)
            for j in range(NT):
                V.max_index(gidx8[:, j, :], gmax8[:, j, :], lgrp[:, j, :])
            V.tensor_scalar(negm, gmax8[:, :, 0], -1.0, None, ALU.mult).then_inc(S["r_dve"], 1)
            dve.wait_ge(S["r_dve"], 1)
            step(V.tensor_copy(egrp, gidx8[:, :, 0]))
            for j in range(NT):
                last = V.tensor_scalar(goh4[:, j, :], iota[:, 0:NG], egrp[:, j:j + 1], None, ALU.is_equal)
            step(last)
            for g in range(NG):
                for j in range(NT):
                    src = logit[:, j, NG + PG * g:NG + PG * (g + 1)]
                    if g == 0:
                        last = V.tensor_scalar(fine[:, j, :], src, goh4[:, j, g:g + 1], None, ALU.mult)
                    else:
                        last = V.scalar_tensor_tensor(fine[:, j, :], src, goh4[:, j, g:g + 1], fine[:, j, :], ALU.mult, ALU.add)
                step(last)
            for j in range(NT):
                last = V.max(fmax8[:, j, :], fine[:, j, :])
            step(last)
            for j in range(NT):
                last = V.max_index(fidx8[:, j, :], fmax8[:, j, :], fine[:, j, :])
            step(last)
            V.tensor_copy(e0, fidx8[:, :, 0])
            step(V.tensor_copy(e1, fidx8[:, :, 1]))
            V.tensor_tensor(vdif, fmax8[:, :, 1], fmax8[:, :, 0], ALU.subtract).then_inc(S["r_dve"], 1)
            V.scalar_tensor_tensor(e0, egrp, float(PG), e0, ALU.mult, ALU.add)
            step(V.scalar_tensor_tensor(e1, egrp, float(PG), e1, ALU.mult, ALU.add))
            for j in range(NT):
                V.tensor_scalar(hit0[:, j, :], iota[:, 0:NE], e0[:, j:j + 1], None, ALU.is_equal)
                last = V.tensor_scalar(hit1[:, j, :], iota[:, 0:NE], e1[:, j:j + 1], None, ALU.is_equal)
            step(last)
            step(V.tensor_tensor(hit, hit0, hit1, ALU.add))
            V.tensor_tensor(hits, hit[:, 0, :], hit[:, 1, :], ALU.add).then_inc(S["r_dve"], 1)
            dve.wait_ge(S["r_act"], 1)
            V.reciprocal(ggate, gsum)
            step(V.tensor_scalar(w0, vdif, 1.0, None, ALU.add))
            step(V.reciprocal(w0, w0))
            step(V.tensor_tensor(w0, w0, ggate, ALU.mult))
            step(V.tensor_tensor(w1, vdif, w0, ALU.mult))
            dve.wait_ge(S["r_pe"], 2)
            step(V.tensor_copy(flat(rank), ps[:, 5, 0:3 * NE]))
            count = rank[:, 2, :]
            one32 = ones[:, 0:NE]
            step(V.tensor_scalar(n_first, count, float(EB), None, ALU.min))
            V.tensor_tensor(n_over, count, n_first, ALU.subtract)
            step(V.tensor_tensor_scan(st_first, one32, n_first, 0.0, ALU.mult, ALU.add))
            step(V.tensor_tensor_scan(st_over, one32, n_over, st_first[:, NE - 1:NE], ALU.mult, ALU.add))
            V.tensor_tensor(st_first, st_first, n_first, ALU.subtract)
            step(V.tensor_tensor(st_over, st_over, n_over, ALU.subtract))
            step(V.scalar_tensor_tensor(st_gap, st_over, float(-EB), st_first, ALU.add, ALU.subtract))
            step(V.tensor_scalar(blocks, n_over, 0.0, None, ALU.is_gt))
            for k in range(1, OVK):
                step(V.tensor_scalar(rtmp, n_over, float(k * EB), None, ALU.is_gt))
                step(V.tensor_tensor(blocks, blocks, rtmp, ALU.add))
            step(V.tensor_tensor_scan(blk_in, one32, blocks, 0.0, ALU.mult, ALU.add))
            step(V.tensor_scalar(rtmp, blk_in, iotap, None, ALU.is_le))
            step(V.tensor_reduce(eid, rtmp, AX.X, ALU.add))
            step(V.tensor_scalar(eid, eid, float(NE - 1), None, ALU.min))
            step(V.tensor_tensor(blocks, blk_in, blocks, ALU.subtract))
            step(V.scalar_tensor_tensor(blocks, blocks, float(-EB), st_over, ALU.mult, ALU.add))
            step(V.tensor_scalar(rtmp, iota[:, 0:NE], eid, None, ALU.is_equal))
            step(V.tensor_tensor(rtmp, rtmp, blocks, ALU.mult))
            step(V.tensor_reduce(ost, rtmp, AX.X, ALU.add))
            step(V.scalar_tensor_tensor(ost, iotap, float(EB), ost, ALU.mult, ALU.add))
            V.tensor_scalar(ost, ost, float(SLOTS), None, ALU.min).then_inc(S["r_dve"], 1)
            for j in range(NT):
                rj = rank[:, j, :]
                step(V.scalar_tensor_tensor(rtmp, rj, float(EB), st_gap, ALU.is_ge, ALU.mult))
                step(V.tensor_tensor(rtmp, rtmp, rj, ALU.add))
                step(V.tensor_tensor(rj, rtmp, st_first, ALU.add))
            slot = rank[:, 0:NT, :]
            step(V.tensor_tensor(hit0, hit0, slot, ALU.mult))
            step(V.tensor_reduce(slot0, hit0, AX.X, ALU.add))
            step(V.tensor_tensor(hit1, hit1, slot, ALU.mult))
            step(V.tensor_reduce(slot1, hit1, AX.X, ALU.add))
            for j in range(NT):
                for sel, a0, a1 in ((sel_r, st[:, 40 + j:41 + j], st[:, 40 + j:41 + j]), (sel_g, w0[:, j:j + 1], w1[:, j:j + 1])):
                    V.tensor_scalar(sel[:, j, :], iota, slot0[:, j:j + 1], a0, ALU.is_equal, ALU.mult)
                    step(V.tensor_scalar(sel_t, iota, slot1[:, j:j + 1], a1, ALU.is_equal, ALU.mult))
                    last = V.tensor_tensor(sel[:, j, :], sel[:, j, :], sel_t, ALU.add)
                    if not (j == 1 and sel is sel_g):
                        step(last)
            last.then_inc(S["tab_dve"], 1)
            dve.wait_ge(S["r_pe"], 3)
            V.tensor_copy(table[0:1, 0:NE], st_first[0:1, :])
            V.tensor_copy(table[0:1, 32:64], ps[0:1, 6, 0:32])
            V.tensor_copy(table[0:1, 64:96], ps[0:1, 6, P:P + 32])
            V.tensor_copy(table[0:1, 96:97], blk_in[0:1, NE - 1:NE]).then_inc(S["tab_dve"], 1)
            for k in range(1, KT, 2):
                dve.wait_ge(S["g_pe"], k + 1)
                V.tensor_scalar(xsT[:, k, 0:SLOTS], ps[:, 4 + k % 4, :], cols[:, 2 * KT + k:2 * KT + k + 1], None, ALU.mult).then_inc(S["g_dve"], 1)
            V.memset(xsT[:, :, SLOTS:], 0.0).then_inc(S["g_dve"], 1)
            def start_of(n):
                at = n if isinstance(n, int) else bass.ds(n, 1)
                return dve.value_load(table[0:1, at:at + 1] if isinstance(n, int) else table[0:1, at], min_val=0, max_val=SLOTS)

            def tokens_lo(n, s):
                dve.wait_ge(S["xe_hi"], n + 1)
                V.tensor_tensor(xe_lo[:], xsT[:, :, bass.ds(s, EB)], xe_hi[:].bitcast(F32), ALU.subtract).then_inc(S["xe_lo"], 1)

            def weights_lo(n, part):
                for i in part:
                    r = i % RING_E
                    dve.wait_ge(S["up_hi"], n * UCH + (i + 1))
                    V.tensor_tensor(up_lo[r][:], ring_up[r], up_hi[r][:].bitcast(F32), ALU.subtract).then_inc(S["up_lo"], 1)

            def gating(n):
                dve.wait_ge(S["up_used"], n * UCH + UCH)
                dve.wait_ge(S["e_sg"], n + 1)
                V.tensor_tensor(sg, ps[0:EB, 1, :], sg, ALU.mult).then_inc(S["e_h"], 1)

            def hidden(n):
                dve.wait_ge(S["e_turn"], n + 1)
                V.tensor_copy(hT, bank(6, FF // P, P)[:, :, 0:EW]).then_inc(S["e_hT"], 1)

            def outputs(n, s):
                for i in (2, 3):
                    dve.wait_ge(S["dn_used"], n * DCH + (i + 1))
                    V.tensor_copy(ysT[:, CH * i:CH * (i + 1), bass.ds(s, EB)], bank(2 + i, CH, EW)[:, :, 0:EB]).then_inc(S["e_yd"], 1)

            def block_n(n, back, back2):
                weights_lo(n, range(0, 1))
                if back is not None:
                    gating(back)
                tokens_lo(n, start_of(n))
                weights_lo(n, range(1, 2))
                if back is not None:
                    hidden(back)
                weights_lo(n, range(2, 3))
                if back2 is not None:
                    outputs(back2, start_of(back2))
                weights_lo(n, range(3, 5))
                if back2 is not None:
                    dve.wait_ge(S["e_yd"], n * 2 - 2)
                weights_lo(n, range(5, UCH))

            dve.wait_ge(S["tab_dve"], 2)
            block_n(0, None, None)
            block_n(1, 0, None)
            with dve.Fori(2, NE) as e:
                block_n(e, e - 1, e - 2)
            gating(NE - 1)
            hidden(NE - 1)
            outputs(NE - 2, start_of(NE - 2))
            dve.wait_ge(S["e_yd"], 2 * NE - 2)
            outputs(NE - 1, start_of(NE - 1))
            nov = dve.value_load(table[0:1, 96:97], min_val=0, max_val=OVB)
            with dve.Fori(0, OVB) as b:
                with dve.If(b < nov):
                    n = b + NE
                    s = start_of(b + 64)
                    tokens_lo(n, s)
                    weights_lo(n, range(UCH))
                    gating(n)
                    hidden(n)
                    dve.wait_ge(S["e_yd"], n * 2)
                    outputs(n, s)
            dve.wait_ge(S["c_tp"], 1)
            V.tensor_copy(st[:, 61:62], ident[:, 0:1]).then_inc(S["c_dve"], 1)
            n = 0
            for s in range(SLOTS // P):
                for kk in range(4):
                    if n % 2 == 1:
                        dve.wait_ge(S["c_tp"], n + 2)
                        V.tensor_copy(ys[:, s, kk * 512:(kk + 1) * 512], ps[:, 4 + n % 4, :]).then_inc(S["c_dve"], 1)
                    n += 1
            for j in range(NT):
                for g in range(4):
                    m = 4 * j + g
                    hv = h[:, j, g * 512:(g + 1) * 512]
                    dve.wait_ge(S["c_pe"], m + 1)
                    V.tensor_tensor(hv, ps[:, m % 4, :], hv, ALU.add).then_inc(S["c_add"], 1)
            norms[0] += 1
            dve.wait_ge(S["sq_act"], norms[0])
            rsqrt(NT, 1.0 / D)
            dve.wait_ge(S["fgain_in"], 16)
            for j in range(NT):
                V.scalar_tensor_tensor(res[:, j, :], h[:, j, :], st[:, 24 + j:25 + j], fgain, ALU.mult, ALU.mult).then_inc(S["fin_dve"], 1)


INS = ["x", "mem", "norm_mix", "norm_cross", "norm_ffn", "norm_final", "norm_mem", "w_in", "mlstm_conv", "mlstm_gate_bias",
       "na_rpb", "group_gain", "w_out", "xa_wq", "xa_wk", "xa_wv", "xa_wo", "moe_router_group", "moe_router_expert",
       "moe_w1", "moe_w3", "moe_w2"]


def kernel(**inputs):
    import numpy as _np
    import concourse.bacc as _bacc
    from concourse import mybir as _mybir
    from concourse.bass_utils import run_bass_kernel_spmd as _run

    nc = _bacc.Bacc("TRN2", target_bir_lowering=False, num_devices=1)
    arrays, aps = {}, {}
    given = {n: inputs[n] for n in INS}
    given.update(constants())
    for name, a in given.items():
        a = _np.ascontiguousarray(a)
        arrays[f"in_{name}_dram"] = a
        aps[name] = nc.dram_tensor(f"in_{name}_dram", a.shape, _mybir.dt.from_np(a.dtype), kind="ExternalInput").ap()
    out = nc.dram_tensor("out_0_dram", (1, T, D), _mybir.dt.float32, kind="ExternalOutput").ap()
    program(nc, aps, out)
    r = _run(nc, [arrays], core_ids=[0])
    return r.results[0]["out_0_dram"]
```

```python
from contextlib import ExitStack

import numpy as np

import concourse.bass as bass
from concourse import mybir

ALU = mybir.AluOpType
ACT = mybir.ActivationFunctionType
AX = mybir.AxisListType
F32 = mybir.dt.float32
I32 = mybir.dt.int32
U32 = mybir.dt.uint32
U8 = mybir.dt.uint8
F32R = mybir.dt.float32r

P = 128
D = 2048
KT = D // P
T = 256
NT = T // P
GW = 512
NH = 4
CH = 4
NCH = KT // CH
RING_A = 4
FF = 512
NE = 32
NG = 4
PG = NE // NG
UCH = 8
DCH = 4
RING_E = 4
EB = 64
EW = 96
OVK = -(-(T - EB) // EB)
OVB = 2 * T // EB
SLOTS = 2 * T
EPS = 1e-6
GRID_W = 64
NA_H = 8
NA_D = 64
NA_KW = 16
RPB_R, RPB_C = 15, 31
XA_H = 4
XA_D = D // XA_H
NEG = -1.0e30
LOWEST = -3.0e38

W_IN = [
    ("mq", True, 0, 1.0), ("mk", True, 512, 1.0), ("mv", False, 1024, 1.0), ("mo", False, 1536, 1.0),
    ("hq", True, 2064, 1.0), ("hff", True, 2576, 1.0), ("hfb", True, 3088, 1.0), ("hi", False, 3600, 1.0),
    ("hg", False, 4112, 1.0), ("fu", True, 4624, 1.0), ("nq", True, 5136, NA_D ** -0.5), ("nk", True, 5648, 1.0),
    ("nv", False, 6160, 1.0),
]
G_COL = 2048
G_IN = len(W_IN)
G_WK, G_WV, G_WO, G_WQ, G_XO = G_IN, G_IN + 4, G_IN + 8, G_IN + 12, G_IN + 16

HG_LEVELS = 8
HG_LEAD = 3
G_ML = 7
NA_CHUNKS = [(3,), (4, 5), (6, 7), (8, 9), (10, 11), (12, 13), (14,), (15,)]
NA_OUT = {0: 0, 2: 1, 4: 2, 7: 3}


def constants():
    c = np.arange(P)
    ang = 2 * np.pi * np.outer(c, c) / P
    s = np.arange(T)
    angs = 2 * np.pi * np.outer(s, s) / T
    norm = 1.0 / np.sqrt(T * P)
    tok = lambda m: m.reshape(NT, P, T).transpose(1, 0, 2).reshape(P, NT * T)
    dft = np.concatenate([np.cos(ang), np.sin(ang), tok(np.cos(angs) * norm), tok(-np.sin(angs) * norm)], 1)
    flip = np.eye(P)[::-1]
    fwd = np.where(c[:, None] <= c[None, :], 0.0, NEG)
    bwd = np.where(c[:, None] >= c[None, :], 0.0, NEG)
    selh = np.zeros((P, NH, P))
    for h in range(NH):
        selh[h, h] = 1.0
    col = np.arange(GRID_W)
    start = np.clip(col - NA_KW // 2, 0, GRID_W - NA_KW)
    ok = (col[None] >= start[:, None]) & (col[None] < start[:, None] + NA_KW)
    win = np.tile(np.where(ok, 0.0, NEG), (NT, 1))
    mix = np.concatenate([flip, fwd, bwd, selh.reshape(P, -1), win], 1)
    masks = np.zeros((P, 2, HG_LEVELS - 1, P), np.float32)
    for lev in range(HG_LEVELS - 1):
        h = 1 << lev
        same = (c[:, None] // (2 * h)) == (c[None, :] // (2 * h))
        odd = (c // h) % 2
        masks[:, 0, lev] = same & (odd[:, None] == 0) & (odd[None, :] == 1)
        masks[:, 1, lev] = same & (odd[:, None] == 1) & (odd[None, :] == 0)
    before = (c[:, None] < c[None, :]) * 1.0
    route = np.concatenate([before, np.ones((P, P)), np.tile(np.arange(SLOTS), (P, 1)), c[:, None] * 1.0], 1)
    return {"c_dft": dft.astype(np.float32), "c_mix": mix.astype(np.float32),
            "c_eye": np.eye(P, dtype=np.float32),
            "c_masks": masks.reshape(P, -1), "c_route": route.astype(np.float32)}


class Arena:

    def __init__(self, tensor):
        self.t = tensor

    def __call__(self, kib, *shape, parts=P):
        a = int(round(kib * 256))
        n = int(np.prod(shape))
        v = self.t[0:parts, a:a + n]
        if len(shape) == 2:
            v = v.rearrange("p (a b) -> p a b", b=shape[1])
        if len(shape) == 3:
            v = v.rearrange("p (a b c) -> p a b c", b=shape[1], c=shape[2])
        if len(shape) == 4:
            v = v.rearrange("p (a b c d) -> p a b c d", b=shape[1], c=shape[2], d=shape[3])
        return v


def flat(v):
    if len(v.shape) == 3:
        return v.rearrange("p a b -> p (a b)")
    return v.rearrange("p a b c -> p (a b c)")


def bc_mid(v, n):
    return v.unsqueeze(1).to_broadcast([v.shape[0], n, v.shape[1]])


def bc_last(v, n):
    return v.unsqueeze(2).to_broadcast([v.shape[0], v.shape[1], n])


def program(nc, ins, out, dbg=None):
    dbg = dbg or {}
    with ExitStack() as ctx:
        def sb(name, shape, dt=F32):
            return ctx.enter_context(nc.sbuf_tensor(name, shape, dt))

        def sem(name):
            return ctx.enter_context(nc.semaphore(name))

        base = -(-nc.sbuf_base // 32) * 32
        arena = Arena(sb("arena", [P, 200 * 256]))

        def at_r(name, kib, shape):
            return nc.alloc_sbuf_tensor_at(name, shape, F32R, offset=base + int(kib * 1024))

        ident = sb("ident", [P, P])
        cols = sb("cols", [P, 104])
        table = sb("table", [1, 128], I32)
        diag = sb("diag", [P, NT, P])
        st = sb("stats", [P, 64])
        hmask = sb("hmask", [P, 2 * (HG_LEVELS - 1) * P], U8).rearrange("p (d l t) -> p d l t", d=2, t=P)
        ps = ctx.enter_context(nc.psum_tensor("ps", [P, 8, 512], F32))

        h = arena(0, NT, D)
        ring_a = [arena(16 + 8 * i, CH, 512) for i in range(RING_A)]
        w_lo = [at_r(f"w_lo{i}", 16 + 8 * i, [P, CH, 512]) for i in range(RING_A)]
        w_hi = [[at_r(f"w_hi{n}{i}", kib + 4 * i, [P, CH // 2, 512]) for i in range(4)] for n, kib in enumerate((0, 168))]
        split = {G_IN: (at_r("x_hi", 64, [P, KT, T]), at_r("x_lo", 48, [P, KT, T])),
                 G_WO: (at_r("y_hi", 136, [P, KT, T]), at_r("y_lo", 64, [P, KT, T])),
                 G_WQ: (at_r("q_hi", 152, [P, KT, T]), at_r("q_lo", 48, [P, KT, T])),
                 G_XO: (at_r("o_hi", 136, [P, KT, T]), at_r("o_lo", 64, [P, KT, T]))}
        xT = arena(48, KT, T)
        memT = arena(64, KT, T)
        mem = arena(80, NT, D)
        y = mem
        kT = arena(96, KT, T)
        v = arena(112, NT, D)
        buf = {}
        buf["q"], buf["k"] = arena(128, NH, T), arena(132, NH, T)
        buf["mv"] = arena(136, NT, NH, P + 1)
        o = 140.25
        for n in ("mo", "hq", "hff", "hfb", "hi", "hg", "fu", "nq", "nk", "nv"):
            a_form = n in ("mo", "hi", "hg", "nv")
            buf[n] = arena(o, NT, GW) if a_form else arena(o, NH, T)
            o += 4
        buf["mq"], buf["mk"] = arena(112, NH, T), arena(116, NH, T)
        decay_to = arena(180.25, NT, NH, T)
        hmask_f = arena(180.25, 2 * (HG_LEVELS - 1) * P)
        dft_c = arena(188.25, 2 * P)
        dft_t = arena(189.25, 2, NT, T)
        mixc = arena(193.25, 7 * P + GRID_W)
        flipm, tri = mixc[:, 0:P], [mixc[:, P:2 * P], mixc[:, 2 * P:3 * P]]
        selh = mixc[0:NH, 3 * P:7 * P].rearrange("p (h t) -> p h t", h=NH)
        win = mixc[:, 7 * P:]
        wg = arena(197, KT, 16)
        rows = arena(198, P)
        gt = arena(120, NH, T, parts=NH)
        gl = arena(124, 2, T, parts=NH)
        lf = arena(126, 2, T, parts=NH)
        gb = arena(96, 2, T, parts=NH)
        gr = arena(98, NH, T, parts=NH)
        gm = arena(102, 2, T, parts=NH)
        gone = arena(104, T)
        gtok = arena(105, NT, 16)
        gbias = st[0:NH, 56:60]
        mlc = arena(106, NT, 4, NH)
        mw = [arena(107, 3, P), arena(108.5, 3, P)]
        msw = [arena(110, 3, P), arena(120, 3, P)]
        marg = [arena(122, T), arena(123, T)]
        mt_ = arena(121.5, P)
        yml = arena(124, NT, GW)
        fa = arena(112, NT, NH, 2, P)
        hb = [arena(48, NH, T), arena(52, NH, T)]
        hqk = [arena(56, NH, T), arena(60, NH, T)]
        he = [arena(112, NH, T), arena(116, NH, T)]
        htmp = arena(120, NH, T)
        hone = arena(124, T)
        nbias = [arena(144.25, 2, T), arena(146.25, 2, T)]
        ns, npr, npt = arena(148.25, 2, T), arena(150.25, 2, T), arena(152.25, 2, NT, P)
        qT = arena(80, KT, T)
        xp = [arena(128 + 2 * i, NT, T) for i in range(XA_H)]
        xpt = [arena(192 + 2 * i, NT, T) for i in range(XA_H)]
        xsT = arena(16, KT, SLOTS + EB)
        ysT = arena(52, KT, SLOTS + EB)
        xe_hi, xe_lo = at_r("xe_hi", 88, [P, KT, EB]), at_r("xe_lo", 92, [P, KT, EB])
        selgT = arena(96, SLOTS // P, T)
        hT = arena(100, FF // P, EW)
        sg = arena(102, FF, parts=EB)
        sel_r, sel_g, sel_t = arena(64, NT, SLOTS), arena(68, NT, SLOTS), arena(78, SLOTS)
        wr = arena(101, KT, 36)
        rt = arena(72, 1024)
        routec = arena(80, 2 * P + SLOTS + 1)
        before, ones, iota, iotap = (routec[:, 0:P], routec[:, P:2 * P], routec[:, 2 * P:2 * P + SLOTS],
                                     routec[:, 2 * P + SLOTS:])
        r_at = [0]

        def small(*shape):
            a = r_at[0]
            r_at[0] += int(np.prod(shape))
            assert r_at[0] <= 1024
            vv = rt[:, a:r_at[0]]
            return vv.rearrange("p (a b) -> p a b", b=shape[1]) if len(shape) == 2 else vv

        logit, lgrp, gmax8, fine, fmax8 = small(NT, 36), small(NT, 8), small(NT, 8), small(NT, 8), small(NT, 8)
        gidx8, fidx8 = small(NT, 8).bitcast(U32), small(NT, 8).bitcast(U32)
        hit0, hit1, hit, rank = small(NT, NE), small(NT, NE), small(NT, NE), small(3, NE)
        hits, n_first, n_over, st_first, st_over, st_gap, blocks, blk_in, rtmp = [small(NE) for _ in range(9)]
        ftmp = small(NT, 8)
        egrp, gsum, ggate, vdif, w0, w1, e0, e1, slot0, slot1, negm, goh = [small(NT) for _ in range(12)]
        goh4 = small(NT, 4)
        eid, ost, gexp = small(1), small(1), small(4)
        ring_up = [arena(136 + 8 * i, CH, 512) for i in range(RING_E)]
        up_lo = [at_r(f"up_lo{i}", 136 + 8 * i, [P, CH, 512]) for i in range(RING_E)]
        up_hi = [at_r(f"up_hi{i}", 104 + 8 * i, [P, CH, 512]) for i in range(RING_E)]
        ring_dn = [arena(168 + 8 * i, CH, 512) for i in range(RING_E)]
        ys = arena(16, SLOTS // P, D)
        fgain = arena(136, D)
        res = arena(144, NT, D)

        def bank(b, *shape):
            w = int(np.prod(shape))
            vv = ps[:, b, 0:w]
            if len(shape) == 2:
                return vv.rearrange("p (a b) -> p a b", b=shape[1])
            if len(shape) == 3:
                return vv.rearrange("p (a b c) -> p a b c", b=shape[1], c=shape[2])
            return vv

        S = {}
        for n in ["x_in", "mem_in", "eye_in", "rows_in", "cmix_in", "cdft_in", "cmask_in", "wg_in", "gbias_in",
                  "bias_in0", "bias_in1", "route_in", "wr_in", "fgain_in", "out_done",
                  "chunk_used", "proj_a", "proj_b", "act_step", "dve_step", "pool_step",
                  "sq_act", "var_dve", "rs_act", "diag_dve", "tp_pe", "tp_act", "tp_dve", "ts_pe", "ts_hi", "ts_lo",
                  "w_hi", "w_lo", "cols_pe", "cols_act",
                  "conv_dve", "silu_act", "gate_pe", "gate_dve", "gate_act", "ml_pe_s", "ml_pe_m", "ml_arg",
                  "ml_w", "ml_sw", "ml_pv", "ml_den", "ml_y", "fn_pe", "fn_act", "fn_dve",
                  "hp_act", "hp_dve", "h_sub", "h_exp", "h_mulq", "h_mulk", "h_pe", "h_cp", "h_o", "h_oev",
                  "na_s", "na_m", "na_max", "na_p", "na_r", "na_t", "na_tev", "na_o", "na_y", "y_done",
                  "xs_pe", "xs_max", "xs_p", "xs_diag", "xs_t", "xs_tev", "xs_o", "xs_oa", "xs_od",
                  "r_pe", "r_dve", "r_act", "g_pe", "g_act", "g_dve", "sg_pe", "sg_act", "tab_dve",
                  "xe_hi", "xe_lo", "up_hi", "up_lo", "up_used", "dn_used", "e_sg", "e_h", "e_turn", "e_hT", "e_ya", "e_yd",
                  "c_tp", "c_act", "c_dve", "c_pe", "c_add", "fin_dve"]:
            S[n] = sem(n)
        s_ring = [sem(f"ring_a{i}") for i in range(RING_A)]
        s_up = [sem(f"ring_up{i}") for i in range(RING_E)]
        s_dn = [sem(f"ring_dn{i}") for i in range(RING_E)]
        block = ctx.enter_context(nc.Block())

        w_src = {G_WK: "xa_wk", G_WV: "xa_wv", G_WO: "w_out", G_WQ: "xa_wq", G_XO: "xa_wo"}
        g1, g3, g2 = ins["moe_w1"][0], ins["moe_w3"][0], ins["moe_w2"][0]

        def split_chunk(g, i):
            return (g * NCH + i, w_hi[0]) if g < G_IN else ((g - G_WO + G_IN) * NCH + i, w_hi[1])

        def dense_chunk(g, i):
            if g < G_IN:
                w, c0 = ins["w_in"][0], W_IN[g][2]
            else:
                base = G_IN + 4 * ((g - G_IN) // 4)
                w, c0 = ins[w_src[base]][0], 512 * (g - base)
            return w[i * CH * P:(i + 1) * CH * P, c0:c0 + 512].rearrange("(c p) n -> p c n", p=P)

        def of_expert(w, e):
            return w[e] if isinstance(e, int) else w[bass.ds(e, 1)].rearrange("a k n -> (a k) n")

        def up_chunk(e, i):
            w, q = of_expert((g1, g3)[i // 4], e), i % 4
            return w[q * CH * P:(q + 1) * CH * P, :].rearrange("(c p) n -> p c n", p=P)

        def down_chunk(e, i):
            return of_expert(g2, e)[:, i * 512:(i + 1) * 512].rearrange("(c p) n -> p c n", p=P)

        @block.sync
        def _(sp):
            sp.dma_start(ident[:], ins["c_eye"]).then_inc(S["eye_in"], 16)
            for n, name in enumerate(["norm_mix", "norm_cross", "norm_ffn", "norm_mem", "group_gain"]):
                src = ins[name] if name == "norm_mem" else ins[name][0]
                sp.dma_start(rows[n * KT:(n + 1) * KT, :], src.rearrange("(k p) -> k p", p=P)).then_inc(S["rows_in"], 16)
            sp.dma_start(rows[80:104, :], ins["mlstm_conv"][0].rearrange("t (c p) -> (t c) p", p=P)).then_inc(S["rows_in"], 16)
            sp.dma_start(h, ins["x"][0].rearrange("(j p) d -> p j d", p=P)).then_inc(S["x_in"], 16)
            sp.dma_start(mem, ins["mem"][0].rearrange("(j p) d -> p j d", p=P)).then_inc(S["mem_in"], 16)

            def load_dense(g):
                for i in range(NCH):
                    c = g * NCH + i
                    if c >= RING_A:
                        sp.wait_ge(S["chunk_used"], c - RING_A + 1)
                    sp.dma_start(ring_a[i], dense_chunk(g, i)).then_inc(s_ring[i], 16)

            for g in range(4):
                load_dense(g)
                if g == 0:
                    with nc.allow_non_contiguous_dma(reason="gate columns"):
                        sp.dma_start(wg, ins["w_in"][0][:, G_COL:G_COL + 16].rearrange("(c p) n -> p c n", p=P)).then_inc(S["wg_in"], 16)
                        sp.dma_start(gbias, ins["mlstm_gate_bias"][0].rearrange("(k h) -> h k", h=NH)).then_inc(S["gbias_in"], 16)
                    sp.dma_start(mixc, ins["c_mix"]).then_inc(S["cmix_in"], 16)
                    sp.dma_start(arena(188.25, 5 * 256), ins["c_dft"]).then_inc(S["cdft_in"], 16)
                    sp.dma_start(hmask_f, ins["c_masks"]).then_inc(S["cmask_in"], 16)
            for g in range(4, G_WO):
                load_dense(g)

            def load_up(e, n, i):
                if not (isinstance(n, int) and n == 0 and i < RING_E):
                    sp.wait_ge(S["up_used"], n * UCH + (i + 1 - RING_E))
                sp.dma_start(ring_up[i % RING_E], up_chunk(e, i)).then_inc(s_up[i % RING_E], 16)

            def load_down(e, n, i):
                if not (isinstance(n, int) and n == 0):
                    sp.wait_ge(S["dn_used"], n * DCH + (i + 1 - RING_E))
                sp.dma_start(ring_dn[i], down_chunk(e, i)).then_inc(s_dn[i], 16)

            sp.wait_ge(S["chunk_used"], G_IN * NCH)
            sp.dma_start(h, ins["x"][0].rearrange("(j p) d -> p j d", p=P)).then_inc(S["x_in"], 16)
            for g in range(G_WO, G_XO + 4):
                load_dense(g)
            sp.wait_ge(S["xs_o"], XA_H)
            with nc.allow_non_contiguous_dma(reason="router columns"):
                sp.dma_start(wr[:, :, 0:NG], ins["moe_router_group"][0].rearrange("(c p) n -> p c n", p=P)).then_inc(S["wr_in"], 16)
                sp.dma_start(wr[:, :, NG:], ins["moe_router_expert"][0].rearrange("(c p) n -> p c n", p=P)).then_inc(S["wr_in"], 16)
            sp.dma_start(routec, ins["c_route"]).then_inc(S["route_in"], 16)
            sp.wait_ge(S["chunk_used"], (G_XO + 4) * NCH)
            for i in range(RING_E):
                load_up(0, 0, i)
            for i in range(DCH):
                load_down(0, 0, i)
            for i in range(RING_E, UCH):
                load_up(0, 0, i)
            for i in range(UCH):
                load_up(1, 1, i)
            with sp.Fori(2, NE) as e:
                for i in range(UCH):
                    load_up(e, e, i)
                    if i % 2 == 1:
                        load_down(e - 1, e - 1, i // 2)
            for i in range(DCH):
                load_down(NE - 1, NE - 1, i)
            sp.wait_ge(S["tab_dve"], 3)
            nov = sp.value_load(table[0:1, 96:97], min_val=0, max_val=OVB)
            with sp.Fori(0, OVB) as b:
                with sp.If(b < nov):
                    e = sp.value_load(table[0:1, bass.ds(b + 32, 1)], min_val=0, max_val=NE - 1)
                    for i in range(UCH):
                        load_up(e, b + NE, i)
                    for i in range(DCH):
                        load_down(e, b + NE, i)
            sp.wait_ge(S["c_tp"], 1)
            sp.dma_start(fgain, ins["norm_final"].rearrange("(a d) -> a d", a=1).to_broadcast([P, D])).then_inc(S["fgain_in"], 16)
            for j in range(NT):
                sp.wait_ge(S["fin_dve"], j + 1)
                sp.dma_start(out[0, j * P:(j + 1) * P, :], res[:, j, :]).then_inc(S["out_done"], 16)
            sp.wait_ge(S["out_done"], 16 * NT)

        @block.gpsimd
        def _(pool):
            nc.gpsimd.memset(gone, 1.0).then_inc(S["pool_step"], 1)
            nc.gpsimd.memset(buf["mv"][:, :, :, P:P + 1], 1.0).then_inc(S["pool_step"], 1)
            for s in range(2 * HG_LEVELS):
                w, half = s // HG_LEVELS, 1 << (s % HG_LEVELS)
                u = 0 if w == 0 else 1
                cut = lambda x: flat(x).rearrange("p (b u t) -> p b u t", u=2, t=half)[:, :, u, :]
                pool.wait_ge(S["h_exp"], s + 1)
                if s >= 1:
                    pool.wait_ge(S["h_pe"], s)
                nc.gpsimd.tensor_tensor(cut(hqk[s % 2]), cut(he[s % 2]), cut(buf["hff" if w == 0 else "hfb"]),
                                        ALU.mult).then_inc(S["h_mulk"], 1)
            rpb = ins["na_rpb"]
            for m in range(NA_H // 2 * NT):
                i, j = m // NT, m % NT
                if m == 0:
                    pool.wait_ge(S["h_pe"], 2 * HG_LEVELS + 1)
                    pool.wait_ge(S["h_mulk"], 2 * HG_LEVELS)
                    pool.wait_ge(S["h_mulq"], 2 * HG_LEVELS)
                if m >= 2:
                    pool.wait_ge(S["na_s"], m - 1)
                for g in range(2):
                    r = 2 * j + 1 - g
                    for u in range(2):
                        hd = 2 * i + u
                        src = bass.AP(tensor=rpb.tensor, offset=rpb.offset + hd * RPB_R * RPB_C + (7 - r) * RPB_C - 48,
                                      ap=[[1, GRID_W], [RPB_C, 4], [1, GRID_W]])
                        pool.dma_start(nbias[m % 2][g * 64:(g + 1) * 64, u, :].rearrange("p (a w) -> p a w", w=GRID_W),
                                       src).then_inc(S["bias_in0" if m % 2 == 0 else "bias_in1"], 16)

        @block.tensor
        def _(pe):
            mm = nc.tensor.matmul

            def turn(n, src, scales, part=range(KT // 2)):
                for kk in part:
                    q = n * (KT // 2) + kk
                    if q >= 4:
                        pe.wait_ge(S["tp_act" if q % 2 == 0 else "tp_dve"], (q - 4) // 2 + 1)
                    o_ = bank(4 + kk % 4, 2, NT, P)
                    for u in range(2):
                        for j in range(NT):
                            k = 2 * kk + u
                            last = mm(o_[:, u, j, :], src[:, j, k * P:(k + 1) * P], scales[j], start=True, stop=True)
                    last.then_inc(S["tp_pe"], 1)

            def turn_split(n, src, scales, part=range(KT // 2)):
                for kk in part:
                    q = n * (KT // 2) + kk
                    if kk >= 4:
                        pe.wait_ge(S["ts_hi"], q - 3)
                        pe.wait_ge(S["ts_lo"], q - 3)
                    o_ = bank(4 + kk % 4, 2, NT, P)
                    for u in range(2):
                        for j in range(NT):
                            k = 2 * kk + u
                            last = mm(o_[:, u, j, :], src[:, j, k * P:(k + 1) * P], scales[j], start=True, stop=True)
                    last.then_inc(S["ts_pe"], 1)

            def turned_split(n):
                pe.wait_ge(S["ts_hi"], (n + 1) * (KT // 2))
                pe.wait_ge(S["ts_lo"], (n + 1) * (KT // 2))

            def group_turned(g0, n, turn_, at):
                pe.wait_ge(S["proj_a"], g0 + n + 1)
                pe.wait_ge(S["proj_b"], g0 + n + 1)
                turn_(at, h, [ident[:]] * 2, part=(2 * n, 2 * n + 1))

            def dense_split(g, feature_major, act, part=range(NCH)):
                b0 = 2 * (g % 2)
                a_hi, a_lo = act
                for i in part:
                    if i == 0 and g >= 2:
                        pe.wait_ge(S["proj_a"], g - 1)
                        pe.wait_ge(S["proj_b"], g - 1)
                    n_split, hi_ring = split_chunk(g, i)
                    for c in range(CH):
                        k, half = i * CH + c, 2 * n_split + c // 2
                        if c % 2 == 0:
                            pe.wait_ge(S["w_lo"], half + 1)
                        hi, lo = hi_ring[half % 4][:, c % 2, :], w_lo[i][:, c, :]
                        if feature_major:
                            for n in range(4):
                                o_ = ps[:, b0 + n // 2, (n % 2) * T:(n % 2 + 1) * T]
                                cut = slice(n * P, (n + 1) * P)
                                mm(o_, hi[:, cut], a_hi[:, k, :], start=(k == 0 and n % 2 == 0), stop=False, skip_group_check=True)
                                mm(o_, hi[:, cut], a_lo[:, k, :], start=False, stop=False, skip_group_check=True)
                                last = mm(o_, lo[:, cut], a_hi[:, k, :], start=False, stop=(k == KT - 1), skip_group_check=True)
                        else:
                            for j in range(NT):
                                o_, rows_ = ps[:, b0 + j, :], slice(j * P, (j + 1) * P)
                                mm(o_, a_hi[:, k, rows_], hi, start=(k == 0), stop=False)
                                mm(o_, a_hi[:, k, rows_], lo, start=False, stop=False)
                                last = mm(o_, a_lo[:, k, rows_], hi, start=False, stop=(k == KT - 1))
                    last.then_inc(S["chunk_used"], 1)

            def dense(g, feature_major, act, part=range(NCH)):
                b0 = 2 * (g % 2)
                for i in part:
                    if i == 0 and g >= 2:
                        pe.wait_ge(S["proj_a"], g - 1)
                        pe.wait_ge(S["proj_b"], g - 1)
                    pe.wait_ge(s_ring[i], 16 * (g + 1))
                    for c in range(CH):
                        k = i * CH + c
                        if feature_major:
                            for n in range(4):
                                last = mm(ps[:, b0 + n // 2, (n % 2) * T:(n % 2 + 1) * T], ring_a[i][:, c, n * P:(n + 1) * P],
                                          act[:, k, :], start=(k == 0 and n % 2 == 0), stop=(k == KT - 1),
                                          skip_group_check=True)
                        else:
                            for j in range(NT):
                                last = mm(ps[:, b0 + j, :], act[:, k, j * P:(j + 1) * P], ring_a[i][:, c, :],
                                          start=(k == 0), stop=(k == KT - 1))
                    last.then_inc(S["chunk_used"], 1)

            pe.wait_ge(S["eye_in"], 16)
            pe.wait_ge(S["rows_in"], 16 * 6)
            mm(ps[:, 0, 0:104], rows[0:104, :], ident[0:104, 0:104], start=True, stop=True).then_inc(S["cols_pe"], 1)
            pe.wait_ge(S["x_in"], 16)
            pe.wait_ge(S["diag_dve"], 1)
            turn_split(0, h, [diag[:, j, :] for j in range(NT)])
            turned_split(0)
            q, k_ml = buf["q"], buf["k"]

            def ml_gates():
                pe.wait_ge(S["gate_dve"], 3)
                pe.wait_ge(S["gate_act"], 2)
                for j in range(NT):
                    for kind in range(4):
                        last = mm(bank(4, NT, 4, NH)[:, j, kind, :], gr[:, kind, j * P:(j + 1) * P], ident[0:NH, 0:NH],
                                  start=True, stop=True)
                last.then_inc(S["gate_pe"], 1)
                pe.wait_ge(S["cmix_in"], 16)
                pe.wait_ge(S["silu_act"], 2)
                pe.wait_ge(S["pool_step"], 2)
                pe.wait_ge(S["proj_a"], 3)
                pe.wait_ge(S["proj_b"], 3)
                pe.wait_ge(S["gate_dve"], 4)

            def ml_scores(hd):
                if hd >= 1:
                    pe.wait_ge(S["ml_sw"], 2 * hd)
                    pe.wait_ge(S["ml_w"], 2 * hd)
                for u in range(NT):
                    last = mm(bank(4, NT, T)[:, u, :], k_ml[:, hd, u * P:(u + 1) * P], q[:, hd, :], start=True, stop=True)
                last.then_inc(S["ml_pe_s"], 1)
                for w in range(2):
                    last = mm(bank(6, 2, T)[:, w, :], selh[:, hd, :], gm[:, w, :], start=True, stop=True)
                last.then_inc(S["ml_pe_m"], 1)

            def ml_values(hd):
                for w in range(2):
                    pe.wait_ge(S["ml_sw"], 2 * hd + w + 1)
                    if hd >= 1:
                        pe.wait_ge(S["ml_y"], hd)
                        pe.wait_ge(S["ml_den"], 2 * hd)
                    o_ = bank(7 if w == 0 else 5, NT, P + 1)
                    parts = [(0, 0, 0, True, True), (1, 1, 0, True, False), (1, 2, 1, False, True)] if w == 0 else \
                            [(0, 0, 0, True, False), (0, 1, 1, False, True), (1, 2, 1, True, True)]
                    for j, tile, u, a, z in parts:
                        last = mm(o_[:, j, :], msw[w][:, tile, :], buf["mv"][:, u, hd, :], start=a, stop=z)
                    last.then_inc(S["ml_pv"], 1)

            pe.wait_ge(S["cols_act"], 1)
            for g, (name, fm, _, _) in enumerate(W_IN):
                dense_split(g, fm, split[G_IN])
                if g == 3:
                    pe.wait_ge(S["wg_in"], 16)
                    for j in range(NT):
                        for k in range(KT):
                            for n, part in enumerate(split[G_IN]):
                                last = mm(bank(4, NT, 16)[:, j, :], part[:, k, j * P:(j + 1) * P].bitcast(F32), wg[:, k, :],
                                          start=(k == 0 and n == 0), stop=(k == KT - 1 and n == 1))
                    last.then_inc(S["gate_pe"], 1)
                    pe.wait_ge(S["gate_dve"], 1)
                    for kind in range(4):
                        for j in range(NT):
                            last = mm(ps[0:NH, 5 + kind // 2, (kind % 2) * T + j * P:(kind % 2) * T + (j + 1) * P],
                                      gtok[:, j, kind * NH:(kind + 1) * NH], ident[:], start=True, stop=True)
                    last.then_inc(S["gate_pe"], 1)
                if g == G_ML - 1:
                    ml_gates()
                if G_ML <= g < G_ML + NH:
                    ml_values(g - G_ML)
                if G_ML - 1 <= g < G_ML - 1 + NH:
                    ml_scores(g - G_ML + 1)
            pe.wait_ge(S["cdft_in"], 16)
            pe.wait_ge(S["proj_a"], G_IN)
            pe.wait_ge(S["proj_b"], G_IN)
            pe.wait_ge(S["ml_y"], NH)
            pe.wait_ge(S["ml_den"], 2 * NH)
            for j in range(NT):
                for g in range(NH):
                    last = mm(bank(4 + 2 * j + g // 2, 2, 2 * P)[:, g % 2, :], buf["fu"][:, g, j * P:(j + 1) * P], dft_c,
                              start=True, stop=True)
            last.then_inc(S["fn_pe"], 1)
            pe.wait_ge(S["fn_act"], 1)
            pe.wait_ge(S["fn_dve"], 1)
            pe.wait_ge(S["mem_in"], 16)
            pe.wait_ge(S["diag_dve"], 2)
            turn(0, mem, [diag[:, j, :] for j in range(NT)])
            pe.wait_ge(S["tp_act"], 4)
            pe.wait_ge(S["tp_dve"], 4)
            for j in range(NT):
                for n, (tab, u) in enumerate([(0, 0), (0, 1), (1, 0), (1, 1)]):
                    last = mm(ps[:, 4 + j, :], dft_t[:, tab, u, j * P:(j + 1) * P], fa[:, u, :, tab, :],
                              start=(n == 0), stop=(n == 3))
            last.then_inc(S["fn_pe"], 1)
            for c in range(HG_LEAD):
                dense(G_WK, True, memT, part=[c])
            pe.wait_ge(S["fn_act"], 2)
            pe.wait_ge(S["fn_dve"], 2)
            pe.wait_ge(S["hp_dve"], 3)
            pe.wait_ge(S["hp_act"], 8)
            pe.wait_ge(S["silu_act"], 4)
            for hd in range(NH):
                for u in range(NT):
                    last = mm(bank(4 + u, NH, P)[:, hd, :], hqk[1][:, hd, u * P:(u + 1) * P],
                              buf["hq"][:, hd, u * P:(u + 1) * P], start=True, stop=True)
            last.then_inc(S["h_pe"], 1)
            for s in range(2 * HG_LEVELS):
                w, lev = s // HG_LEVELS, s % HG_LEVELS
                g, c = G_WK + (s + HG_LEAD) // NCH, (s + HG_LEAD) % NCH
                dense(g, g < G_WV, memT, part=[c])
                pe.wait_ge(S["h_mulq"], s + 1)
                pe.wait_ge(S["h_mulk"], s + 1)
                if s >= 1:
                    pe.wait_ge(S["h_cp"], s)
                qk = hqk[s % 2]
                b0 = 6 - 2 * (s % 2)
                for hd in range(NH):
                    if lev < HG_LEVELS - 1:
                        for u in range(NT):
                            t_ = qk[:, hd, u * P:(u + 1) * P]
                            last = mm(bank(b0 + u, NH, P)[:, hd, :], t_, t_, start=True, stop=True)
                    else:
                        a, z = qk[:, hd, 0:P], qk[:, hd, P:2 * P]
                        last = mm(bank(b0, NH, P)[:, hd, :], *((a, z) if w == 0 else (z, a)), start=True, stop=True)
                last.then_inc(S["h_pe"], 1)
            pe.wait_ge(S["h_cp"], 2 * HG_LEVELS + 1)
            for j in range(NT):
                for hd in range(NH):
                    for u in range(NT):
                        last = mm(bank(4 + j, NH, P)[:, hd, :], decay_to[:, u, hd, j * P:(j + 1) * P],
                                  buf["hi"][:, u, hd * P:(hd + 1) * P], start=(u == 0), stop=(u == NT - 1))
            last.then_inc(S["h_o"], 1)
            def chunk_of_wv(part):
                for c in part:
                    dense(G_WV + c // NCH, False, memT, part=[c % NCH])

            for m in range(NA_H // 2 * NT):
                i, j = m // NT, m % NT
                if m == 0:
                    pe.wait_ge(S["h_oev"], 2)
                else:
                    pe.wait_ge(S["na_m"], m)
                pe.wait_ge(S["bias_in0" if m % 2 == 0 else "bias_in1"], 64 * (m // 2 + 1))
                for u in range(2):
                    o_ = ps[:, 4 + 3 * u, 0:T]
                    mm(o_, flipm, nbias[m % 2][:, u, :], start=True, stop=False)
                    last = mm(o_, buf["nq"][64 * u:64 * u + 64, i, j * P:(j + 1) * P], buf["nk"][64 * u:64 * u + 64, i, :],
                              start=False, stop=True)
                last.then_inc(S["na_s"], 1)
                chunk_of_wv(NA_CHUNKS[m][:1])
                pe.wait_ge(S["na_p"], 2 * (m + 1))
                if m >= 1:
                    pe.wait_ge(S["na_tev"], m)
                for u in range(2):
                    for s in range(NT):
                        last = mm(bank(5, 2, NT, P)[:, u, s, :], npr[:, u, s * P:(s + 1) * P], ident[:], start=True, stop=True)
                last.then_inc(S["na_t"], 1)
                chunk_of_wv(NA_CHUNKS[m][1:])
                pe.wait_ge(S["na_tev"], m + 1)
                if m >= 1:
                    pe.wait_ge(S["na_y"], 2 * m)
                for u in range(2):
                    for s in range(NT):
                        last = mm(bank(6, 2, NA_D)[:, u, :], npt[:, u, s, :], buf["nv"][:, s, (2 * i + u) * NA_D:(2 * i + u + 1) * NA_D],
                                  start=(s == 0), stop=(s == NT - 1))
                last.then_inc(S["na_o"], 1)
            pe.wait_ge(S["y_done"], 4)
            turn_split(1, y, [ident[:]] * 2)
            turned_split(1)
            for n in range(4):
                dense_split(G_WO + n, False, split[G_WO])
                if n >= 1:
                    group_turned(G_WO, n - 1, turn_split, 2)
            for i in range(NCH):
                pe.wait_ge(S["ts_lo"], 2 * KT // 2 + 2 * (i + 1))
                dense_split(G_WQ, True, split[G_WQ], part=[i])
                if i == 0:
                    group_turned(G_WO, 3, turn_split, 2)

            def xa_scores(hd):
                pe.wait_ge(S["proj_a"], G_WQ + hd + 1)
                pe.wait_ge(S["proj_b"], G_WQ + hd + 1)
                for j in range(NT):
                    for c in range(NH):
                        last = mm(bank(4 + hd, NT, T)[:, j, :], qT[:, 4 * hd + c, j * P:(j + 1) * P], kT[:, 4 * hd + c, :],
                                  start=(c == 0), stop=(c == NH - 1))
                last.then_inc(S["xs_pe"], 1)

            def xa_turn(hd):
                pe.wait_ge(S["xs_diag"], hd + 1)
                for s in range(NT):
                    for j in range(NT):
                        last = mm(bank(4 + hd, NT, NT, P)[:, s, j, :], xp[hd][:, j, s * P:(s + 1) * P], diag[:, j, :], start=True, stop=True)
                last.then_inc(S["xs_t"], 1)

            def xa_values(hd):
                pe.wait_ge(S["xs_tev"], hd + 1)
                if hd >= 2:
                    pe.wait_ge(S["xs_oa"], hd - 1)
                    pe.wait_ge(S["xs_od"], hd - 1)
                for c in range(NH):
                    for s in range(NT):
                        last = mm(bank(2 * (hd % 2) + c // 2, 2, T)[:, c % 2, :], v[:, s, (4 * hd + c) * P:(4 * hd + c + 1) * P],
                                  xpt[hd][:, s, :], start=(s == 0), stop=(s == NT - 1))
                last.then_inc(S["xs_o"], 1)

            for n in range(1, 4):
                dense_split(G_WQ + n, True, split[G_WQ])
                if n >= 2:
                    xa_turn(n - 2)
                xa_scores(n - 1)
            xa_scores(3)
            xa_values(0)
            xa_turn(2)
            xa_values(1)
            xa_turn(3)
            xa_values(2)
            xa_values(3)
            pe.wait_ge(S["xs_oa"], XA_H)
            pe.wait_ge(S["xs_od"], XA_H)
            for n in range(4):
                dense_split(G_XO + n, False, split[G_XO])
                if n >= 1:
                    group_turned(G_XO, n - 1, turn, 1)
            group_turned(G_XO, 3, turn, 1)
            pe.wait_ge(S["tp_act"], 8)
            pe.wait_ge(S["tp_dve"], 8)
            pe.wait_ge(S["wr_in"], 32)
            for j in range(NT):
                for k_ in range(KT):
                    last = mm(bank(4, NT, 36)[:, j, :], xT[:, k_, j * P:(j + 1) * P], wr[:, k_, :], start=(k_ == 0), stop=(k_ == KT - 1))
            last.then_inc(S["r_pe"], 1)
            pe.wait_ge(S["route_in"], 16)
            pe.wait_ge(S["r_dve"], 3)
            o_ = bank(5, 3, NE)
            mm(o_[:, 0, :], before, hit[:, 0, :], start=True, stop=True)
            mm(o_[:, 1, :], before, hit[:, 1, :], start=True, stop=False)
            mm(o_[:, 1, :], ones, hit[:, 0, :], start=False, stop=True)
            mm(o_[:, 2, :], ones, hits, start=True, stop=True).then_inc(S["r_pe"], 1)
            pe.wait_ge(S["tab_dve"], 1)
            for k_ in range(KT):
                if k_ >= 4:
                    pe.wait_ge(S["g_act" if k_ % 2 == 0 else "g_dve"], (k_ - 4) // 2 + 1)
                for j in range(NT):
                    last = mm(ps[:, 4 + k_ % 4, :], h[:, j, k_ * P:(k_ + 1) * P], sel_r[:, j, :], start=(j == 0), stop=(j == NT - 1))
                last.then_inc(S["g_pe"], 1)
            pe.wait_ge(S["g_act"], KT // 2)
            pe.wait_ge(S["g_dve"], KT // 2 + 1)
            pe.wait_ge(S["r_dve"], 4)
            mm(ps[0:1, 6, 0:P], eid, ident[:], start=True, stop=True)
            mm(ps[0:1, 6, P:2 * P], ost, ident[:], start=True, stop=True).then_inc(S["r_pe"], 1)
            pe.wait_ge(S["tab_dve"], 2)
            for s in range(SLOTS // P):
                for j in range(NT):
                    last = mm(bank(4 + s // 2, 2, NT, P)[:, s % 2, j, :], sel_g[:, j, s * P:(s + 1) * P], ident[:], start=True, stop=True)
            last.then_inc(S["sg_pe"], 1)
            def up(n, i):
                r = i % RING_E
                if i == 0:
                    pe.wait_ge(S["xe_lo"], n + 1)
                pe.wait_ge(S["up_lo"], n * UCH + (i + 1))
                for c in range(CH):
                    k_ = (i % 4) * CH + c
                    o_ = ps[0:EB, i // 4, :]
                    mm(o_, xe_hi[:, k_, :], up_hi[r][:, c, :], start=(k_ == 0), stop=False)
                    mm(o_, xe_hi[:, k_, :], up_lo[r][:, c, :], start=False, stop=False)
                    last = mm(o_, xe_lo[:, k_, :], up_hi[r][:, c, :], start=False, stop=(k_ == KT - 1))
                last.then_inc(S["up_used"], 1)

            def turn_h(n):
                pe.wait_ge(S["e_h"], n + 1)
                for f in range(FF // P):
                    last = mm(bank(6, FF // P, P)[:, f, :], sg[:, f * P:(f + 1) * P], ident[0:EB, :], start=True, stop=True)
                last.then_inc(S["e_turn"], 1)

            def down(n, i):
                if i == 0:
                    pe.wait_ge(S["e_hT"], n + 1)
                if not (isinstance(n, int) and n == 0):
                    pe.wait_ge(S["e_ya" if i < 2 else "e_yd"], n * 2 + (i % 2 - 1))
                pe.wait_ge(s_dn[i], (n + 1) * 16)
                for c in range(CH):
                    for f in range(FF // P):
                        last = mm(bank(2 + i, CH, EW)[:, c, :], ring_dn[i][:, f, c * P:(c + 1) * P],
                                  hT[:, f, :], start=(f == 0), stop=(f == FF // P - 1))
                last.then_inc(S["dn_used"], 1)

            def block_n(n, back):
                if back is not None:
                    turn_h(back)
                for i in range(UCH):
                    up(n, i)
                    if back is not None and i % 2 == 1:
                        down(back, i // 2)

            pe.wait_ge(S["sg_act"], 1)
            pe.wait_ge(S["proj_b"], G_XO + 4)
            block_n(0, None)
            block_n(1, 0)
            with pe.Fori(2, NE) as e:
                block_n(e, e - 1)
            turn_h(NE - 1)
            for i in range(DCH):
                down(NE - 1, i)
            pe.wait_ge(S["tab_dve"], 3)
            nov = pe.value_load(table[0:1, 96:97], min_val=0, max_val=OVB)
            with pe.Fori(0, OVB) as b:
                with pe.If(b < nov):
                    block_n(b + NE, None)
                    turn_h(b + NE)
                    for i in range(DCH):
                        down(b + NE, i)
            nc.tensor.matmul(ps[:, 6, 0:P], ident[:], ident[:], start=True, stop=True).then_inc(S["c_tp"], 1)
            pe.wait_ge(S["c_act"], 1)
            pe.wait_ge(S["c_dve"], 1)
            n = 0
            for s in range(SLOTS // P):
                for kk in range(4):
                    if n >= 4:
                        pe.wait_ge(S["c_act" if n % 2 == 0 else "c_dve"], (n - 4) // 2 + 2)
                    for u in range(4):
                        k_ = 4 * kk + u
                        last = mm(ps[:, 4 + n % 4, u * P:(u + 1) * P], ysT[:, k_, s * P:(s + 1) * P], ident[:], start=True, stop=True)
                    last.then_inc(S["c_tp"], 1)
                    n += 1
            pe.wait_ge(S["c_act"], 9)
            pe.wait_ge(S["c_dve"], 9)
            for j in range(NT):
                for g in range(4):
                    m = 4 * j + g
                    if m >= 4:
                        pe.wait_ge(S["c_add"], m - 3)
                    for s in range(SLOTS // P):
                        last = mm(ps[:, m % 4, :], selgT[:, s, j * P:(j + 1) * P], ys[:, s, g * 512:(g + 1) * 512],
                                  start=(s == 0), stop=(s == SLOTS // P - 1))
                    last.then_inc(S["c_pe"], 1)

        @block.scalar
        def _(act):
            fn = nc.scalar.activation
            steps, calls = [0], [0]

            def step(ins_):
                steps[0] += 1
                ins_.then_inc(S["act_step"], 1)
                act.wait_ge(S["act_step"], steps[0])

            def squares(src, to=None):
                to = flat(ps[:, 0:4, :]) if to is None else to
                step(fn(to, src[:, 0, :], ACT.Square, accum_out=st[:, 0:1]))
                fn(to, src[:, 1, :], ACT.Square, accum_out=st[:, 1:2]).then_inc(S["sq_act"], 1)

            def rsqrt(w):
                calls[0] += 1
                act.wait_ge(S["var_dve"], calls[0])
                step(fn(st[:, 16:16 + w], st[:, 8:8 + w], ACT.Ln))
                fn(st[:, 24:24 + w], st[:, 16:16 + w], ACT.Exp, scale=-0.5).then_inc(S["rs_act"], 1)

            def turned(n, dst, gain, part=range(KT // 2)):
                for kk in part[::2]:
                    act.wait_ge(S["tp_pe"], n * (KT // 2) + kk + 1)
                    for u in range(2):
                        k = 2 * kk + u
                        last = fn(dst[:, k, :], ps[:, 4 + kk % 4, u * T:(u + 1) * T], ACT.Copy, scale=cols[:, gain * KT + k:gain * KT + k + 1])
                    last.then_inc(S["tp_act"], 1)

            def turned_hi(n, dst, gain, part=range(KT // 2)):
                for kk in part:
                    act.wait_ge(S["ts_pe"], n * (KT // 2) + kk + 1)
                    for u in range(2):
                        k = 2 * kk + u
                        last = fn(dst[:, k, :], ps[:, 4 + kk % 4, u * T:(u + 1) * T], ACT.Copy, scale=cols[:, gain * KT + k:gain * KT + k + 1])
                    last.then_inc(S["ts_hi"], 1)

            def high(g, part):
                for i in part:
                    act.wait_ge(s_ring[i], 16 * (g + 1))
                    if g * NCH + i >= 2:
                        act.wait_ge(S["chunk_used"], g * NCH + i - 1)
                    n, hi_ring = split_chunk(g, i)
                    for u in range(2):
                        fn(hi_ring[(2 * n + u) % 4][:], ring_a[i][:, 2 * u:2 * u + 2, :], ACT.Copy).then_inc(S["w_hi"], 1)

            def dense_out(g, dst, scale=1.0):
                act.wait_ge(S["chunk_used"], NCH * (g + 1))
                fn(dst, ps[:, 2 * (g % 2), :] if len(dst.shape) == 2 else bank(2 * (g % 2), NH, P), ACT.Copy, scale=scale).then_inc(S["proj_a"], 1)

            def w_in_out(g, name, fm, _, scale):
                if name == "mv":
                    dst = buf[name][:, 0, :, 0:P]
                elif fm:
                    dst = flat(buf[name][:, 0:2, :])
                else:
                    dst = buf[name][:, 0, :]
                dense_out(g, dst, scale)
                if g == 2:
                    act.wait_ge(S["conv_dve"], 1)
                    fn(flat(buf["q"]), flat(buf["q"]), ACT.Silu).then_inc(S["silu_act"], 1)
                    act.wait_ge(S["conv_dve"], 2)
                    fn(flat(buf["k"]), flat(buf["k"]), ACT.Silu).then_inc(S["silu_act"], 1)
                if g in (3, 4, 8):
                    b_ = buf[name]
                    act.wait_ge(S["proj_a"], g + 1)
                    act.wait_ge(S["proj_b"], g + 1)
                    fn(flat(b_), flat(b_), ACT.Sigmoid if g == 3 else ACT.Silu).then_inc(S["silu_act"], 1)
                if g == 5:
                    act.wait_ge(S["gate_dve"], 2)
                    step(fn(gl, gt[:, 1::2, :], ACT.Abs))
                    step(fn(gl, gl, ACT.Exp, scale=-1.0))
                    fn(gl, gl, ACT.Ln, bias=1.0).then_inc(S["gate_act"], 1)
                    act.wait_ge(S["gate_dve"], 3)
                    fn(gr[:, 2:4, :], gr[:, 2:4, :], ACT.Exp, scale=-1.0).then_inc(S["gate_act"], 1)

            act.wait_ge(S["cols_pe"], 1)
            fn(cols[:], ps[:, 0, 0:104], ACT.Copy).then_inc(S["cols_act"], 1)
            act.wait_ge(S["cols_act"], 1)
            act.wait_ge(S["x_in"], 16)
            squares(h)
            rsqrt(NT)
            act.wait_ge(S["mem_in"], 16)
            act.wait_ge(S["diag_dve"], 1)
            squares(mem)
            turned_hi(0, split[G_IN][0], 0)
            rsqrt(NT)

            def ml_decays(hd):
                act.wait_ge(S["ml_pe_m"], hd + 1)
                for w in range(2):
                    act.wait_ge(S["ml_arg"], 2 * hd + 2)
                    if hd >= 1:
                        act.wait_ge(S["ml_sw"], 2 * hd - 1 + w)
                    nm = bank(6, 2, T)[:, w, :]
                    tiles = [(marg[w], 0, 0), (nm, 1, 0), (marg[w], 1, 1)] if w == 0 else [(marg[w], 0, 0), (nm, 0, 1), (marg[w], 1, 1)]
                    for n, (src, j, u) in enumerate(tiles):
                        last = fn(mw[w][:, n, :], src[:, j * P:(j + 1) * P], ACT.Exp, bias=mlc[:, u, w, hd:hd + 1])
                    last.then_inc(S["ml_w"], 1)

            def ml_normaliser(hd):
                if hd >= 1:
                    act.wait_ge(S["ml_y"], hd)
                for w in range(2):
                    act.wait_ge(S["ml_pv"], 2 * hd + w + 1)
                    fn(st[:, 44 + 2 * w:46 + 2 * w], bank(7 if w == 0 else 5, NT, P + 1)[:, :, P], ACT.Abs).then_inc(S["ml_den"], 1)

            for g in range(G_IN + 1):
                if g < G_IN:
                    high(g, (0, 1))
                if g >= 1:
                    w_in_out(g - 1, *W_IN[g - 1])
                if g == G_ML:
                    act.wait_ge(S["gate_dve"], 4)
                if G_ML < g <= G_ML + NH:
                    ml_normaliser(g - G_ML - 1)
                if G_ML <= g < G_ML + NH:
                    ml_decays(g - G_ML)
                if g < G_IN:
                    high(g, (2, 3))
            act.wait_ge(S["fn_pe"], 1)
            fn(fa[:, 0].rearrange("p g c n -> p (g c n)"), flat(ps[:, 4:6, :]), ACT.Copy).then_inc(S["fn_act"], 1)
            turned(0, memT, 3)
            act.wait_ge(S["fn_pe"], 2)
            fn(y[:, 0, 2 * GW:3 * GW], ps[:, 4, :], ACT.Copy).then_inc(S["fn_act"], 1)
            for w, name in enumerate(("hff", "hfb")):
                f = flat(buf[name])
                if w == 1:
                    act.wait_ge(S["hp_act"], 4)
                act.wait_ge(S["ml_y"], NH)
                fn(flat(htmp), f, ACT.Abs).then_inc(S["hp_act"], 1)
                act.wait_ge(S["hp_act"], 4 * w + 1)
                fn(flat(htmp), flat(htmp), ACT.Exp, scale=-1.0).then_inc(S["hp_act"], 1)
                act.wait_ge(S["hp_act"], 4 * w + 2)
                fn(flat(htmp), flat(htmp), ACT.Ln, bias=1.0).then_inc(S["hp_act"], 1)
                act.wait_ge(S["hp_dve"], w + 1)
                fn(f, flat(htmp), ACT.Exp).then_inc(S["hp_act"], 1)
            for _ in range(2):
                rsqrt(NT)
            for s in range(2 * HG_LEVELS):
                act.wait_ge(S["h_sub"], s + 1)
                fn(flat(he[s % 2]), flat(he[s % 2]), ACT.Exp).then_inc(S["h_exp"], 1)
                if (s + HG_LEAD) % NCH == 3:
                    g = G_WK + (s + HG_LEAD) // NCH
                    dense_out(g, flat(kT[:, 4 * (g - G_WK):4 * (g - G_WK) + 2, :]))
            act.wait_ge(S["h_o"], 1)
            fn(y[:, 0, GW:2 * GW], ps[:, 4, :], ACT.Copy).then_inc(S["h_oev"], 1)
            rsqrt(NT * NH)
            rsqrt(NT)
            for m in range(NA_H // 2 * NT):
                act.wait_ge(S["na_max"], m + 1)
                if m >= 1:
                    act.wait_ge(S["na_t"], m)
                    act.wait_ge(S["na_r"], m)
                for u in range(2):
                    fn(npr[:, u, :], ns[:, u, :], ACT.Exp, bias=st[:, 52 + u:53 + u], accum_out=st[:, 54 + u:55 + u]).then_inc(S["na_p"], 1)
                act.wait_ge(S["na_t"], m + 1)
                if m >= 1:
                    act.wait_ge(S["na_o"], m)
                fn(npt.rearrange("p u s t -> p (u s t)"), ps[:, 5, :], ACT.Copy).then_inc(S["na_tev"], 1)
                if m in NA_OUT:
                    n = NA_OUT[m]
                    dense_out(G_WV + n, v[:, 0, GW * n:GW * (n + 1)])
            rsqrt(NT)
            turned_hi(1, split[G_WO][0], 4)

            def groups(g0, turned_, *args):
                for n in range(5):
                    if n < 4:
                        high(g0 + n, (0, 1))
                    if n >= 2:
                        turned_(*args, part=range(2 * n - 4, 2 * n - 2))
                    if n < 4:
                        high(g0 + n, (2, 3))

            groups(G_WO, turned_hi, 2, split[G_WQ][0], 1)
            high(G_WQ, (0, 1))
            turned_hi(2, split[G_WQ][0], 1, part=range(6, 8))
            high(G_WQ, (2, 3))
            squares(h, arena(184, D))
            rsqrt(NT)

            def xa_exp(hd):
                act.wait_ge(S["xs_max"], hd + 1)
                if hd >= 1:
                    act.wait_ge(S["xs_diag"], hd)
                for j in range(NT):
                    fn(xp[hd][:, j, :], bank(4 + hd, NT, T)[:, j, :], ACT.Exp, bias=st[:, 52 + j:53 + j], scale=st[:, 62 + j:63 + j],
                       accum_out=st[:, 54 + j:55 + j]).then_inc(S["xs_p"], 1)

            def xa_turned(hd):
                act.wait_ge(S["xs_t"], hd + 1)
                fn(flat(xpt[hd]), ps[:, 4 + hd, :], ACT.Copy).then_inc(S["xs_tev"], 1)

            def xa_out_hi(hd):
                b0 = 2 * (hd % 2)
                act.wait_ge(S["xs_o"], hd + 1)
                fn(split[G_XO][0][:, 4 * hd:4 * hd + 4, :].rearrange("p c t -> p (c t)"), flat(ps[:, b0:b0 + 2, :]), ACT.Copy).then_inc(S["xs_oa"], 1)

            for n in range(5):
                g = G_WQ + n
                if 1 <= n < 4:
                    high(g, (0, 1))
                if n >= 1:
                    dense_out(g - 1, flat(qT[:, 4 * n - 4:4 * n - 2, :]))
                if n >= 2:
                    xa_exp(n - 2)
                if n >= 3:
                    xa_turned(n - 3)
                if 1 <= n < 4:
                    high(g, (2, 3))
            xa_exp(3)
            xa_out_hi(0)
            xa_turned(2)
            xa_out_hi(1)
            xa_turned(3)
            xa_out_hi(2)
            xa_out_hi(3)
            groups(G_XO, turned, 1, xT, 2)
            act.wait_ge(S["proj_a"], G_XO + 4)
            act.wait_ge(S["proj_b"], G_XO + 4)
            turned(1, xT, 2, part=range(6, 8))
            squares(h)
            rsqrt(NT)
            act.wait_ge(S["r_dve"], 1)
            for j in range(NT):
                step(fn(gexp, logit[:, j, 0:NG], ACT.Exp, bias=negm[:, j:j + 1], accum_out=gsum[:, j:j + 1]))
            act.wait_ge(S["r_dve"], 2)
            fn(vdif, vdif, ACT.Exp).then_inc(S["r_act"], 1)
            for k in range(0, KT, 2):
                act.wait_ge(S["g_pe"], k + 1)
                fn(xsT[:, k, 0:SLOTS], ps[:, 4 + k % 4, :], ACT.Copy, scale=cols[:, 2 * KT + k:2 * KT + k + 1]).then_inc(S["g_act"], 1)
            act.wait_ge(S["sg_pe"], 1)
            fn(flat(selgT), flat(ps[:, 4:6, :]), ACT.Copy).then_inc(S["sg_act"], 1)
            act.wait_ge(S["sg_act"], 1)
            def start_of(n):
                at = n if isinstance(n, int) else bass.ds(n, 1)
                return act.value_load(table[0:1, at:at + 1] if isinstance(n, int) else table[0:1, at], min_val=0, max_val=SLOTS)

            def tokens_hi(n, s):
                if not (isinstance(n, int) and n == 0):
                    act.wait_ge(S["up_used"], n * UCH)
                fn(xe_hi[:], xsT[:, :, bass.ds(s, EB)], ACT.Copy).then_inc(S["xe_hi"], 1)

            def weights_hi(n, part):
                for i in part:
                    r = i % RING_E
                    act.wait_ge(s_up[r], n * 32 + 16 * (i // RING_E + 1))
                    fn(up_hi[r][:], ring_up[r], ACT.Copy).then_inc(S["up_hi"], 1)

            def silu(n):
                act.wait_ge(S["up_used"], n * UCH + 4)
                if not (isinstance(n, int) and n == 0):
                    act.wait_ge(S["e_turn"], n)
                fn(sg, ps[0:EB, 0, :], ACT.Silu).then_inc(S["e_sg"], 1)

            def output(n, s, i):
                act.wait_ge(S["dn_used"], n * DCH + (i + 1))
                if not (isinstance(n, int) and n == 0):
                    act.wait_ge(S["e_ya"], n * 2 + (i - 1))
                fn(ysT[:, CH * i:CH * (i + 1), bass.ds(s, EB)], bank(2 + i, CH, EW)[:, :, 0:EB], ACT.Copy).then_inc(S["e_ya"], 1)

            def block_n(n, back):
                weights_hi(n, range(0, 1))
                tokens_hi(n, start_of(n))
                weights_hi(n, range(1, 4))
                if back is not None:
                    sb_ = start_of(back)
                    output(back, sb_, 0)
                weights_hi(n, range(4, 6))
                silu(n)
                if back is not None:
                    output(back, sb_, 1)
                weights_hi(n, range(6, UCH))

            act.wait_ge(S["tab_dve"], 3)
            block_n(0, None)
            block_n(1, 0)
            with act.Fori(2, NE) as e:
                block_n(e, e - 1)
            for i in range(2):
                output(NE - 1, start_of(NE - 1), i)
            nov = act.value_load(table[0:1, 96:97], min_val=0, max_val=OVB)
            with act.Fori(0, OVB) as b:
                with act.If(b < nov):
                    s = start_of(b + 64)
                    tokens_hi(b + NE, s)
                    weights_hi(b + NE, range(0, 6))
                    silu(b + NE)
                    weights_hi(b + NE, range(6, UCH))
                    for i in range(2):
                        output(b + NE, s, i)
            act.wait_ge(S["c_tp"], 1)
            fn(st[:, 60:61], ident[:, 0:1], ACT.Copy).then_inc(S["c_act"], 1)
            n = 0
            for s in range(SLOTS // P):
                for kk in range(4):
                    if n % 2 == 0:
                        act.wait_ge(S["c_tp"], n + 2)
                        fn(ys[:, s, kk * 512:(kk + 1) * 512], ps[:, 4 + n % 4, :], ACT.Copy).then_inc(S["c_act"], 1)
                    n += 1
            for j in range(NT):
                act.wait_ge(S["c_add"], 4 * (j + 1))
                fn(arena(104, D), h[:, j, :], ACT.Square, accum_out=st[:, 0:1]).then_inc(S["sq_act"], 1)
                rsqrt(1)

        @block.vector
        def _(dve):
            V = nc.vector
            steps, calls, norms = [0], [0], [0]

            def step(ins_):
                steps[0] += 1
                ins_.then_inc(S["dve_step"], 1)
                dve.wait_ge(S["dve_step"], steps[0])

            def rsqrt(w, inv):
                calls[0] += 1
                ss, var, r, t_ = st[:, 0:w], st[:, 8:8 + w], st[:, 24:24 + w], st[:, 32:32 + w]
                V.tensor_scalar(var, ss, inv, EPS, ALU.mult, ALU.add).then_inc(S["var_dve"], 1)
                dve.wait_ge(S["rs_act"], calls[0])
                step(V.tensor_tensor(t_, r, r, ALU.mult))
                step(V.tensor_tensor(t_, t_, var, ALU.mult))
                step(V.tensor_scalar(t_, t_, -0.5, 1.5, ALU.mult, ALU.add))
                step(V.tensor_tensor(r, r, t_, ALU.mult))

            def row_rms():
                norms[0] += 1
                dve.wait_ge(S["sq_act"], norms[0])
                rsqrt(NT, 1.0 / D)

            def row_scale():
                row_rms()
                for j in range(NT):
                    last = V.tensor_scalar(diag[:, j, :], ident[:], st[:, 24 + j:25 + j], None, ALU.mult)
                last.then_inc(S["diag_dve"], 1)

            def turned(n, dst, gain, part=range(KT // 2)):
                for kk in part[1::2]:
                    dve.wait_ge(S["tp_pe"], n * (KT // 2) + kk + 1)
                    for u in range(2):
                        k = 2 * kk + u
                        last = V.tensor_scalar(dst[:, k, :], ps[:, 4 + kk % 4, u * T:(u + 1) * T],
                                               cols[:, gain * KT + k:gain * KT + k + 1], None, ALU.mult)
                    last.then_inc(S["tp_dve"], 1)

            def turned_lo(n, dst, hi, gain, part=range(KT // 2)):
                for kk in part:
                    dve.wait_ge(S["ts_hi"], n * (KT // 2) + kk + 1)
                    for u in range(2):
                        k = 2 * kk + u
                        last = V.scalar_tensor_tensor(dst[:, k, :], ps[:, 4 + kk % 4, u * T:(u + 1) * T],
                                                      cols[:, gain * KT + k:gain * KT + k + 1], hi[:, k, :].bitcast(F32),
                                                      ALU.mult, ALU.subtract)
                    last.then_inc(S["ts_lo"], 1)

            def low(g, part):
                for i in part:
                    n, hi_ring = split_chunk(g, i)
                    for u in range(2):
                        dve.wait_ge(S["w_hi"], 2 * n + u + 1)
                        V.tensor_tensor(w_lo[i][:, 2 * u:2 * u + 2, :], ring_a[i][:, 2 * u:2 * u + 2, :],
                                        hi_ring[(2 * n + u) % 4][:].bitcast(F32), ALU.subtract).then_inc(S["w_lo"], 1)

            def dense_out(g, dst, scale=1.0):
                dve.wait_ge(S["chunk_used"], NCH * (g + 1))
                src = ps[:, 2 * (g % 2) + 1, :] if len(dst.shape) == 2 else bank(2 * (g % 2) + 1, NH, P)
                (V.tensor_copy(dst, src) if scale == 1.0 else V.tensor_scalar(dst, src, scale, None, ALU.mult)).then_inc(S["proj_b"], 1)

            def dense_add(g, n):
                dve.wait_ge(S["chunk_used"], NCH * (g + 1))
                for j in range(NT):
                    hv = h[:, j, GW * n:GW * (n + 1)]
                    V.tensor_tensor(hv, ps[:, 2 * (g % 2) + j, :], hv, ALU.add).then_inc(S["proj_a" if j == 0 else "proj_b"], 1)

            def group_norm(m):
                yv = y[:, :, GW * m:GW * (m + 1)]
                gtmp = arena(128, NT, GW)
                step(V.tensor_tensor(gtmp, yv, yv, ALU.mult))
                step(V.tensor_reduce(st[:, 0:NT], gtmp, AX.X, ALU.add))
                rsqrt(NT, 1.0 / GW)
                for j in range(NT):
                    last = V.tensor_scalar(yv[:, j, :], yv[:, j, :], st[:, 24 + j:25 + j], None, ALU.mult)
                last.then_inc(S["y_done"], 1)

            def w_in_out(g, name, fm, _, scale):
                if name == "mv":
                    dst = buf[name][:, 1, :, 0:P]
                elif fm:
                    dst = flat(buf[name][:, 2:4, :])
                else:
                    dst = buf[name][:, 1, :]
                dense_out(g, dst, scale)
                if g == 0:
                    dve.wait_ge(S["cmask_in"], 16)
                    step(V.tensor_copy(hmask.rearrange("p d l t -> p (d l t)"), hmask_f))
                if g == 1:
                    dve.wait_ge(S["proj_a"], 2)
                    dve.wait_ge(S["proj_b"], 2)
                    for n, (raw, dst) in enumerate((("mq", "q"), ("mk", "k"))):
                        tap = lambda t_, c: cols[:, 80 + 8 * t_ + 4 * n + c:81 + 8 * t_ + 4 * n + c]
                        for c in range(NH):
                            last = V.tensor_scalar(buf[dst][:, c, :], buf[raw][:, c, :], tap(1, c), None, ALU.mult)
                        step(last)
                        for c in range(NH):
                            o_, i_ = buf[dst][:, c, 1:T], buf[raw][:, c, 0:T - 1]
                            last = V.scalar_tensor_tensor(o_, i_, tap(0, c), o_, ALU.mult, ALU.add)
                        step(last)
                        for c in range(NH):
                            o_, i_ = buf[dst][:, c, 0:T - 1], buf[raw][:, c, 1:T]
                            last = V.scalar_tensor_tensor(o_, i_, tap(2, c), o_, ALU.mult, ALU.add)
                        last.then_inc(S["conv_dve"], 1)
                if g == 3:
                    dve.wait_ge(S["gate_pe"], 1)
                    V.tensor_copy(gtok, bank(4, NT, 16)).then_inc(S["gate_dve"], 1)
                    dve.wait_ge(S["gbias_in"], 16)
                    dve.wait_ge(S["gate_pe"], 2)
                    for kind in range(4):
                        last = V.tensor_scalar(gt[:, kind, :], ps[0:NH, 5 + kind // 2, (kind % 2) * T:(kind % 2 + 1) * T],
                                               gbias[:, kind:kind + 1], None, ALU.add)
                    last.then_inc(S["gate_dve"], 1)
                if g == 5:
                    dve.wait_ge(S["gate_dve"], 2)
                    dve.wait_ge(S["gate_act"], 1)
                    dve.wait_ge(S["pool_step"], 1)
                    step(V.scalar_tensor_tensor(lf, gt[:, 1::2, :], 0.0, gl, ALU.min, ALU.subtract))
                    V.tensor_tensor_scan(gb[:, 0, :], gone[0:NH, :], lf[:, 0, :], 0.0, ALU.mult, ALU.add)
                    step(V.tensor_tensor_scan(gb[:, 1, ::-1], gone[0:NH, :], lf[:, 1, ::-1], 0.0, ALU.mult, ALU.add))
                    step(V.tensor_tensor(gr[:, 0:2, :], gt[:, 0::2, :], gb, ALU.subtract))
                    V.tensor_tensor_scan(gm[:, 0, :], gr[:, 0, :], gr[:, 0, :], 0.0, ALU.max, ALU.max)
                    step(V.tensor_tensor_scan(gm[:, 1, ::-1], gr[:, 1, ::-1], gr[:, 1, ::-1], 0.0, ALU.max, ALU.max))
                    step(V.tensor_tensor(gr[:, 2:4, :], gb, gm, ALU.add))
                    V.tensor_scalar(gm, gm, -1.0, None, ALU.mult).then_inc(S["gate_dve"], 1)

            dve.wait_ge(S["eye_in"], 16)
            row_scale()
            dve.wait_ge(S["cols_act"], 1)
            turned_lo(0, split[G_IN][1], split[G_IN][0], 0)
            dve.wait_ge(S["ts_pe"], 8)
            row_scale()
            den, rden = st[:, 44:48].rearrange("p (w j) -> p w j", w=2), st[:, 48:52].rearrange("p (w j) -> p w j", w=2)

            def ml_weights(hd):
                dve.wait_ge(S["ml_pe_m"], hd + 1)
                for w in range(2):
                    if hd >= 1:
                        dve.wait_ge(S["ml_w"], 2 * hd - 1 + w)
                    V.tensor_tensor(marg[w].rearrange("p (j t) -> p j t", j=NT), bank(6, 2, NT, P)[:, w], bc_mid(tri[w], NT),
                                    ALU.add).then_inc(S["ml_arg"], 1)
                dve.wait_ge(S["ml_pe_s"], hd + 1)
                for w in range(2):
                    dve.wait_ge(S["ml_w"], 2 * hd + w + 1)
                    if hd >= 1:
                        dve.wait_ge(S["ml_pv"], 2 * hd - 1 + w)
                    sc = ps[:, 4, :]
                    cuts = [(0, 2, 0), (2, 3, 3)] if w == 0 else [(0, 1, 0), (1, 3, 2)]
                    for a, z, at in cuts:
                        last = V.scalar_tensor_tensor(flat(msw[w][:, a:z, :]), sc[:, at * P:(at + z - a) * P], P ** -0.5,
                                                      flat(mw[w][:, a:z, :]), ALU.mult, ALU.mult)
                    last.then_inc(S["ml_sw"], 1)

            def ml_output(hd):
                dve.wait_ge(S["ml_den"], 2 * hd + 2)
                step(V.tensor_tensor(den, den, mlc[:, :, 2:4, hd].rearrange("p j w -> p w j"), ALU.max))
                step(V.reciprocal(rden, den))
                for j in range(NT):
                    step(V.tensor_scalar(mt_, bank(7, NT, P + 1)[:, j, 0:P], rden[:, 0, j:j + 1], None, ALU.mult))
                    last = V.scalar_tensor_tensor(yml[:, j, hd * P:(hd + 1) * P], bank(5, NT, P + 1)[:, j, 0:P], rden[:, 1, j:j + 1],
                                                  mt_, ALU.mult, ALU.add)
                    if j == 0:
                        step(last)
                last.then_inc(S["ml_y"], 1)

            for g in range(G_IN + 1):
                if g < G_IN:
                    low(g, (0, 1))
                if g >= 1:
                    w_in_out(g - 1, *W_IN[g - 1])
                if g == G_ML:
                    dve.wait_ge(S["gate_pe"], 3)
                    V.tensor_copy(mlc.rearrange("p j k h -> p (j k h)"), ps[:, 4, 0:NT * 4 * NH]).then_inc(S["gate_dve"], 1)
                    dve.wait_ge(S["gate_dve"], 4)
                    dve.wait_ge(S["cmix_in"], 16)
                if G_ML < g <= G_ML + NH:
                    ml_output(g - G_ML - 1)
                if G_ML <= g < G_ML + NH:
                    ml_weights(g - G_ML)
                if g < G_IN:
                    low(g, (2, 3))
            dve.wait_ge(S["fn_pe"], 1)
            V.tensor_copy(fa[:, 1].rearrange("p g c n -> p (g c n)"), flat(ps[:, 6:8, :])).then_inc(S["fn_dve"], 1)
            turned(0, memT, 3)
            dve.wait_ge(S["ml_y"], NH)
            dve.wait_ge(S["silu_act"], 3)
            step(V.tensor_tensor(y[:, :, 0:GW], yml, buf["mo"], ALU.mult))
            dve.wait_ge(S["fn_pe"], 2)
            V.tensor_copy(y[:, 1, 2 * GW:3 * GW], ps[:, 5, :]).then_inc(S["fn_dve"], 1)
            dve.wait_ge(S["proj_a"], G_IN)
            dve.wait_ge(S["proj_b"], G_IN)
            step(V.memset(hone, 1.0))
            for w, name in enumerate(("hff", "hfb")):
                f = flat(buf[name])
                dve.wait_ge(S["hp_act"], 4 * w + 3)
                step(V.scalar_tensor_tensor(flat(he[w]), f, 0.0, flat(htmp), ALU.min, ALU.subtract))
                V.tensor_tensor(flat(htmp), flat(he[w]), f, ALU.subtract).then_inc(S["hp_dve"], 1)
                for c in range(NH):
                    o_, i_ = hb[w][:, c, :], he[w][:, c, :]
                    if w == 1:
                        o_, i_ = o_[:, ::-1], i_[:, ::-1]
                    last = V.tensor_tensor_scan(o_, hone, i_, 0.0, ALU.mult, ALU.add)
                step(last)
            dve.wait_ge(S["hp_act"], 8)
            V.tensor_tensor(flat(hqk[1]), flat(buf["hff"]), flat(buf["hfb"]), ALU.add).then_inc(S["hp_dve"], 1)
            group_norm(0)
            dve.wait_ge(S["fn_act"], 2)
            dve.wait_ge(S["fn_dve"], 2)
            dve.wait_ge(S["y_done"], 1)
            group_norm(2)

            def halves(x, half):
                vv = flat(x).rearrange("p (b u t) -> p b u t", u=2, t=half)
                return vv[:, :, 0, :], vv[:, :, 1, :]

            def decay(s):
                w, half = s // HG_LEVELS, 1 << (s % HG_LEVELS)
                if s >= 2:
                    dve.wait_ge(S["h_mulk"], s - 1)
                    dve.wait_ge(S["h_mulq"], s - 1)
                (e0_, e1_), (b0_, b1_) = halves(he[s % 2], half), halves(hb[w], half)
                mid = (b0_[:, :, half - 1:half] if w == 0 else b1_[:, :, 0:1]).to_broadcast(list(b0_.shape))
                if w == 0:
                    V.tensor_tensor(e0_, mid, b0_, ALU.subtract)
                    V.tensor_tensor(e1_, b1_, mid, ALU.subtract).then_inc(S["h_sub"], 1)
                else:
                    V.tensor_tensor(e0_, b0_, mid, ALU.subtract)
                    V.tensor_tensor(e1_, mid, b1_, ALU.subtract).then_inc(S["h_sub"], 1)

            def queries(s):
                w, half = s // HG_LEVELS, 1 << (s % HG_LEVELS)
                dve.wait_ge(S["h_exp"], s + 1)
                if s >= 1:
                    dve.wait_ge(S["h_pe"], s)
                u = 1 if w == 0 else 0
                V.tensor_tensor(halves(hqk[s % 2], half)[u], halves(he[s % 2], half)[u], halves(buf["hq"], half)[u],
                                ALU.mult).then_inc(S["h_mulq"], 1)

            def scores(s):
                w, lev = s // HG_LEVELS, s % HG_LEVELS
                dve.wait_ge(S["h_pe"], s + 2)
                dve.wait_ge(S["h_cp"], s + 1)
                b0 = 6 - 2 * (s % 2)
                if lev == HG_LEVELS - 1:
                    o_ = decay_to[:, w, :, P:2 * P] if w == 0 else decay_to[:, w, :, 0:P]
                    V.tensor_copy(o_, bank(b0, NH, P)).then_inc(S["h_cp"], 1)
                else:
                    for u in range(NT):
                        last = V.copy_predicated(decay_to[:, u, :, u * P:(u + 1) * P], bc_mid(hmask[:, w, lev, :], NH), bank(b0 + u, NH, P))
                    last.then_inc(S["h_cp"], 1)

            dve.wait_ge(S["silu_act"], 4)
            decay(0)
            dve.wait_ge(S["h_pe"], 1)
            for u in range(NT):
                last = V.tensor_copy(decay_to[:, u, :, u * P:(u + 1) * P], bank(4 + u, NH, P))
            last.then_inc(S["h_cp"], 1)
            for s in range(2 * HG_LEVELS):
                if s + 1 < 2 * HG_LEVELS:
                    decay(s + 1)
                queries(s)
                if s >= 1:
                    scores(s - 1)
                if s >= 1 and (s - 1 + HG_LEAD) % NCH == 3:
                    g = G_WK + (s - 1 + HG_LEAD) // NCH
                    dense_out(g, flat(kT[:, 4 * (g - G_WK) + 2:4 * (g - G_WK) + 4, :]))
            scores(2 * HG_LEVELS - 1)
            dve.wait_ge(S["h_o"], 1)
            V.tensor_copy(y[:, 1, GW:2 * GW], ps[:, 5, :]).then_inc(S["h_oev"], 1)
            dve.wait_ge(S["h_oev"], 2)
            dve.wait_ge(S["y_done"], 2)
            yh = y[:, :, GW:2 * GW]
            sq = arena(128, NT, GW)
            step(V.tensor_tensor(sq, yh, yh, ALU.mult))
            step(V.tensor_reduce(st[:, 0:NT * NH], sq.rearrange("p j (h d) -> p (j h) d", h=NH), AX.X, ALU.add))
            rsqrt(NT * NH, 1.0 / P)
            for j in range(NT):
                yj = yh[:, j, :].rearrange("p (h d) -> p h d", h=NH)
                last = V.tensor_tensor(yj, yj, bc_last(st[:, 24 + NH * j:24 + NH * (j + 1)], P), ALU.mult)
            step(last)
            dve.wait_ge(S["silu_act"], 5)
            step(V.tensor_tensor(yh, yh, buf["hg"], ALU.mult))
            group_norm(1)
            for m in range(NA_H // 2 * NT):
                i, j = m // NT, m % NT
                dve.wait_ge(S["na_s"], m + 1)
                if m >= 1:
                    dve.wait_ge(S["na_p"], 2 * m)
                grid = lambda x: x.rearrange("p u (a w) -> p u a w", w=GRID_W)
                V.tensor_tensor(grid(ns), grid(ps[:, 4::3, 0:T]), win.unsqueeze(1).unsqueeze(1).to_broadcast([P, 2, 4, GRID_W]),
                                ALU.add).then_inc(S["na_m"], 1)
                dve.wait_ge(S["na_m"], m + 1)
                step(V.tensor_reduce(st[:, 52:54], ns, AX.X, ALU.max))
                V.tensor_scalar(st[:, 52:54], st[:, 52:54], -1.0, None, ALU.mult).then_inc(S["na_max"], 1)
                dve.wait_ge(S["na_p"], 2 * m + 2)
                V.reciprocal(st[:, 44:46], st[:, 54:56]).then_inc(S["na_r"], 1)
                dve.wait_ge(S["na_r"], m + 1)
                dve.wait_ge(S["na_o"], m + 1)
                for u in range(2):
                    c0 = 3 * GW + (2 * i + u) * NA_D
                    V.tensor_scalar(y[:, j, c0:c0 + NA_D], bank(6, 2, NA_D)[:, u, :], st[:, 44 + u:45 + u], None, ALU.mult).then_inc(S["na_y"], 1)
                if m in NA_OUT:
                    n = NA_OUT[m]
                    dense_out(G_WV + n, v[:, 1, GW * n:GW * (n + 1)])
            dve.wait_ge(S["na_y"], 16)
            dve.wait_ge(S["y_done"], 3)
            group_norm(3)
            turned_lo(1, split[G_WO][1], split[G_WO][0], 4)
            dve.wait_ge(S["x_in"], 32)

            def add_groups(g0, turned_, *args):
                for n in range(5):
                    if n < 4:
                        low(g0 + n, (0, 1))
                    if n >= 1:
                        dense_add(g0 + n - 1, n - 1)
                    if n >= 2:
                        turned_(*args, part=range(2 * n - 4, 2 * n - 2))
                    if n < 4:
                        low(g0 + n, (2, 3))

            add_groups(G_WO, turned_lo, 2, split[G_WQ][1], split[G_WQ][0], 1)
            low(G_WQ, (0, 1))
            turned_lo(2, split[G_WQ][1], split[G_WQ][0], 1, part=range(6, 8))
            low(G_WQ, (2, 3))
            row_rms()
            step(V.tensor_scalar(st[:, 62:64], st[:, 24:26], XA_D ** -0.5, None, ALU.mult))

            def xa_max(hd):
                dve.wait_ge(S["xs_pe"], hd + 1)
                if hd >= 1:
                    dve.wait_ge(S["xs_p"], 2 * hd)
                step(V.tensor_reduce(st[:, 52:54], bank(4 + hd, NT, T), AX.X, ALU.max))
                V.scalar_tensor_tensor(st[:, 52:54], st[:, 52:54], -1.0, st[:, 62:64], ALU.mult, ALU.mult).then_inc(S["xs_max"], 1)

            def xa_diag(hd):
                dve.wait_ge(S["xs_p"], 2 * hd + 2)
                step(V.reciprocal(st[:, 44:46], st[:, 54:56]))
                if hd >= 1:
                    dve.wait_ge(S["xs_t"], hd)
                for j in range(NT):
                    last = V.tensor_scalar(diag[:, j, :], ident[:], st[:, 44 + j:45 + j], None, ALU.mult)
                last.then_inc(S["xs_diag"], 1)

            def xa_out_lo(hd):
                b0 = 2 * (hd % 2)
                heads = lambda x: x[:, 4 * hd:4 * hd + 4, :].rearrange("p c t -> p (c t)")
                dve.wait_ge(S["xs_oa"], hd + 1)
                V.tensor_tensor(heads(split[G_XO][1]), flat(ps[:, b0:b0 + 2, :]), heads(split[G_XO][0]).bitcast(F32),
                                ALU.subtract).then_inc(S["xs_od"], 1)

            for n in range(5):
                g = G_WQ + n
                if 1 <= n < 4:
                    low(g, (0, 1))
                if n >= 1:
                    dense_out(g - 1, flat(qT[:, 4 * n - 2:4 * n, :]))
                if n >= 2:
                    xa_max(n - 2)
                    xa_diag(n - 2)
                if 1 <= n < 4:
                    low(g, (2, 3))
            xa_max(3)
            xa_out_lo(0)
            xa_diag(3)
            xa_out_lo(1)
            xa_out_lo(2)
            xa_out_lo(3)
            add_groups(G_XO, turned, 1, xT, 2)
            turned(1, xT, 2, part=range(6, 8))
            row_rms()
            step(V.tensor_copy(st[:, 40:42], st[:, 24:26]))
            dve.wait_ge(S["r_pe"], 1)
            dve.wait_ge(S["route_in"], 16)
            V.memset(lgrp, LOWEST)
            for j in range(NT):
                last = V.tensor_scalar(logit[:, j, :], bank(4, NT, 36)[:, j, :], st[:, 40 + j:41 + j], None, ALU.mult)
            step(last)
            step(V.tensor_copy(lgrp[:, :, 0:NG], logit[:, :, 0:NG]))
            for j in range(NT):
                last = V.max(gmax8[:, j, :], lgrp[:, j, :])
            step(last)
            for j in range(NT):
                V.max_index(gidx8[:, j, :], gmax8[:, j, :], lgrp[:, j, :])
            V.tensor_scalar(negm, gmax8[:, :, 0], -1.0, None, ALU.mult).then_inc(S["r_dve"], 1)
            dve.wait_ge(S["r_dve"], 1)
            step(V.tensor_copy(egrp, gidx8[:, :, 0]))
            for j in range(NT):
                last = V.tensor_scalar(goh4[:, j, :], iota[:, 0:NG], egrp[:, j:j + 1], None, ALU.is_equal)
            step(last)
            for g in range(NG):
                for j in range(NT):
                    src = logit[:, j, NG + PG * g:NG + PG * (g + 1)]
                    if g == 0:
                        last = V.tensor_scalar(fine[:, j, :], src, goh4[:, j, g:g + 1], None, ALU.mult)
                    else:
                        last = V.scalar_tensor_tensor(fine[:, j, :], src, goh4[:, j, g:g + 1], fine[:, j, :], ALU.mult, ALU.add)
                step(last)
            for j in range(NT):
                last = V.max(fmax8[:, j, :], fine[:, j, :])
            step(last)
            for j in range(NT):
                last = V.max_index(fidx8[:, j, :], fmax8[:, j, :], fine[:, j, :])
            step(last)
            V.tensor_copy(e0, fidx8[:, :, 0])
            step(V.tensor_copy(e1, fidx8[:, :, 1]))
            V.tensor_tensor(vdif, fmax8[:, :, 1], fmax8[:, :, 0], ALU.subtract).then_inc(S["r_dve"], 1)
            V.scalar_tensor_tensor(e0, egrp, float(PG), e0, ALU.mult, ALU.add)
            step(V.scalar_tensor_tensor(e1, egrp, float(PG), e1, ALU.mult, ALU.add))
            for j in range(NT):
                V.tensor_scalar(hit0[:, j, :], iota[:, 0:NE], e0[:, j:j + 1], None, ALU.is_equal)
                last = V.tensor_scalar(hit1[:, j, :], iota[:, 0:NE], e1[:, j:j + 1], None, ALU.is_equal)
            step(last)
            step(V.tensor_tensor(hit, hit0, hit1, ALU.add))
            V.tensor_tensor(hits, hit[:, 0, :], hit[:, 1, :], ALU.add).then_inc(S["r_dve"], 1)
            dve.wait_ge(S["r_act"], 1)
            V.reciprocal(ggate, gsum)
            step(V.tensor_scalar(w0, vdif, 1.0, None, ALU.add))
            step(V.reciprocal(w0, w0))
            step(V.tensor_tensor(w0, w0, ggate, ALU.mult))
            step(V.tensor_tensor(w1, vdif, w0, ALU.mult))
            dve.wait_ge(S["r_pe"], 2)
            step(V.tensor_copy(flat(rank), ps[:, 5, 0:3 * NE]))
            count = rank[:, 2, :]
            one32 = ones[:, 0:NE]
            step(V.tensor_scalar(n_first, count, float(EB), None, ALU.min))
            V.tensor_tensor(n_over, count, n_first, ALU.subtract)
            step(V.tensor_tensor_scan(st_first, one32, n_first, 0.0, ALU.mult, ALU.add))
            step(V.tensor_tensor_scan(st_over, one32, n_over, st_first[:, NE - 1:NE], ALU.mult, ALU.add))
            V.tensor_tensor(st_first, st_first, n_first, ALU.subtract)
            step(V.tensor_tensor(st_over, st_over, n_over, ALU.subtract))
            step(V.scalar_tensor_tensor(st_gap, st_over, float(-EB), st_first, ALU.add, ALU.subtract))
            for j in range(NT):
                rj = rank[:, j, :]
                step(V.scalar_tensor_tensor(rtmp, rj, float(EB), st_gap, ALU.is_ge, ALU.mult))
                step(V.tensor_tensor(rtmp, rtmp, rj, ALU.add))
                step(V.tensor_tensor(rj, rtmp, st_first, ALU.add))
            slot = rank[:, 0:NT, :]
            step(V.tensor_tensor(hit0, hit0, slot, ALU.mult))
            step(V.tensor_reduce(slot0, hit0, AX.X, ALU.add))
            step(V.tensor_tensor(hit1, hit1, slot, ALU.mult))
            step(V.tensor_reduce(slot1, hit1, AX.X, ALU.add))

            def selection(sel, scale0, scale1):
                for j in range(NT):
                    V.tensor_scalar(sel[:, j, :], iota, slot0[:, j:j + 1], scale0[:, j:j + 1], ALU.is_equal, ALU.mult)
                    step(V.tensor_scalar(sel_t, iota, slot1[:, j:j + 1], scale1[:, j:j + 1], ALU.is_equal, ALU.mult))
                    last = V.tensor_tensor(sel[:, j, :], sel[:, j, :], sel_t, ALU.add)
                    if j < NT - 1:
                        step(last)
                last.then_inc(S["tab_dve"], 1)

            def gathered(k):
                dve.wait_ge(S["g_pe"], k + 1)
                V.tensor_scalar(xsT[:, k, 0:SLOTS], ps[:, 4 + k % 4, :], cols[:, 2 * KT + k:2 * KT + k + 1], None, ALU.mult).then_inc(S["g_dve"], 1)

            selection(sel_r, st[:, 40:42], st[:, 40:42])
            step(V.tensor_scalar(blocks, n_over, 0.0, None, ALU.is_gt))
            for k in range(1, OVK):
                step(V.tensor_scalar(rtmp, n_over, float(k * EB), None, ALU.is_gt))
                step(V.tensor_tensor(blocks, blocks, rtmp, ALU.add))
            step(V.tensor_tensor_scan(blk_in, one32, blocks, 0.0, ALU.mult, ALU.add))
            step(V.tensor_scalar(rtmp, blk_in, iotap, None, ALU.is_le))
            step(V.tensor_reduce(eid, rtmp, AX.X, ALU.add))
            step(V.tensor_scalar(eid, eid, float(NE - 1), None, ALU.min))
            step(V.tensor_tensor(blocks, blk_in, blocks, ALU.subtract))
            step(V.scalar_tensor_tensor(blocks, blocks, float(-EB), st_over, ALU.mult, ALU.add))
            step(V.tensor_scalar(rtmp, iota[:, 0:NE], eid, None, ALU.is_equal))
            step(V.tensor_tensor(rtmp, rtmp, blocks, ALU.mult))
            step(V.tensor_reduce(ost, rtmp, AX.X, ALU.add))
            step(V.scalar_tensor_tensor(ost, iotap, float(EB), ost, ALU.mult, ALU.add))
            V.tensor_scalar(ost, ost, float(SLOTS), None, ALU.min).then_inc(S["r_dve"], 1)
            gathered(1)
            dve.wait_ge(S["tab_dve"], 1)
            selection(sel_g, w0, w1)
            for k in range(3, KT, 2):
                gathered(k)
            V.memset(xsT[:, :, SLOTS:], 0.0).then_inc(S["g_dve"], 1)
            dve.wait_ge(S["r_pe"], 3)
            V.tensor_copy(table[0:1, 0:NE], st_first[0:1, :])
            V.tensor_copy(table[0:1, 32:64], ps[0:1, 6, 0:32])
            V.tensor_copy(table[0:1, 64:96], ps[0:1, 6, P:P + 32])
            V.tensor_copy(table[0:1, 96:97], blk_in[0:1, NE - 1:NE]).then_inc(S["tab_dve"], 1)
            def start_of(n):
                at = n if isinstance(n, int) else bass.ds(n, 1)
                return dve.value_load(table[0:1, at:at + 1] if isinstance(n, int) else table[0:1, at], min_val=0, max_val=SLOTS)

            def tokens_lo(n, s):
                dve.wait_ge(S["xe_hi"], n + 1)
                V.tensor_tensor(xe_lo[:], xsT[:, :, bass.ds(s, EB)], xe_hi[:].bitcast(F32), ALU.subtract).then_inc(S["xe_lo"], 1)

            def weights_lo(n, part):
                for i in part:
                    r = i % RING_E
                    dve.wait_ge(S["up_hi"], n * UCH + (i + 1))
                    V.tensor_tensor(up_lo[r][:], ring_up[r], up_hi[r][:].bitcast(F32), ALU.subtract).then_inc(S["up_lo"], 1)

            def gating(n):
                dve.wait_ge(S["up_used"], n * UCH + UCH)
                dve.wait_ge(S["e_sg"], n + 1)
                V.tensor_tensor(sg, ps[0:EB, 1, :], sg, ALU.mult).then_inc(S["e_h"], 1)

            def hidden(n):
                dve.wait_ge(S["e_turn"], n + 1)
                V.tensor_copy(hT, bank(6, FF // P, P)[:, :, 0:EW]).then_inc(S["e_hT"], 1)

            def outputs(n, s):
                for i in (2, 3):
                    dve.wait_ge(S["dn_used"], n * DCH + (i + 1))
                    V.tensor_copy(ysT[:, CH * i:CH * (i + 1), bass.ds(s, EB)], bank(2 + i, CH, EW)[:, :, 0:EB]).then_inc(S["e_yd"], 1)

            def block_n(n, back, back2):
                weights_lo(n, range(0, 1))
                if back is not None:
                    gating(back)
                tokens_lo(n, start_of(n))
                weights_lo(n, range(1, 2))
                if back is not None:
                    hidden(back)
                weights_lo(n, range(2, 3))
                if back2 is not None:
                    outputs(back2, start_of(back2))
                weights_lo(n, range(3, 5))
                if back2 is not None:
                    dve.wait_ge(S["e_yd"], n * 2 - 2)
                weights_lo(n, range(5, UCH))

            dve.wait_ge(S["tab_dve"], 3)
            block_n(0, None, None)
            block_n(1, 0, None)
            with dve.Fori(2, NE) as e:
                block_n(e, e - 1, e - 2)
            gating(NE - 1)
            hidden(NE - 1)
            outputs(NE - 2, start_of(NE - 2))
            dve.wait_ge(S["e_yd"], 2 * NE - 2)
            outputs(NE - 1, start_of(NE - 1))
            nov = dve.value_load(table[0:1, 96:97], min_val=0, max_val=OVB)
            with dve.Fori(0, OVB) as b:
                with dve.If(b < nov):
                    n = b + NE
                    s = start_of(b + 64)
                    tokens_lo(n, s)
                    weights_lo(n, range(UCH))
                    gating(n)
                    hidden(n)
                    dve.wait_ge(S["e_yd"], n * 2)
                    outputs(n, s)
            dve.wait_ge(S["c_tp"], 1)
            V.tensor_copy(st[:, 61:62], ident[:, 0:1]).then_inc(S["c_dve"], 1)
            n = 0
            for s in range(SLOTS // P):
                for kk in range(4):
                    if n % 2 == 1:
                        dve.wait_ge(S["c_tp"], n + 2)
                        V.tensor_copy(ys[:, s, kk * 512:(kk + 1) * 512], ps[:, 4 + n % 4, :]).then_inc(S["c_dve"], 1)
                    n += 1
            for j in range(NT):
                for g in range(4):
                    m = 4 * j + g
                    hv = h[:, j, g * 512:(g + 1) * 512]
                    dve.wait_ge(S["c_pe"], m + 1)
                    V.tensor_tensor(hv, ps[:, m % 4, :], hv, ALU.add).then_inc(S["c_add"], 1)
                norms[0] += 1
                dve.wait_ge(S["sq_act"], norms[0])
                rsqrt(1, 1.0 / D)
                dve.wait_ge(S["fgain_in"], 16)
                V.scalar_tensor_tensor(res[:, j, :], h[:, j, :], st[:, 24:25], fgain, ALU.mult, ALU.mult).then_inc(S["fin_dve"], 1)


INS = ["x", "mem", "norm_mix", "norm_cross", "norm_ffn", "norm_final", "norm_mem", "w_in", "mlstm_conv", "mlstm_gate_bias",
       "na_rpb", "group_gain", "w_out", "xa_wq", "xa_wk", "xa_wv", "xa_wo", "moe_router_group", "moe_router_expert",
       "moe_w1", "moe_w3", "moe_w2"]


def kernel(**inputs):
    import numpy as _np
    import concourse.bacc as _bacc
    from concourse import mybir as _mybir
    from concourse.bass_utils import run_bass_kernel_spmd as _run

    nc = _bacc.Bacc("TRN2", target_bir_lowering=False, num_devices=1)
    arrays, aps = {}, {}
    given = {n: inputs[n] for n in INS}
    given.update(constants())
    for name, a in given.items():
        a = _np.ascontiguousarray(a)
        arrays[f"in_{name}_dram"] = a
        aps[name] = nc.dram_tensor(f"in_{name}_dram", a.shape, _mybir.dt.from_np(a.dtype), kind="ExternalInput").ap()
    out = nc.dram_tensor("out_0_dram", (1, T, D), _mybir.dt.float32, kind="ExternalOutput").ap()
    program(nc, aps, out)
    r = _run(nc, [arrays], core_ids=[0])
    return r.results[0]["out_0_dram"]
```
